# Optimizing a Trainium2 kernel written in Bass

```python
import jax, jax.numpy as jnp
from jax import lax
import numpy as np

D_MODEL = 1024
BATCH = 1
SEQ = 256
DEPTH = 1
DEC_BATCH = 8
DEC_SEQ = 16
PAST_LEN = 128

CHUNK = 64
HEAD_DIM = 64
N_HEADS_A = D_MODEL // (2 * HEAD_DIM)
N_HEADS_B = D_MODEL // (2 * HEAD_DIM)
IDX_HEADS = 8
IDX_DIM = 32
TOPK_MAX = 256
QBLK = 128
BAND_PREV = 8
BAND_PAST = BAND_PREV * CHUNK
BAND_W = BAND_PAST + CHUNK
REL_CLIP = 128
PEER_HEADS = 8
PEER_DQ = 256
N_KEYS = 128
N_EXPERTS = N_KEYS * N_KEYS
PEER_TOPK = 16
PEER_BLK = 128
ROPE_THETA = 10000.0
EPS = 1e-6
NEG = -1e30
COL_SIZES = (N_HEADS_A * HEAD_DIM, N_HEADS_A * HEAD_DIM, N_HEADS_A * HEAD_DIM,
             IDX_HEADS * IDX_DIM, IDX_DIM, IDX_HEADS,
             N_HEADS_B * HEAD_DIM, N_HEADS_B * HEAD_DIM, N_HEADS_B * HEAD_DIM,
             2 * D_MODEL)
D_IN = sum(COL_SIZES)

kernel_name = 'chunk_hybrid_dsa_band_peer_step'

def _rmsnorm(x, g):
    xf = x.astype(jnp.float32)
    y = xf * lax.rsqrt(jnp.mean(xf * xf, axis=-1, keepdims=True) + EPS)
    return (y * g.astype(jnp.float32)).astype(x.dtype)

def _rope(x, pos):
    half = x.shape[-1] // 2
    inv = jnp.power(ROPE_THETA, -jnp.arange(half, dtype=jnp.float32) / half)
    ang = pos.astype(jnp.float32)[:, None] * inv[None, :]
    cos = jnp.cos(ang)[:, None, :]
    sin = jnp.sin(ang)[:, None, :]
    xf = x.astype(jnp.float32)
    x1, x2 = xf[..., :half], xf[..., half:]
    return jnp.concatenate([x1 * cos - x2 * sin, x2 * cos + x1 * sin], axis=-1).astype(x.dtype)

def _dsa_one(q, k, v, iq, ik, iw, qpos, kpos):
    T, H, d = q.shape
    L = k.shape[0]
    n_sel = min(TOPK_MAX, L // 4)
    blk = min(QBLK, T)
    nb = -(-T // blk)
    pad = nb * blk - T
    qb = jnp.pad(q, ((0, pad), (0, 0), (0, 0))).reshape(nb, blk, H, d)
    iqb = jnp.pad(iq, ((0, pad), (0, 0), (0, 0))).reshape(nb, blk, IDX_HEADS, IDX_DIM)
    iwb = jnp.pad(iw, ((0, pad), (0, 0))).reshape(nb, blk, IDX_HEADS)
    pb = (qpos[0] + jnp.arange(nb * blk)).reshape(nb, blk)
    kchunk = kpos // CHUNK
    scale = HEAD_DIM ** -0.5

    def block(args):
        qx, iqx, iwx, px = args
        rel = jax.nn.relu(jnp.einsum('qhd,sd->qhs', iqx, ik).astype(jnp.float32))
        score = jnp.einsum('qhs,qh->qs', rel, iwx.astype(jnp.float32))
        adm = kchunk[None, :] <= (px // CHUNK)[:, None]
        score = jnp.where(adm, score, NEG)
        _, sel = lax.top_k(score, n_sel)
        ok = jnp.take_along_axis(adm, sel, axis=1)
        kg = k[sel]
        vg = v[sel]
        logits = jnp.einsum('qhd,qkhd->qhk', qx, kg).astype(jnp.float32) * scale
        logits = jnp.where(ok[:, None, :], logits, NEG)
        p = jax.nn.softmax(logits, axis=-1).astype(vg.dtype)
        return jnp.einsum('qhk,qkhd->qhd', p, vg)

    out = lax.map(block, (qb, iqb, iwb, pb))
    return out.reshape(nb * blk, H, d)[:T]

def _band_one(q, k, v, qpos, kpos, rel_bias):
    T, H, d = q.shape
    P = k.shape[0] - T
    nqc = -(-T // CHUNK)
    tp = nqc * CHUNK
    front = BAND_PAST - P
    back = tp - T
    kp = jnp.pad(k, ((front, back), (0, 0), (0, 0)))
    vp = jnp.pad(v, ((front, back), (0, 0), (0, 0)))
    valid = jnp.pad(jnp.ones((P + T,), dtype=bool), (front, back))
    kposp = jnp.pad(kpos, (front, back))
    qc = jnp.pad(q, ((0, back), (0, 0), (0, 0))).reshape(nqc, CHUNK, H, d)
    qposc = (qpos[0] + jnp.arange(tp)).reshape(nqc, CHUNK)
    idx = (jnp.arange(nqc) * CHUNK)[:, None] + jnp.arange(BAND_W)[None, :]
    kb = kp[idx]
    vb = vp[idx]
    kposb = kposp[idx]
    validb = valid[idx]
    s = jnp.einsum('cqhd,ckhd->chqk', qc, kb).astype(jnp.float32) * (HEAD_DIM ** -0.5)
    rel = jnp.clip(qposc[:, :, None] - kposb[:, None, :], -REL_CLIP, REL_CLIP) + REL_CLIP
    bias = jnp.moveaxis(rel_bias.astype(jnp.float32)[:, rel], 0, 1)
    cq = (qposc // CHUNK)[:, :, None]
    ck = (kposb // CHUNK)[:, None, :]
    ok = (ck <= cq) & (ck >= cq - BAND_PREV) & validb[:, None, :]
    s = jnp.where(ok[:, None, :, :], s + bias, NEG)
    p = jax.nn.softmax(s, axis=-1).astype(vb.dtype)
    o = jnp.einsum('chqk,ckhd->cqhd', p, vb)
    return o.reshape(tp, H, d)[:T]

def _peer(h, w_pq, c1, c2, u, v):
    N = h.shape[0]
    nb = -(-N // PEER_BLK)
    pad = nb * PEER_BLK - N
    hb = jnp.pad(h, ((0, pad), (0, 0))).reshape(nb, PEER_BLK, D_MODEL)
    half = PEER_DQ // 2

    def block(hx):
        q = (hx @ w_pq).astype(jnp.float32).reshape(PEER_BLK, PEER_HEADS, PEER_DQ)
        s1 = jnp.einsum('nhd,kd->nhk', q[..., :half], c1.astype(jnp.float32))
        s2 = jnp.einsum('nhd,kd->nhk', q[..., half:], c2.astype(jnp.float32))
        v1, i1 = lax.top_k(s1, PEER_TOPK)
        v2, i2 = lax.top_k(s2, PEER_TOPK)
        cand = (v1[..., :, None] + v2[..., None, :]).reshape(PEER_BLK, PEER_HEADS, PEER_TOPK * PEER_TOPK)
        cidx = (i1[..., :, None] * N_KEYS + i2[..., None, :]).reshape(PEER_BLK, PEER_HEADS, PEER_TOPK * PEER_TOPK)
        sv, si = lax.top_k(cand, PEER_TOPK)
        e = jnp.take_along_axis(cidx, si, axis=-1)
        g = jax.nn.softmax(sv, axis=-1)
        ue = u[e]
        ve = v[e]
        a = jax.nn.gelu(jnp.einsum('nhkd,nd->nhk', ue, hx).astype(jnp.float32), approximate=False)
        return jnp.einsum('nhk,nhkd->nd', (g * a).astype(ve.dtype), ve)

    return lax.map(block, hb).reshape(nb * PEER_BLK, D_MODEL)[:N]

def _layer(x, start, ca_k, ca_v, ca_ik, cb_k, cb_v, g_attn, w_in, g_qa, g_ka, g_ik, g_qb, g_kb,
           rel_bias, w_br_a, w_br_b, w_out, g_ffn, w_pq, c1, c2, u, v):
    B, T, _ = x.shape
    pos = start + jnp.arange(T)
    h = _rmsnorm(x, g_attn)
    proj = h @ w_in
    splits = [int(s) for s in np.cumsum(COL_SIZES)[:-1]]
    aq, ak, av, iq, ik, iw, bq, bk, bv, gates = jnp.split(proj, splits, axis=-1)
    aq = _rope(_rmsnorm(aq.reshape(B, T, N_HEADS_A, HEAD_DIM), g_qa), pos)
    ak = _rope(_rmsnorm(ak.reshape(B, T, N_HEADS_A, HEAD_DIM), g_ka), pos)
    av = av.reshape(B, T, N_HEADS_A, HEAD_DIM)
    iq = _rope(iq.reshape(B, T, IDX_HEADS, IDX_DIM), pos)
    ik = _rope(_rmsnorm(ik, g_ik)[:, :, None, :], pos)[:, :, 0, :]
    iw = iw * (IDX_HEADS ** -0.5)
    bq = _rmsnorm(bq.reshape(B, T, N_HEADS_B, HEAD_DIM), g_qb)
    bk = _rmsnorm(bk.reshape(B, T, N_HEADS_B, HEAD_DIM), g_kb)
    bv = bv.reshape(B, T, N_HEADS_B, HEAD_DIM)

    pa = ca_k.shape[1]
    pb = cb_k.shape[1]
    ka_all = jnp.concatenate([ca_k.astype(ak.dtype), ak], axis=1)
    va_all = jnp.concatenate([ca_v.astype(av.dtype), av], axis=1)
    ika_all = jnp.concatenate([ca_ik.astype(ik.dtype), ik], axis=1)
    kb_all = jnp.concatenate([cb_k.astype(bk.dtype), bk], axis=1)
    vb_all = jnp.concatenate([cb_v.astype(bv.dtype), bv], axis=1)
    kpos_a = start - pa + jnp.arange(pa + T)
    kpos_b = start - pb + jnp.arange(pb + T)

    oa = lax.map(lambda a: _dsa_one(a[0], a[1], a[2], a[3], a[4], a[5], pos, kpos_a),
                 (aq, ka_all, va_all, iq, ika_all, iw))
    ob = lax.map(lambda a: _band_one(a[0], a[1], a[2], pos, kpos_b, rel_bias),
                 (bq, kb_all, vb_all))

    ga, gb = jnp.split(jax.nn.sigmoid(gates.astype(jnp.float32)).astype(x.dtype), 2, axis=-1)
    merged = ga * (oa.reshape(B, T, -1) @ w_br_a) + gb * (ob.reshape(B, T, -1) @ w_br_b)
    x = x + merged @ w_out
    y_ffn = _peer(_rmsnorm(x, g_ffn).reshape(B * T, D_MODEL), w_pq, c1, c2, u, v)
    x = x + y_ffn.reshape(B, T, D_MODEL)
    keep = min(BAND_PAST, T)
    return x, (ak, av, ik, bk[:, T - keep:], bv[:, T - keep:])

def setup_inputs(seed: int = 0) -> dict:
    key = jax.random.key(seed)
    ks = jax.random.split(key, 24)
    f32 = jnp.float32
    band_rows = min(BAND_PAST, PAST_LEN)
    wa = N_HEADS_A * HEAD_DIM
    wb = N_HEADS_B * HEAD_DIM

    def nrm(k, shape, scale):
        return jax.random.normal(k, shape, f32) * scale

    def gain(k, n):
        return 1.0 + 0.05 * jax.random.normal(k, (DEPTH, n), f32)

    return {
        'x_prompt': nrm(ks[0], (BATCH, SEQ, D_MODEL), 1.0),
        'x_sample': nrm(ks[1], (DEC_BATCH, DEC_SEQ, D_MODEL), 1.0),
        'cache_a_k': nrm(ks[2], (DEPTH, DEC_BATCH, PAST_LEN, N_HEADS_A, HEAD_DIM), 1.0),
        'cache_a_v': nrm(ks[3], (DEPTH, DEC_BATCH, PAST_LEN, N_HEADS_A, HEAD_DIM), 1.0),
        'cache_a_ik': nrm(ks[4], (DEPTH, DEC_BATCH, PAST_LEN, IDX_DIM), 1.0),
        'cache_b_k': nrm(ks[5], (DEPTH, DEC_BATCH, band_rows, N_HEADS_B, HEAD_DIM), 1.0),
        'cache_b_v': nrm(ks[6], (DEPTH, DEC_BATCH, band_rows, N_HEADS_B, HEAD_DIM), 1.0),
        'g_attn': gain(ks[7], D_MODEL),
        'w_in': nrm(ks[8], (DEPTH, D_MODEL, D_IN), D_MODEL ** -0.5),
        'g_qa': gain(ks[9], HEAD_DIM),
        'g_ka': gain(ks[10], HEAD_DIM),
        'g_ik': gain(ks[11], IDX_DIM),
        'g_qb': gain(ks[12], HEAD_DIM),
        'g_kb': gain(ks[13], HEAD_DIM),
        'rel_bias': nrm(ks[14], (DEPTH, N_HEADS_B, 2 * REL_CLIP + 1), 0.1),
        'w_br_a': nrm(ks[15], (DEPTH, wa, D_MODEL), wa ** -0.5),
        'w_br_b': nrm(ks[16], (DEPTH, wb, D_MODEL), wb ** -0.5),
        'w_out': nrm(ks[17], (DEPTH, D_MODEL, D_MODEL), D_MODEL ** -0.5),
        'g_ffn': gain(ks[18], D_MODEL),
        'w_pq': nrm(ks[19], (DEPTH, D_MODEL, PEER_HEADS * PEER_DQ), D_MODEL ** -0.5),
        'peer_c1': nrm(ks[20], (DEPTH, N_KEYS, PEER_DQ // 2), (PEER_DQ // 2) ** -0.5),
        'peer_c2': nrm(ks[21], (DEPTH, N_KEYS, PEER_DQ // 2), (PEER_DQ // 2) ** -0.5),
        'peer_u': nrm(ks[22], (DEPTH, N_EXPERTS, D_MODEL), D_MODEL ** -0.5),
        'peer_v': nrm(ks[23], (DEPTH, N_EXPERTS, D_MODEL), PEER_HEADS ** -0.5),
    }

def reference(x_prompt, x_sample, cache_a_k, cache_a_v, cache_a_ik, cache_b_k, cache_b_v,
              g_attn, w_in, g_qa, g_ka, g_ik, g_qb, g_kb, rel_bias, w_br_a, w_br_b, w_out,
              g_ffn, w_pq, peer_c1, peer_c2, peer_u, peer_v):
    xp = x_prompt
    xs = x_sample
    bp = x_prompt.shape[0]
    past_len = cache_a_k.shape[2]
    sp = []
    ss = []
    for l in range(DEPTH):
        w = (g_attn[l], w_in[l], g_qa[l], g_ka[l], g_ik[l], g_qb[l], g_kb[l], rel_bias[l],
             w_br_a[l], w_br_b[l], w_out[l], g_ffn[l], w_pq[l], peer_c1[l], peer_c2[l],
             peer_u[l], peer_v[l])
        xp, st_p = _layer(xp, 0,
                          jnp.zeros((bp, 0, N_HEADS_A, HEAD_DIM), xp.dtype),
                          jnp.zeros((bp, 0, N_HEADS_A, HEAD_DIM), xp.dtype),
                          jnp.zeros((bp, 0, IDX_DIM), xp.dtype),
                          jnp.zeros((bp, 0, N_HEADS_B, HEAD_DIM), xp.dtype),
                          jnp.zeros((bp, 0, N_HEADS_B, HEAD_DIM), xp.dtype),
                          *w)
        xs, st_s = _layer(xs, past_len, cache_a_k[l], cache_a_v[l], cache_a_ik[l],
                          cache_b_k[l], cache_b_v[l], *w)
        sp.append(st_p)
        ss.append(st_s)
    a_k_prompt = jnp.stack([s[0] for s in sp])
    a_v_prompt = jnp.stack([s[1] for s in sp])
    a_ik_prompt = jnp.stack([s[2] for s in sp])
    b_k_prompt = jnp.stack([s[3] for s in sp])
    b_v_prompt = jnp.stack([s[4] for s in sp])
    a_k_sample = jnp.stack([s[0] for s in ss])
    a_v_sample = jnp.stack([s[1] for s in ss])
    a_ik_sample = jnp.stack([s[2] for s in ss])
    b_k_sample = jnp.stack([s[3] for s in ss])
    b_v_sample = jnp.stack([s[4] for s in ss])
    return (xp, xs, a_k_prompt, a_v_prompt, a_ik_prompt, b_k_prompt, b_v_prompt,
            a_k_sample, a_v_sample, a_ik_sample, b_k_sample, b_v_sample)


_drawn_inputs = setup_inputs


def setup_inputs(seed=0):
    import zlib

    import numpy as np

    out = dict(_drawn_inputs(seed))
    spreads = {}
    factors = {'g_qa': 3.381, 'g_qb': 4.853, 'rel_bias': 3.209}
    for name, (base, spread) in spreads.items():
        noise = np.random.default_rng([zlib.crc32(name.encode()), seed]).standard_normal(out[name].shape)
        drawn = base * np.exp(spread * noise) if base else spread * noise
        out[name] = __import__('jax').numpy.asarray(drawn.astype(out[name].dtype))
    for name, factor in factors.items():
        out[name] = (out[name] * factor).astype(out[name].dtype)
    return out
```

```python
from contextlib import ExitStack

import numpy as np

import concourse.bass as bass
from concourse import mybir

F32 = mybir.dt.float32
U32 = mybir.dt.uint32
ALU = mybir.AluOpType
ACT = mybir.ActivationFunctionType
AX = mybir.AxisListType.X

P = 128
D = 1024
DC = D // P
TILES = 3
SAMPLE = 2
NTOK = TILES * P
STREAMS, NEW, PAST = 8, 16, 128
HEADS, HD = 8, 64
PAIRS = HEADS // 2
IH, ID = 8, 32
CHUNK = 64
REL = 128
PEER_H, PEER_K, NKEYS, DQ = 8, 16, 128, 256
SLOTS = PEER_H * PEER_K
EPS = 1e-6
NEG = -1e30
TAKEN = -3e38
PAD = -2e30
BQ_COL = 1832
GATE_COL = 3368
GROUPS = [("aq", 0, 512), ("ak", 512, 512), ("ix", 1536, 296), ("av", 1024, 512),
          ("bq", BQ_COL, 512), ("bk", BQ_COL + 512, 512), ("bv", BQ_COL + 1024, 512)]
GROUPS += [(f"gate{n}", GATE_COL + 512 * n, 512) for n in range(4)]
NG = len(GROUPS)
SEEN = [128, 256, 256]
SELECT = [64, 64, 36]
RING = 8
EXT = 384
ROUNDS = SLOTS // RING
MIDDLE = ROUNDS // 4


def build(nc, i, o):
    with ExitStack() as ctx:
        def sb(name, shape, dt=F32):
            return ctx.enter_context(nc.sbuf_tensor(name, shape, dt))

        def psum(name, shape):
            return ctx.enter_context(nc.psum_tensor(name, shape, F32))

        sems, counts = {}, {}

        def S(name):
            if name not in sems:
                sems[name] = ctx.enter_context(nc.semaphore(name))
                counts[name] = 0
            return sems[name]

        def signal(ins, name):
            ins.then_inc(S(name), 1)
            counts[name] += 1

        def chain(eng, ins, name):
            signal(ins, name)
            eng.wait_ge(sems[name], counts[name])

        ident = sb("ident", [P, P])
        ropet = sb("ropet", [P, 2, TILES, HD // 2])
        ropei = sb("ropei", [P, 2, TILES, ID // 2])
        gain = sb("gain", [P, D])
        hgain = sb("hgain", [P, 4, HD])
        igain = sb("igain", [P, ID])
        iota16 = sb("iota16", [P, 16])
        big = sb("big", [P, 16 * D])
        ring = sb("ring", [P, 2, 4096])
        qkv = sb("qkv", [P, 6, TILES, 512])
        ix = sb("ix", [P, TILES, 296])
        prob = sb("prob", [P, HEADS * 256])
        qk = sb("qk", [P, 2, PAIRS, NTOK])
        probT = sb("probT", [P, 2, 512])
        score = sb("score", [P, TILES, 264])
        mask = sb("mask", [P, TILES, 256])
        ikT = sb("ikT", [P, NTOK])
        cikT = sb("cikT", [P, STREAMS, P])
        diag = sb("diag", [P, RING, P])
        own = sb("own", [P, P])
        cT = sb("cT", [P, 2, P])
        rtop = sb("rtop", [P, 16, 16])
        rtopi = sb("rtopi", [P, 16, 16], U32)
        rtopf = sb("rtopf", [P, 16, 16])
        sv = sb("sv", [P, PEER_H, PEER_K])
        si = sb("si", [P, PEER_H, PEER_K], U32)
        sj = sb("sj", [P, PEER_H, PEER_K], U32)
        sif = sb("sif", [P, 2, SLOTS])
        expert = sb("expert", [P, TILES, SLOTS], U32)
        gate = sb("gate", [P, TILES, SLOTS])
        staged = sb("staged", [P, 2, RING], U32)
        dots = sb("dots", [P, 2, RING])
        gelu = sb("gelu", [P, 2, RING])
        wexp = sb("wexp", [P, 2, RING])
        ssx = sb("ssx", [P, 2, TILES])
        rsx = sb("rsx", [P, 2, TILES])
        ssh = sb("ssh", [P, 5, 24])
        rsh = sb("rsh", [P, 5, 24])
        mhalf = sb("mhalf", [P, 24])
        mx8 = sb("mx8", [P, 8])
        rowmax = sb("rowmax", [P, HEADS])
        rowsum = sb("rowsum", [P, HEADS])
        rowinv = sb("rowinv", [P, HEADS])

        bias = big[:, 0:4096].rearrange("p (a h k) -> p a h k", a=4, h=HEADS)
        B_NEAR, B_FAR, B_CACHE, B_OWN = range(4)
        SB0 = 4096
        raw = big[:, SB0:SB0 + 2048].rearrange("p (s b c) -> p s b c", s=2, b=STREAMS)
        kcT = big[:, SB0 + 2048:SB0 + 4096].rearrange("p (s b c) -> p s b c", s=2, b=STREAMS)
        vc = big[:, SB0 + 4096:SB0 + 6144].rearrange("p (s b c) -> p s b c", s=2, b=STREAMS)
        QM = 9 * P
        qm = big[:, SB0 + 6144:SB0 + 6144 + 2 * QM].rearrange("p (s c) -> p s c", s=2)
        HT0 = SB0 + 6144 + 2 * QM
        hT = big[:, HT0:HT0 + 3072].rearrange("p (c n) -> p c n", c=DC)
        iqT = big[:, HT0 + 3072:HT0 + 3072 + 768].rearrange("p (c n) -> p c n", c=2)
        xin = big[:, SB0:SB0 + 3072].rearrange("p (t c) -> p t c", t=TILES)
        hin = big[:, SB0 + 3072:SB0 + 6144].rearrange("p (t c) -> p t c", t=TILES)
        merged = xin
        pqT = big[:, SB0:SB0 + 6144].rearrange("p (g n) -> p g n", g=16)
        ubuf = big[:, 0:RING * D].rearrange("p (s c) -> p s c", s=RING)
        vbuf = big[:, RING * D:2 * RING * D].rearrange("p (s c) -> p s c", s=RING)
        AQ, BQ, AK, AV, BK, BV = range(6)
        where = {"aq": AQ, "bq": BQ, "ak": AK, "av": AV, "bk": BK, "bv": BV}
        flat = qkv.ap() if hasattr(qkv, "ap") else qkv[:, :, :, :]
        flat = qkv[:, :, :, :].rearrange("p a t c -> p (a t c)")
        oT = [flat[:, 0:1536].rearrange("p (c n) -> p c n", c=PAIRS),
              flat[:, 1536:3072].rearrange("p (c n) -> p c n", c=PAIRS)]
        x1 = flat[:, 3072:6144].rearrange("p (t c) -> p t c", t=TILES)
        h2 = flat[:, 6144:9216].rearrange("p (t c) -> p t c", t=TILES)
        rbias = flat[:, 3072:3072 + HEADS * 257].rearrange("p (h k) -> p h k", h=HEADS)
        ext = flat[:, 6144:9216].rearrange("p (h k) -> p h k", h=HEADS)
        qkf = qk[:, :, :, :].rearrange("p a c n -> p (a c n)")
        cik = prob[:, 0:256].rearrange("p (b d) -> p b d", b=STREAMS)
        cikrep = prob[:, 256:1280].rearrange("p (b r d) -> p b r d", b=STREAMS, r=4)
        ikrep = prob[:, 1280:1664].rearrange("p (t r d) -> p t r d", t=TILES, r=4)
        probs = prob[:, :].rearrange("p (h k) -> p h k", h=HEADS)
        gbuf = diag[:, :, :].rearrange("p a b -> p (a b)").rearrange("p (s c) -> p s c", s=2)
        gtile = prob[:, :]
        ringf = ring[:, :, :].rearrange("p s c -> p (s c)")
        sc = ringf[:, 0:6144].rearrange("p (t g k) -> p t g k", t=TILES, g=16)
        cand = prob[:, :].rearrange("p (h k) -> p h k", h=PEER_H)
        pick = [ringf[:, 6144:8192].rearrange("p (h k j) -> p h k j", h=PEER_H, k=PEER_K),
                qkf[:, 0:2048].rearrange("p (h k j) -> p h k j", h=PEER_H, k=PEER_K)]

        wide = psum("wide", [P, 4, 512])
        widef = wide[:, :, :].rearrange("p b c -> p (b c)")
        logits = widef.rearrange("p (h k) -> p h k", h=HEADS)
        trans = [psum("transA", [P, 512]), psum("transB", [P, 512])]
        accum = [psum("accumA", [P, 512]), psum("accumB", [P, 512])]

        bias_rows = nc.dram_tensor("bias_rows", [P, HEADS * EXT], F32).ap()
        gates_dram = nc.dram_tensor("gates_dram", [TILES, P, 4 * 512], F32).ap()

        def slot_weights(n):
            if n < NG:
                c = GROUPS[n][2]
                return ring[:, n % 2, 0:DC * c].rearrange("p (k c) -> p k c", k=DC)
            if n < NG + 2:
                return ring[:, n % 2, :].rearrange("p (k c) -> p k c", k=PAIRS)
            return ring[:, n % 2, :].rearrange("p (k c) -> p k c", k=DC)

        def weights_dram(n):
            if n < NG:
                _, c0, c = GROUPS[n]
                return i["w_in"][:, c0:c0 + c].rearrange("(k p) c -> p k c", p=P)
            if n < NG + 2:
                w = i["w_br_a"] if n == NG else i["w_br_b"]
                return w.rearrange("(k p) c -> p k c", p=P)
            if n < NG + 4:
                c0 = 512 * (n - NG - 2)
                return i["w_out"][:, c0:c0 + 512].rearrange("(k p) c -> p k c", p=P)
            c0 = 512 * (n - NG - 4)
            return i["w_pq"][:, c0:c0 + 512].rearrange("(k p) c -> p k c", p=P)

        NW = NG + 8
        BR, OUT, PQ = NG, NG + 2, NG + 4

        def weights_wait(eng, n):
            eng.wait_ge(S(f"weights_in{n % 2}"), 16 * (n // 2 + 1))

        def at(h):
            return (h % 2) * 4 + h // 2

        def at_index(h):
            return (h % 4) * 2 + h // 4

        def toks(t):
            return slice(t * P, t * P + P)

        def to_all_rows(row):
            return bass.AP(tensor=row.tensor, offset=row.offset, ap=[[0, P], [1, row.shape[-1]]])

        BATCHES = [("h", t, half) for t in range(TILES) for half in range(2)]
        BATCHES += [("cik", half) for half in range(2)] + [("index", t) for t in range(TILES)]
        for br in range(2):
            BATCHES += [("q", br, t) for t in range(TILES)] + [("k", br, t) for t in range(TILES)]
            for t in range(TILES):
                if t == SAMPLE:
                    BATCHES += [("cache", br, hp, half) for hp in range(PAIRS) for half in range(2)]
                BATCHES += [("prob", br, t, hp) for hp in range(PAIRS)]
        BATCHES += [("centroids",)]
        BATCHES += [("merged", t, half) for t in range(TILES) for half in range(2)]
        BATCHES += [("h2", t, half) for t in range(TILES) for half in range(2)]

        def batch(*key):
            return BATCHES.index(key)

        block = ctx.enter_context(nc.Block())

        @block.sync
        def _(sp):
            for t in range(TILES):
                src = i["x_prompt"][0, toks(t), :] if t < SAMPLE else i["x_sample"].rearrange("b s c -> (b s) c")
                sp.dma_start(xin[:, t, :], src).then_inc(S(f"x_in{t}"), 16)
                if t == 0:
                    sp.dma_start(gain[:, :], to_all_rows(i["g_attn"])).then_inc(S("gain_in"), 16)
                    for n in range(2):
                        sp.dma_start(slot_weights(n), weights_dram(n)).then_inc(S(f"weights_in{n}"), 16)
            sp.dma_start(ropet[:, :, :, :], i["rope_head"]).then_inc(S("rope_in"), 16)
            sp.dma_start(ropei[:, :, :, :], i["rope_index"]).then_inc(S("rope_in"), 16)
            for n, g in enumerate(("g_qa", "g_ka", "g_qb", "g_kb")):
                sp.dma_start(hgain[:, n, :], to_all_rows(i[g])).then_inc(S("rope_in"), 16)
            sp.dma_start(igain[:, :], to_all_rows(i["g_ik"])).then_inc(S("rope_in"), 16)
            sp.dma_start(rbias, bass.AP(tensor=i["rel_bias"].tensor, offset=i["rel_bias"].offset,
                                        ap=[[0, P], [2 * REL + 1, HEADS], [1, 2 * REL + 1]])).then_inc(S("rbias_in"), 16)
            sp.dma_start(cik, i["cache_a_ik"][0].rearrange("b k d -> k b d")).then_inc(S("cik_in"), 16)
            sp.wait_ge(S("ext_built"), 1)
            sp.dma_start(bias_rows, ext.rearrange("p h k -> p (h k)")).then_inc(S("ext_stored"), 16)
            sp.wait_ge(S("ext_stored"), 16)

            def skew(rows, first, keys):
                for odd in range(2):
                    yield odd, bass.AP(tensor=bias_rows.tensor, offset=bias_rows.offset + odd * EXT + first,
                                       ap=[[HEADS * EXT - 1, rows], [2 * EXT, 4], [1, keys]])

            nbias = 0
            for kind, first in ((B_NEAR, 255), (B_FAR, 127)):
                for odd, src in skew(P, first, P):
                    sp.dma_start(bias[:, kind, 4 * odd:4 * odd + 4, :], src).then_inc(S("bias_in"), 16)
                    nbias += 1
            sp.wait_ge(S("bias_cleared"), 1)
            for b in range(STREAMS):
                rows = slice(b * NEW, b * NEW + NEW)
                for odd, src in skew(NEW, 127, P):
                    sp.dma_start(bias[rows, B_CACHE, 4 * odd:4 * odd + 4, :], src).then_inc(S("bias_in"), 16)
                for odd, src in skew(NEW, 255, NEW):
                    sp.dma_start(bias[rows, B_OWN, 4 * odd:4 * odd + 4, rows], src).then_inc(S("bias_in"), 16)
                nbias += 4
            assert nbias == 36
            for n in range(2, NG):
                sp.wait_ge(S("group_done"), TILES * (n - 1))
                sp.dma_start(slot_weights(n), weights_dram(n)).then_inc(S(f"weights_in{n % 2}"), 16)

            def cache_load(what, n):
                br, hp = divmod(n, PAIRS)
                name = f"cache_{'ab'[br]}_{what}"
                src = i[name][0].rearrange("b k h d -> k b (h d)")[:, :, hp * P:hp * P + P]
                if n >= 2:
                    b2, hp2 = divmod(n - 2, PAIRS)
                    if what == "k":
                        sp.wait_ge(S("transposed"), batch("cache", b2, hp2, 1) + 1)
                    else:
                        sp.wait_ge(S("pv_done"), (b2 * TILES + SAMPLE) * PAIRS + hp2 + 1)
                dst = raw if what == "k" else vc
                sp.dma_start(dst[:, n % 2], src).then_inc(S(f"{what}cache_in{n % 2}"), 16)

            sp.wait_ge(S("transposes_copied"), 2 * TILES)
            for n in range(2):
                cache_load("k", n)
                cache_load("v", n)
            for n in range(BR, BR + 2):
                sp.wait_ge(S("group_done"), TILES * (n - 1))
                sp.dma_start(slot_weights(n), weights_dram(n)).then_inc(S(f"weights_in{n % 2}"), 16)
            for what, first, last in (("k", 2, 6), ("v", 2, 6), ("k", 6, 8), ("v", 6, 8)):
                for n in range(first, last):
                    cache_load(what, n)
            sp.wait_ge(S("attended"), 6)
            for n in range(2):
                sp.dma_start(probT[:, 0, n * P:n * P + P], i[f"peer_c{n + 1}"][0]).then_inc(S("centroids_in"), 16)
            for t in range(TILES):
                src = i["x_prompt"][0, toks(t), :] if t < SAMPLE else i["x_sample"].rearrange("b s c -> (b s) c")
                if t == 0:
                    sp.wait_ge(S("state_stored"), 16 * 10)
                sp.dma_start(x1[:, t, :], src).then_inc(S(f"x_again{t}"), 16)
            sp.dma_start(gain[:, :], to_all_rows(i["g_ffn"])).then_inc(S("gain_in"), 16)
            for t in range(TILES):
                if t == 0:
                    sp.wait_ge(S("gates_stored0"), 16 * 6)
                    sp.wait_ge(S("gates_stored1"), 16 * 6)
                else:
                    sp.wait_ge(S("merged_ready"), t)
                sp.dma_start(gtile, gates_dram[t]).then_inc(S("gates_in"), 16)
            sp.wait_ge(S("branches_done"), TILES)
            for n in (OUT, OUT + 1):
                sp.dma_start(slot_weights(n), weights_dram(n)).then_inc(S(f"weights_in{n % 2}"), 16)
            for n in range(PQ, NW):
                if n < PQ + 2:
                    sp.wait_ge(S("out_done"), TILES * (n - PQ + 1))
                else:
                    sp.wait_ge(S("query_done"), 4 * (n - PQ - 1))
                sp.dma_start(slot_weights(n), weights_dram(n)).then_inc(S(f"weights_in{n % 2}"), 16)
            for t in range(TILES):
                sp.wait_ge(S("y_ready"), t + 1)
                dst = o["y_prompt"][0, toks(t), :] if t < SAMPLE else o["y_sample"].rearrange("b s c -> (b s) c")
                sp.dma_start(dst, x1[:, t, :]).then_inc(S("y_stored"), 16)
            sp.wait_ge(S("y_stored"), 16 * TILES)

        @block.gpsimd
        def _(pool):
            pool.memset(mhalf[:, :], -0.5).then_inc(S("pool_set"), 1)
            pool.memset(ident[:, :], 0.0).then_inc(S("pool_set"), 1)
            pool.wait_ge(S("pool_set"), 2)
            pool.affine_select(out=ident[:, :], in_=ident[:, :], compare_op=ALU.not_equal, fill=1.0, base=0,
                               pattern=[[-1, P]], channel_multiplier=1).then_inc(S("ident_set"), 1)
            pool.iota(iota16[:, :], pattern=[[1, 16]], base=0, channel_multiplier=0,
                      allow_small_or_imprecise_dtypes=True).then_inc(S("iota_set"), 1)
            own3 = own[:, :].rearrange("p (b j) -> p b j", j=NEW)
            pool.memset(own[:, :], 0.0).then_inc(S("pool_set"), 1)
            pool.memset(qm[:, :, :], 0.0).then_inc(S("pool_set"), 1)
            pool.wait_ge(S("pool_set"), 4)
            pool.affine_select(out=own3, in_=own3, compare_op=ALU.is_ge, fill=NEG, base=0,
                               pattern=[[-NEW, STREAMS], [0, NEW]], channel_multiplier=1).then_inc(S("pool_set"), 1)
            pool.wait_ge(S("pool_set"), 5)
            pool.affine_select(out=own3, in_=own3, compare_op=ALU.is_ge, fill=NEG, base=NEW - 1,
                               pattern=[[NEW, STREAMS], [0, NEW]], channel_multiplier=-1).then_inc(S("own_set"), 1)

            def inverse_rms(src, dst, n, width, signalled):
                chain(pool, pool.tensor_scalar(src, src, 1.0 / width, EPS, ALU.mult, ALU.add), "pool_step")
                signal(pool.tensor_tensor(dst, src, mhalf[:, 0:n], ALU.pow), signalled)

            for t in range(TILES):
                pool.wait_ge(S("squares_summed"), t + 1)
                inverse_rms(ssx[:, 0, t:t + 1], rsx[:, 0, t:t + 1], 1, D, "row_scale")

            def store_state(src, prompt, sample, width):
                pool.dma_start(prompt.rearrange("(t p) c -> p t c", p=P), src[:, 0:2, 0:width]).then_inc(
                    S("state_stored"), 16)
                pool.dma_start(sample, src[:, 2, 0:width]).then_inc(S("state_stored"), 16)

            def flat_state(name, heads=True):
                p, s = o[name + "_prompt"], o[name + "_sample"]
                if heads:
                    return p[0, 0].rearrange("t h d -> t (h d)"), s[0].rearrange("b t h d -> (b t) (h d)")
                return p[0, 0], s[0].rearrange("b t d -> (b t) d")

            def store_gates(g):
                for t in range(TILES):
                    u = (g - 7) * TILES + t
                    pool.wait_ge(S("gate_copied"), u + 1)
                    pool.dma_start(gates_dram[t, :, (g - 7) * 512:(g - 6) * 512], gbuf[:, u % 2, :]).then_inc(
                        S(f"gates_stored{u % 2}"), 16)

            for g, (name, _, _) in enumerate(GROUPS):
                if name in ("aq", "ak", "bq", "bk"):
                    k = ("aq", "ak", "bq", "bk").index(name)
                    pool.wait_ge(S("heads_squared"), k + 1 if k < 2 else k + 2)
                    inverse_rms(ssh[:, k, :], rsh[:, k, :], 24, HD, "head_scale")
                if name == "ix":
                    pool.wait_ge(S("heads_squared"), 3)
                    inverse_rms(ssh[:, 4, 0:3], rsh[:, 4, 0:3], 3, ID, "head_scale")
                    pool.wait_ge(S("ik_ready"), 1)
                    store_state(ix[:, :, 256:288], *flat_state("a_ik", False), ID)
                if name in ("ak", "bk"):
                    pool.wait_ge(S("heads_ready"), 2 if name == "ak" else 4)
                    store_state(qkv[:, where[name]], *flat_state("a_k" if name == "ak" else "b_k"), 512)
                if name in ("av", "bv"):
                    pool.wait_ge(S("group_copied"), TILES * (g + 1))
                    store_state(qkv[:, where[name]], *flat_state("a_v" if name == "av" else "b_v"), 512)
                if name.startswith("gate"):
                    store_gates(g)
            for t in range(TILES):
                pool.wait_ge(S("squares_summed"), TILES + t + 1)
                inverse_rms(ssx[:, 1, t:t + 1], rsx[:, 1, t:t + 1], 1, D, "row_scale")

            pool.wait_ge(S("score_done"), TILES)
            u_rows, v_rows = i["peer_u"][0], i["peer_v"][0]

            def gather(t, j):
                for sub in range(2):
                    n = (j * 2) + (t * ROUNDS + sub)
                    first = isinstance(n, int) and n == 0
                    pool.tensor_copy(staged[:, sub, :], expert[:, t, bass.ds(j * 2 * RING + sub * RING, RING)]).then_inc(
                        S(f"experts_staged{sub}"), 1)
                    pool.wait_ge(S(f"experts_staged{sub}"), j + (t * ROUNDS // 2 + 1))
                    for s in range(RING):
                        if not first:
                            pool.wait_ge(S("dot_done"), n * RING + (s + 1 - RING))
                            pool.sem_inc(S("u_slot_free"), 1)
                        pool.indirect_dma_start(ubuf[:, s, :], None, u_rows,
                                                bass.IndirectOffsetOnAxis(ap=staged[:, sub, s:s + 1], axis=0)
                                                ).then_inc(S(f"u_rows{s}"), 16)
                    for s in range(RING):
                        if not first:
                            pool.wait_ge(S("v_added"), n * RING + (s + 1 - RING))
                            pool.sem_inc(S("v_slot_free"), 1)
                        pool.indirect_dma_start(vbuf[:, s, :], None, v_rows,
                                                bass.IndirectOffsetOnAxis(ap=staged[:, sub, s:s + 1], axis=0)
                                                ).then_inc(S(f"v_rows{s}"), 16)

            for t in range(TILES):
                pool.wait_ge(S("routed"), t + 1)
                if t == 0:
                    gather(0, 0)
                with pool.Fori(1 if t == 0 else 0, ROUNDS // 2) as j:
                    gather(t, j)
            pool.wait_ge(S("state_stored"), 16 * 10)

        @block.scalar
        def _(act):
            for t in range(TILES):
                act.wait_ge(S(f"x_in{t}"), 16)
                chain(act, act.activation(flat[:, 0:D], xin[:, t, :], ACT.Square, accum_out=ssx[:, 0, t:t + 1]),
                      "squares_summed")

            def copy_out(key, pieces, *waits):
                n = batch(*key)
                act.wait_ge(S("transposed"), n + 1)
                for name, value in waits:
                    act.wait_ge(S(name), value)
                for m, (dst, c0, c1) in enumerate(pieces):
                    src = trans[n % 2][:, c0:c1]
                    if len(dst.shape) == 3:
                        src = src.rearrange("p (c n) -> p c n", c=dst.shape[1])
                    ins = act.activation(dst, src, ACT.Copy)
                    if m == len(pieces) - 1:
                        ins.then_inc(S("transposes_copied"), 1)

            def copy_rows(name, t, half):
                copy_out((name, t, half), [(hT[:, 4 * half:4 * half + 4, toks(t)], 0, 512)])

            for t in range(TILES):
                for half in range(2):
                    copy_rows("h", t, half)
            for g, (name, _, cols) in enumerate(GROUPS):
                if name == "ak":
                    act.wait_ge(S("ext_built"), 1)
                if name == "bk":
                    act.wait_ge(S("ext_stored"), 16)
                for t in range(TILES):
                    u = g * TILES + t
                    act.wait_ge(S("group_done"), u + 1)
                    if name.startswith("gate"):
                        m = u - 7 * TILES
                        if m >= 2:
                            act.wait_ge(S(f"gates_stored{m % 2}"), 16 * (m // 2))
                        act.activation(gbuf[:, m % 2, :], accum[u % 2][:, :], ACT.Sigmoid).then_inc(S("gate_copied"), 1)
                    else:
                        dst = ix[:, t, :] if name == "ix" else qkv[:, where[name], t, :]
                        act.activation(dst, accum[u % 2][:, 0:cols], ACT.Copy).then_inc(S("group_copied"), 1)
            for half in range(2):
                copy_out(("cik", half), [(cikT[:, 4 * half:4 * half + 4, :], 0, 512)])
            for t in range(TILES):
                copy_out(("index", t), [(iqT[:, :, toks(t)], 0, 256), (ikT[:, toks(t)], 256, 384)])

            def heads_out(br):
                for m, name in enumerate("qk"):
                    for t in range(TILES):
                        copy_out((name, br, t), [(qk[:, m, :, toks(t)], 0, 512)])

            heads_out(0)
            for t in range(TILES):
                act.wait_ge(S("index_done"), t + 1)
                if t:
                    act.wait_ge(S("scored"), t)
                act.activation(probs[:, :, 0:SEEN[t]], logits[:, :, 0:SEEN[t]], ACT.Relu).then_inc(S("relu_done"), 1)
            for br in range(2):
                if br:
                    heads_out(1)
                for t in range(TILES):
                    r = br * TILES + t
                    nk = SEEN[t] // P
                    if t == SAMPLE:
                        for hp in range(PAIRS):
                            n = br * PAIRS + hp
                            for half in range(2):
                                waits = [("pair_scored", n - 1)] if n >= 2 else []
                                copy_out(("cache", br, hp, half), [(kcT[:, n % 2, 4 * half:4 * half + 4, :], 0, 512)],
                                         *waits)
                    act.wait_ge(S("rowmax_ready"), r + 1)
                    for h in range(HEADS):
                        act.activation(probs[:, h, 0:SEEN[t]], probs[:, h, 0:SEEN[t]], ACT.Exp, bias=rowmax[:, h:h + 1],
                                       accum_out=rowsum[:, h:h + 1]).then_inc(S("exp_done"), 1)
                    for hp in range(PAIRS):
                        m = r * PAIRS + hp
                        waits = [("pv_done", m - 1)] if m >= 2 else []
                        copy_out(("prob", br, t, hp), [(probT[:, hp % 2, 0:2 * nk * P], 0, 2 * nk * P)], *waits)
                    act.wait_ge(S("pv_done"), (r + 1) * PAIRS)
                    act.activation(oT[br][:, :, toks(t)], accum[r % 2][:, :].rearrange("p (c n) -> p c n", c=PAIRS),
                                   ACT.Copy).then_inc(S("attended"), 1)
            copy_out(("centroids",), [(cT[:, :, :], 0, 256)])
            for t in range(TILES):
                for half in range(2):
                    copy_rows("merged", t, half)
            for t in range(TILES):
                act.wait_ge(S("x1_added"), TILES + t + 1)
                chain(act, act.activation(prob[:, 0:D], x1[:, t, :], ACT.Square, accum_out=ssx[:, 1, t:t + 1]),
                      "squares_summed")
            for t in range(TILES):
                for half in range(2):
                    copy_rows("h2", t, half)
            for u in range(16):
                act.wait_ge(S("query_done"), u + 1)
                act.activation(pqT[:, u, :], accum[u % 2][:, 0:NTOK], ACT.Copy).then_inc(S("query_copied"), 1)
            for t in range(TILES):
                act.wait_ge(S("score_done"), t + 1)
                act.activation(sc[:, t, :, :], widef.rearrange("p (g k) -> p g k", g=16), ACT.Copy).then_inc(
                    S("router_copied"), 1)

            def softmax_exp(t):
                act.wait_ge(S("picked"), t + 1)
                act.activation(sv[:, :, :], sv[:, :, :], ACT.Exp).then_inc(S("expert_exp"), 1)

            def weigh(t, j):
                for sub in range(2):
                    n = (j * 2) + (t * ROUNDS + sub)
                    known = isinstance(n, int)
                    act.wait_ge(S("dot_done"), n * RING + RING)
                    act.activation(gelu[:, sub, :], dots[:, sub, :], ACT.Gelu).then_inc(S("gelu_done"), 1)
                    act.wait_ge(S("wexp_ready"), n + 1)
                    for s in range(RING):
                        if not (known and n == 0):
                            act.wait_ge(S("v_added"), n * RING + (s + 1 - RING))
                        act.activation(diag[:, s, :], ident[:, :], ACT.Copy, scale=wexp[:, sub, s:s + 1]).then_inc(
                            S("diag_done"), 1)

            softmax_exp(0)
            for t in range(TILES):
                if t == 0:
                    weigh(0, 0)
                with act.Fori(1 if t == 0 else 0, MIDDLE) as j:
                    weigh(t, j)
                if t + 1 < TILES:
                    softmax_exp(t + 1)
                with act.Fori(MIDDLE, ROUNDS // 2) as j:
                    weigh(t, j)

        @block.tensor
        def _(pe):
            pe.wait_ge(S("ident_set"), 1)

            def transposes(key, sources):
                n = batch(*key)
                if n >= 2:
                    pe.wait_ge(S("transposes_copied"), n - 1)
                for m, src in enumerate(sources):
                    ins = pe.transpose(trans[n % 2][:, m * P:m * P + P], src, ident[:, :])
                ins.then_inc(S("transposed"), 1)

            def rows(name, src, t, half):
                transposes((name, t, half), [src[:, t, c * P:c * P + P] for c in range(4 * half, 4 * half + 4)])

            for t in range(TILES):
                pe.wait_ge(S("h_ready"), t + 1)
                for half in range(2):
                    rows("h", hin, t, half)
            pe.wait_ge(S("transposes_copied"), 2 * TILES)
            for g, (name, _, cols) in enumerate(GROUPS):
                weights_wait(pe, g)
                w = slot_weights(g)
                for t in range(TILES):
                    u = g * TILES + t
                    if u >= 2:
                        if u - 2 < 7 * TILES:
                            pe.wait_ge(S("group_copied"), u - 1)
                        else:
                            pe.wait_ge(S("gate_copied"), u - 1 - 7 * TILES)
                    for c in range(DC):
                        ins = pe.matmul(accum[u % 2][:, 0:cols], hT[:, c, toks(t)], w[:, c, :], start=c == 0,
                                        stop=c == DC - 1)
                    ins.then_inc(S("group_done"), 1)
            pe.wait_ge(S("index_ready"), 1)
            pe.wait_ge(S("heads_ready"), 4)
            for half in range(2):
                transposes(("cik", half), [cikrep[:, b].rearrange("p r d -> p (r d)")
                                           for b in range(4 * half, 4 * half + 4)])
            for t in range(TILES):
                transposes(("index", t), [ix[:, t, 0:P], ix[:, t, P:2 * P], ikrep[:, t].rearrange("p r d -> p (r d)")])

            def heads_in(br):
                for name, w in (("q", BQ if br else AQ), ("k", BK if br else AK)):
                    for t in range(TILES):
                        transposes((name, br, t), [qkv[:, w, t, hp * P:hp * P + P] for hp in range(PAIRS)])

            heads_in(0)
            pe.wait_ge(S("transposes_copied"), batch("index", 2) + 1)
            for t in range(TILES):
                if t:
                    pe.wait_ge(S("relu_done"), t)
                if t == SAMPLE:
                    pe.wait_ge(S("iqm_ready"), 1)
                for h in range(IH):
                    r0 = ID * (h % 4)
                    part = slice(r0, r0 + ID)
                    c0 = at_index(h) * 256
                    q = iqT[part, h // 4, toks(t)]
                    if t < SAMPLE:
                        ins = pe.matmul(widef[:, c0:c0 + SEEN[t]], q, ikT[part, 0:SEEN[t]], start=True, stop=True,
                                        tile_position=(r0, 0))
                    else:
                        for b in range(STREAMS):
                            pe.matmul(widef[:, c0:c0 + P], qm[part, h // 4, b * P:b * P + P], cikT[part, b, :],
                                      start=b == 0, stop=b == STREAMS - 1, tile_position=(r0, 0))
                        ins = pe.matmul(widef[:, c0 + P:c0 + 2 * P], q, ikT[part, toks(SAMPLE)], start=True, stop=True,
                                        tile_position=(r0, 0))
                ins.then_inc(S("index_done"), 1)

            def score_heads(br, t):
                r = br * TILES + t
                if r == 0:
                    pe.wait_ge(S("relu_done"), TILES)
                else:
                    pe.wait_ge(S("logits_read"), r)
                if t == 0:
                    pe.wait_ge(S("transposes_copied"), batch("k", br, 2) + 1)
                if t < SAMPLE:
                    for hp in range(PAIRS):
                        for odd in range(2):
                            part = slice(HD * odd, HD * odd + HD)
                            c0 = (odd * 4 + hp) * 256
                            ins = pe.matmul(widef[:, c0:c0 + SEEN[t]], qk[part, 0, hp, toks(t)],
                                            qk[part, 1, hp, 0:SEEN[t]], start=True, stop=True)
                    ins.then_inc(S("logits_done"), 1)
                    return
                for hp in range(PAIRS):
                    n = br * PAIRS + hp
                    pe.wait_ge(S(f"kcache_in{n % 2}"), 16 * (n // 2 + 1))
                    for half in range(2):
                        transposes(("cache", br, hp, half), [raw[:, n % 2, b] for b in range(4 * half, 4 * half + 4)])
                    pe.wait_ge(S("transposes_copied"), batch("cache", br, hp, 1) + 1)
                    pe.wait_ge(S("qm_ready"), n + 1)
                    for odd in range(2):
                        part = slice(HD * odd, HD * odd + HD)
                        c0 = (odd * 4 + hp) * 256
                        pe.matmul(widef[:, c0 + P:c0 + 2 * P], qk[part, 0, hp, toks(t)], qk[part, 1, hp, toks(t)],
                                  start=True, stop=True)
                        for b in range(STREAMS):
                            ins = pe.matmul(widef[:, c0:c0 + P], qm[part, n % 2, b * P:b * P + P],
                                            kcT[part, n % 2, b, :], start=b == 0, stop=b == STREAMS - 1)
                    ins.then_inc(S("pair_scored"), 1)

            def weigh_values(br, t):
                r = br * TILES + t
                nk = SEEN[t] // P
                v = BV if br else AV
                pe.wait_ge(S("probs_ready"), r + 1)
                if r < 2:
                    pe.wait_ge(S("gate_copied"), 4 * TILES)
                else:
                    pe.wait_ge(S("attended"), r - 1)
                for hp in range(PAIRS):
                    transposes(("prob", br, t, hp), [probs[:, odd * 4 + hp, k * P:k * P + P]
                                                     for odd in range(2) for k in range(nk)])
                    pe.wait_ge(S("transposes_copied"), batch("prob", br, t, hp) + 1)
                    if t == SAMPLE:
                        n = br * PAIRS + hp
                        pe.wait_ge(S(f"vcache_in{n % 2}"), 16 * (n // 2 + 1))
                    for odd in range(2):
                        out = accum[r % 2][HD * odd:HD * odd + HD, hp * P:hp * P + P]
                        cols = slice(hp * P + HD * odd, hp * P + HD * odd + HD)
                        if t < SAMPLE:
                            for k in range(nk):
                                ins = pe.matmul(out, qkv[:, v, k, cols], probT[:, hp % 2, (odd * nk + k) * P:
                                                                               (odd * nk + k) * P + P],
                                                start=k == 0, stop=k == nk - 1)
                        else:
                            p0 = odd * 2 * P
                            pe.matmul(out, qkv[:, v, SAMPLE, cols], probT[:, hp % 2, p0 + P:p0 + 2 * P], start=True,
                                      stop=False, skip_group_check=True)
                            for b in range(STREAMS):
                                ins = pe.matmul(out[:, b * NEW:b * NEW + NEW], vc[:, n % 2, b, HD * odd:HD * odd + HD],
                                                probT[:, hp % 2, p0 + b * NEW:p0 + b * NEW + NEW], start=False,
                                                stop=b == STREAMS - 1, skip_group_check=True)
                    ins.then_inc(S("pv_done"), 1)

            for br in range(2):
                if br:
                    heads_in(1)
                for t in range(TILES):
                    score_heads(br, t)
                    weigh_values(br, t)
            pe.wait_ge(S("centroids_in"), 32)
            transposes(("centroids",), [probT[:, 0, n * P:n * P + P] for n in range(2)])
            weights_wait(pe, BR)
            weights_wait(pe, BR + 1)
            pe.wait_ge(S("attended"), 6)
            pe.wait_ge(S("logits_read"), 6)
            for t in range(TILES):
                if t:
                    pe.wait_ge(S("branches_read"), t)
                for br in range(2):
                    for n in range(2):
                        for c in range(PAIRS):
                            ins = pe.matmul(wide[:, 2 * br + n, :], oT[br][:, c, toks(t)],
                                            slot_weights(BR + br)[:, c, 512 * n:512 * n + 512], start=c == 0,
                                            stop=c == PAIRS - 1)
                ins.then_inc(S("branches_done"), 1)
            for t in range(TILES):
                pe.wait_ge(S("merged_ready"), t + 1)
                for half in range(2):
                    rows("merged", merged, t, half)
            for n in range(2):
                weights_wait(pe, OUT + n)
                for t in range(TILES):
                    u = n * TILES + t
                    pe.wait_ge(S("transposes_copied"), batch("merged", t, 1) + 1)
                    if u >= 2:
                        pe.wait_ge(S("x1_added"), u - 1)
                    for c in range(DC):
                        ins = pe.matmul(accum[u % 2][:, :], hT[:, c, toks(t)], slot_weights(OUT + n)[:, c, :],
                                        start=c == 0, stop=c == DC - 1)
                    ins.then_inc(S("out_done"), 1)
            for t in range(TILES):
                pe.wait_ge(S("h_ready"), TILES + t + 1)
                for half in range(2):
                    rows("h2", h2, t, half)
            pe.wait_ge(S("transposes_copied"), len(BATCHES))
            for u in range(16):
                if u % 4 == 0:
                    weights_wait(pe, PQ + u // 4)
                pe.wait_ge(S("x1_added"), 6) if u < 2 else pe.wait_ge(S("query_copied"), u - 1)
                for c in range(DC):
                    ins = pe.matmul(accum[u % 2][:, 0:NTOK], slot_weights(PQ + u // 4)[:, c, (u % 4) * P:(u % 4) * P + P],
                                    hT[:, c, :], start=c == 0, stop=c == DC - 1)
                ins.then_inc(S("query_done"), 1)
            pe.wait_ge(S("query_copied"), 16)
            pe.wait_ge(S("branches_read"), TILES)
            for t in range(TILES):
                if t:
                    pe.wait_ge(S("router_copied"), t)
                for u in range(16):
                    ins = pe.matmul(widef[:, u * P:u * P + P], pqT[:, u, toks(t)], cT[:, u % 2, :], start=True, stop=True)
                ins.then_inc(S("score_done"), 1)

            def add_rows(t, j, start=False, stop=False):
                bank = trans if t % 2 else accum
                for sub in range(2):
                    n = (j * 2) + (t * ROUNDS + sub)
                    for s in range(RING):
                        pe.wait_ge(S("diag_done"), n * RING + (s + 1))
                        pe.wait_ge(S(f"v_rows{s}"), n * 16 + 16)
                        for m in range(2):
                            ins = pe.matmul(bank[m][:, :], diag[:, s, :], vbuf[:, s, m * 512:m * 512 + 512],
                                            start=start and sub == 0 and s == 0,
                                            stop=stop and sub == 1 and s == RING - 1)
                        ins.then_inc(S("v_added"), 1)

            for t in range(TILES):
                if t == 2:
                    pe.wait_ge(S("y_ready"), 1)
                add_rows(t, 0, start=True)
                with pe.Fori(1, ROUNDS // 2 - 1) as j:
                    add_rows(t, j)
                add_rows(t, ROUNDS // 2 - 1, stop=True)

        @block.vector
        def _(v):
            def step(ins, name="dve_step"):
                chain(v, ins, name)

            step(v.memset(bias[:, B_OWN], NEG), "bias_cleared")
            v.wait_ge(S("rbias_in"), 16)
            step(v.tensor_copy(ext[:, :, 0:REL - 1],
                               rbias[:, :, 2 * REL:2 * REL + 1].to_broadcast([P, HEADS, REL - 1])))
            step(v.tensor_copy(ext[:, :, REL - 1:EXT], rbias[:, :, ::-1]), "ext_built")
            v.wait_ge(S("gain_in"), 16)
            for t in range(TILES):
                v.wait_ge(S("row_scale"), t + 1)
                signal(v.scalar_tensor_tensor(out=hin[:, t, :], in0=xin[:, t, :], scalar=rsx[:, 0, t:t + 1],
                                              in1=gain[:, :], op0=ALU.mult, op1=ALU.mult), "h_ready")
            v.wait_ge(S("cik_in"), 16)
            step(v.tensor_copy(cikrep, cik.unsqueeze(2).to_broadcast([P, STREAMS, 4, ID])))
            v.wait_ge(S("bias_in"), 16 * 36)
            step(v.memset(bias[0:CHUNK, B_NEAR, :, CHUNK:P], NEG), "bias_masked")

            def rope(x, cos, sin, half, tmp, ready):
                lo, hi = x[..., 0:half], x[..., half:2 * half]
                signal(v.tensor_tensor(tmp[0], lo, cos, ALU.mult), "dve_step")
                signal(v.tensor_tensor(tmp[1], hi, sin, ALU.mult), "dve_step")
                signal(v.tensor_tensor(tmp[2], hi, cos, ALU.mult), "dve_step")
                step(v.tensor_tensor(tmp[3], lo, sin, ALU.mult))
                step(v.tensor_tensor(lo, tmp[0], tmp[1], ALU.subtract))
                step(v.tensor_tensor(hi, tmp[2], tmp[3], ALU.add), ready)

            v.wait_ge(S("rope_in"), 16 * 7)
            head = 0
            for g, (name, _, _) in enumerate(GROUPS):
                if name in ("aq", "ak", "bq", "bk"):
                    k = ("aq", "ak", "bq", "bk").index(name)
                    v.wait_ge(S("group_copied"), TILES * (g + 1))
                    x = qkv[:, where[name]].rearrange("p t (h d) -> p (t h) d", d=HD)
                    sq = qkf[:, 0:1536].rearrange("p (n d) -> p n d", d=HD)
                    step(v.tensor_tensor(sq, x, x, ALU.mult))
                    step(v.tensor_reduce(ssh[:, k, :], sq, AX, ALU.add), "heads_squared")
                    head += 1
                    v.wait_ge(S("head_scale"), head)
                    step(v.tensor_tensor(x, x, rsh[:, k, :].unsqueeze(2).to_broadcast([P, 24, HD]), ALU.mult))
                    last = v.tensor_tensor(x, x, hgain[:, k:k + 1, :].to_broadcast([P, 24, HD]), ALU.mult)
                    if name[0] == "b":
                        step(last, "heads_ready")
                        continue
                    step(last)
                    tmp = [qkf[:, m * 768:m * 768 + 768].rearrange("p (t h d) -> p t h d", t=TILES, h=HEADS)
                           for m in range(4)]
                    cs = [ropet[:, m].unsqueeze(2).to_broadcast([P, TILES, HEADS, HD // 2]) for m in range(2)]
                    rope(qkv[:, where[name]].rearrange("p t (h d) -> p t h d", d=HD), cs[0], cs[1], HD // 2, tmp,
                         "heads_ready")
                if name == "ix":
                    v.wait_ge(S("group_copied"), TILES * (g + 1))
                    ik = ix[:, :, 256:288]
                    sq = qkf[:, 0:96].rearrange("p (t d) -> p t d", d=ID)
                    step(v.tensor_tensor(sq, ik, ik, ALU.mult))
                    step(v.tensor_reduce(ssh[:, 4, 0:3], sq, AX, ALU.add), "heads_squared")
                    head += 1
                    step(v.tensor_scalar(ix[:, :, 288:296], ix[:, :, 288:296], IH ** -0.5, None, ALU.mult))
                    iq = ix[:, :, 0:256].rearrange("p t (h d) -> p t h d", d=ID)
                    tmp = [qkf[:, m * 384:m * 384 + 384].rearrange("p (t h d) -> p t h d", t=TILES, h=IH)
                           for m in range(4)]
                    cs = [ropei[:, m].unsqueeze(2).to_broadcast([P, TILES, IH, ID // 2]) for m in range(2)]
                    rope(iq, cs[0], cs[1], ID // 2, tmp, "iq_ready")
                    v.wait_ge(S("head_scale"), head)
                    step(v.tensor_tensor(ik, ik, rsh[:, 4, 0:3].unsqueeze(2).to_broadcast([P, TILES, ID]), ALU.mult))
                    step(v.tensor_tensor(ik, ik, igain[:, :].unsqueeze(1).to_broadcast([P, TILES, ID]), ALU.mult))
                    tmp = [qkf[:, m * 48:m * 48 + 48].rearrange("p (t d) -> p t d", t=TILES) for m in range(4)]
                    rope(ik, ropei[:, 0], ropei[:, 1], ID // 2, tmp, "ik_ready")
                    step(v.tensor_copy(ikrep, ik.unsqueeze(2).to_broadcast([P, TILES, 4, ID])), "index_ready")

            def streams_apart(dst, src):
                return v.tensor_copy(dst.rearrange("p (b c) -> p b c", c=P + NEW)[:, :, 0:NEW],
                                     src.rearrange("p (b j) -> p b j", j=NEW))

            v.wait_ge(S("pool_set"), 4)
            v.wait_ge(S("transposes_copied"), batch("index", 2) + 1)
            for c in range(2):
                ins = streams_apart(qm[:, c, :], iqT[:, c, toks(SAMPLE)])
                signal(ins, "dve_step" if c == 0 else "iqm_ready")

            v.wait_ge(S("own_set"), 1)
            for t in range(TILES):
                n = SEEN[t]
                v.wait_ge(S("relu_done"), t + 1)
                s = score[:, t, 0:n]
                for h in range(IH):
                    rel = probs[:, at_index(h), 0:n]
                    w = ix[:, t, 288 + h:289 + h]
                    if h == 0:
                        step(v.tensor_scalar(s, rel, w, None, ALU.mult))
                    else:
                        step(v.scalar_tensor_tensor(out=s, in0=rel, scalar=w, in1=s, op0=ALU.mult, op1=ALU.add),
                             "scored" if h == IH - 1 else "dve_step")
                if t < SAMPLE:
                    step(v.memset(score[0:CHUNK, t, n - CHUNK:n], NEG))
                else:
                    step(v.tensor_tensor(score[:, t, P:2 * P], score[:, t, P:2 * P], own[:, :], ALU.add))
                    step(v.memset(score[:, t, 256:264], PAD))
                for _ in range(SELECT[t] // 8):
                    step(v.max(mx8[:, :], s))
                    step(v.match_replace(s, mx8[:, :], s, TAKEN))
                if SELECT[t] % 8:
                    step(v.max(mx8[:, :], s))
                    step(v.memset(mx8[:, SELECT[t] % 8:8], PAD))
                    step(v.match_replace(score[:, t, :], mx8[:, :], score[:, t, :], TAKEN))
                step(v.tensor_scalar(mask[:, t, 0:n], s, TAKEN / 2, NEG, ALU.is_gt, ALU.mult), "mask_ready")

            for br in range(2):
                for t in range(TILES):
                    r = br * TILES + t
                    n = SEEN[t]
                    pr = probs[:, :, 0:n]
                    if t == SAMPLE:
                        v.wait_ge(S("transposes_copied"), batch("q", br, SAMPLE) + 1)
                        for hp in range(PAIRS):
                            m = br * PAIRS + hp
                            v.wait_ge(S("index_done"), TILES) if m < 2 else v.wait_ge(S("pair_scored"), m - 1)
                            signal(streams_apart(qm[:, m % 2, :], qk[:, 0, hp, toks(SAMPLE)]), "qm_ready")
                        v.wait_ge(S("pair_scored"), (br + 1) * PAIRS)
                    else:
                        v.wait_ge(S("logits_done"), br * 2 + t + 1)
                    if r:
                        v.wait_ge(S("transposed"), batch("prob", *divmod(r - 1, TILES), PAIRS - 1) + 1)
                    if br == 0:
                        step(v.scalar_tensor_tensor(out=pr, in0=logits[:, :, 0:n], scalar=HD ** -0.5,
                                                    in1=mask[:, t:t + 1, 0:n].to_broadcast([P, HEADS, n]),
                                                    op0=ALU.mult, op1=ALU.add), "logits_read")
                    else:
                        kinds = [[B_NEAR], [B_FAR, B_NEAR], [B_CACHE, B_OWN]][t]
                        for k, kind in enumerate(kinds):
                            step(v.scalar_tensor_tensor(out=probs[:, :, k * P:k * P + P],
                                                        in0=logits[:, :, k * P:k * P + P], scalar=HD ** -0.5,
                                                        in1=bias[:, kind], op0=ALU.mult, op1=ALU.add),
                                 "logits_read" if k == len(kinds) - 1 else "dve_step")
                    step(v.tensor_reduce(rowmax[:, :], pr, AX, ALU.max))
                    step(v.tensor_scalar(rowmax[:, :], rowmax[:, :], -1.0, None, ALU.mult), "rowmax_ready")
                    v.wait_ge(S("exp_done"), HEADS * (r + 1))
                    step(v.reciprocal(rowinv[:, :], rowsum[:, :]))
                    step(v.tensor_tensor(pr, pr, rowinv[:, :].unsqueeze(2).to_broadcast([P, HEADS, n]), ALU.mult),
                         "probs_ready")

            for t in range(TILES):
                v.wait_ge(S("branches_done"), t + 1)
                v.wait_ge(S("gates_in"), 16 * (t + 1))
                step(v.tensor_tensor(merged[:, t, :], widef[:, 0:D], gtile[:, 0:D], ALU.mult))
                step(v.tensor_tensor(qkf[:, 0:D], widef[:, D:2 * D], gtile[:, D:2 * D], ALU.mult), "branches_read")
                step(v.tensor_tensor(merged[:, t, :], merged[:, t, :], qkf[:, 0:D], ALU.add), "merged_ready")
            for n in range(2):
                for t in range(TILES):
                    u = n * TILES + t
                    v.wait_ge(S("out_done"), u + 1)
                    v.wait_ge(S(f"x_again{t}"), 16)
                    part = x1[:, t, n * 512:n * 512 + 512]
                    step(v.tensor_tensor(part, accum[u % 2][:, :], part, ALU.add), "x1_added")
            v.wait_ge(S("gain_in"), 32)
            for t in range(TILES):
                v.wait_ge(S("row_scale"), TILES + t + 1)
                signal(v.scalar_tensor_tensor(out=h2[:, t, :], in0=x1[:, t, :], scalar=rsx[:, 1, t:t + 1],
                                              in1=gain[:, :], op0=ALU.mult, op1=ALU.mult), "h_ready")

            def together(instructions, name="dve_step"):
                for ins in instructions:
                    signal(ins, name)
                v.wait_ge(sems[name], counts[name])

            def top16(values, top, index, rows):
                together(v.max(top(n)[:, 0:8], values(n)) for n in range(rows))
                together(v.max_index(index(n)[:, 0:8], top(n)[:, 0:8], values(n)) for n in range(rows))
                together(v.match_replace(values(n), top(n)[:, 0:8], values(n), TAKEN) for n in range(rows))
                together(v.max(top(n)[:, 8:16], values(n)) for n in range(rows))
                together(v.max_index(index(n)[:, 8:16], top(n)[:, 8:16], values(n)) for n in range(rows))

            def route(t):
                v.wait_ge(S("router_copied"), t + 1)
                top16(lambda n: sc[:, t, n, :], lambda n: rtop[:, n, :], lambda n: rtopi[:, n, :], 16)
                step(v.tensor_copy(rtopf[:, :, :], rtopi[:, :, :]))
                r4 = rtop[:, :, :].rearrange("p (h s) k -> p h s k", s=2)
                f4 = rtopf[:, :, :].rearrange("p (h s) k -> p h s k", s=2)
                full = [P, PEER_H, PEER_K, PEER_K]
                cand4 = cand.rearrange("p h (a b) -> p h a b", b=PEER_K)
                step(v.tensor_tensor(cand4, r4[:, :, 0, :].unsqueeze(3).to_broadcast(full),
                                     r4[:, :, 1, :].unsqueeze(2).to_broadcast(full), ALU.add))
                top16(lambda n: cand[:, n, :], lambda n: sv[:, n, :], lambda n: si[:, n, :], PEER_H)
                first = sv[:, :, 0:1].to_broadcast([P, PEER_H, PEER_K])
                gt = gate[:, t, :].rearrange("p (h k) -> p h k", k=PEER_K)
                step(v.tensor_tensor(gt, sv[:, :, :], first, ALU.subtract))
                step(v.tensor_copy(sv[:, :, :], gt), "picked")
                step(v.tensor_scalar(sj[:, :, :], si[:, :, :], 4, None, ALU.logical_shift_right))
                step(v.tensor_copy(sif[:, 0, :], sj[:, :, :].rearrange("p h k -> p (h k)")))
                step(v.tensor_scalar(sj[:, :, :], si[:, :, :], 15, None, ALU.bitwise_and))
                step(v.tensor_copy(sif[:, 1, :], sj[:, :, :].rearrange("p h k -> p (h k)")))
                io = iota16[:, :].unsqueeze(1).unsqueeze(1).to_broadcast(full)
                for s in range(2):
                    at_s = sif[:, s, :].rearrange("p (h k) -> p h k", k=PEER_K).unsqueeze(3).to_broadcast(full)
                    step(v.tensor_tensor(pick[s], at_s, io, ALU.is_equal))
                    step(v.tensor_tensor(pick[s], pick[s], f4[:, :, s, :].unsqueeze(2).to_broadcast(full), ALU.mult))
                    step(v.tensor_reduce(sif[:, s, :].rearrange("p (h k) -> p h k", k=PEER_K), pick[s], AX, ALU.add))
                step(v.scalar_tensor_tensor(out=sif[:, 0, :], in0=sif[:, 0, :], scalar=float(NKEYS), in1=sif[:, 1, :],
                                            op0=ALU.mult, op1=ALU.add))
                v.wait_ge(S("expert_exp"), t + 1)
                step(v.tensor_reduce(rowsum[:, :], sv[:, :, :], AX, ALU.add))
                step(v.reciprocal(rowinv[:, :], rowsum[:, :]))
                step(v.tensor_tensor(gt, sv[:, :, :], rowinv[:, :].unsqueeze(2).to_broadcast([P, PEER_H, PEER_K]),
                                     ALU.mult))
                step(v.tensor_copy(expert[:, t, :], sif[:, 0, :]), "routed")

            def dot(t, j):
                for sub in range(2):
                    n = (j * 2) + (t * ROUNDS + sub)
                    known = isinstance(n, int)
                    for s in range(RING):
                        v.wait_ge(S(f"u_rows{s}"), n * 16 + 16)
                        v.tensor_tensor_reduce(ubuf[:, s, :], ubuf[:, s, :], h2[:, t, :], 1.0, 0.0, ALU.mult, ALU.add,
                                               dots[:, sub, s:s + 1]).then_inc(S("dot_done"), 1)
                    v.wait_ge(S("gelu_done"), n + 1)
                    if not (known and n < 2):
                        v.wait_ge(S("diag_done"), n * RING - RING)
                    v.tensor_tensor(wexp[:, sub, :], gelu[:, sub, :],
                                    gate[:, t, bass.ds(j * 2 * RING + sub * RING, RING)], ALU.mult).then_inc(
                        S("wexp_ready"), 1)

            route(0)
            for t in range(TILES):
                if t == 0:
                    dot(0, 0)
                with v.Fori(1 if t == 0 else 0, MIDDLE) as j:
                    dot(t, j)
                if t + 1 < TILES:
                    route(t + 1)
                with v.Fori(MIDDLE, ROUNDS // 2) as j:
                    dot(t, j)
                bank = trans if t % 2 else accum
                v.wait_ge(S("v_added"), (t + 1) * SLOTS)
                for m in range(2):
                    part = x1[:, t, m * 512:m * 512 + 512]
                    signal(v.tensor_tensor(part, bank[m][:, :], part, ALU.add), "y_ready" if m else "dve_step")


NAMES = ["x_prompt", "x_sample", "cache_a_k", "cache_a_v", "cache_a_ik", "cache_b_k", "cache_b_v", "g_attn", "w_in",
         "g_qa", "g_ka", "g_ik", "g_qb", "g_kb", "rel_bias", "w_br_a", "w_br_b", "w_out", "g_ffn", "w_pq",
         "peer_c1", "peer_c2", "peer_u", "peer_v"]
MATRICES = ("w_in", "w_br_a", "w_br_b", "w_out", "w_pq")
OUTS = [("y_prompt", (1, 256, D)), ("y_sample", (STREAMS, NEW, D)),
        ("a_k_prompt", (1, 1, 256, HEADS, HD)), ("a_v_prompt", (1, 1, 256, HEADS, HD)),
        ("a_ik_prompt", (1, 1, 256, ID)), ("b_k_prompt", (1, 1, 256, HEADS, HD)),
        ("b_v_prompt", (1, 1, 256, HEADS, HD)),
        ("a_k_sample", (1, STREAMS, NEW, HEADS, HD)), ("a_v_sample", (1, STREAMS, NEW, HEADS, HD)),
        ("a_ik_sample", (1, STREAMS, NEW, ID)), ("b_k_sample", (1, STREAMS, NEW, HEADS, HD)),
        ("b_v_sample", (1, STREAMS, NEW, HEADS, HD))]


def rope_table(half):
    inverse = np.power(np.float32(10000.0), -np.arange(half, dtype=np.float32) / np.float32(half))
    row = np.arange(P)
    positions = np.stack([row, row + P, PAST + row % NEW], axis=1).astype(np.float32)
    angle = (positions[:, :, None] * inverse[None, None, :].astype(np.float32)).astype(np.float32)
    return np.ascontiguousarray(np.stack([np.cos(angle), np.sin(angle)], axis=1).astype(np.float32))


def kernel(**inputs):
    import concourse.bacc as bacc
    from concourse.bass_utils import run_bass_kernel_spmd

    nc = bacc.Bacc("TRN2", target_bir_lowering=False, num_devices=1)
    arrays, ins, outs = {}, {}, {}
    given = {n: np.ascontiguousarray(inputs[n]) for n in NAMES}
    given["rope_head"] = rope_table(HD // 2)
    given["rope_index"] = rope_table(ID // 2)
    for name, a in given.items():
        arrays[f"in_{name}"] = a
        ap = nc.dram_tensor(f"in_{name}", a.shape, mybir.dt.from_np(a.dtype), kind="ExternalInput").ap()
        ins[name] = ap[0] if name in MATRICES else ap
    for name, shape in OUTS:
        outs[name] = nc.dram_tensor(f"out_{name}", shape, F32, kind="ExternalOutput").ap()
    build(nc, ins, outs)
    r = run_bass_kernel_spmd(nc, [arrays], core_ids=[0])
    return tuple(r.results[0][f"out_{name}"] for name, _ in OUTS)
```

```python
from contextlib import ExitStack

import numpy as np

import concourse.bass as bass
from concourse import mybir

F32 = mybir.dt.float32
U32 = mybir.dt.uint32
ALU = mybir.AluOpType
ACT = mybir.ActivationFunctionType
AX = mybir.AxisListType.X

P = 128
D = 1024
DC = D // P
TILES = 3
SAMPLE = 2
NTOK = TILES * P
STREAMS, NEW, PAST = 8, 16, 128
HEADS, HD = 8, 64
PAIRS = HEADS // 2
IH, ID = 8, 32
CHUNK = 64
REL = 128
PEER_H, PEER_K, NKEYS, DQ = 8, 16, 128, 256
SLOTS = PEER_H * PEER_K
EPS = 1e-6
NEG = -1e30
TAKEN = -3e38
PAD = -2e30
BQ_COL = 1832
GATE_COL = 3368
GROUPS = [("aq", 0, 512), ("ak", 512, 512), ("ix", 1536, 296), ("av", 1024, 512),
          ("bq", BQ_COL, 512), ("bk", BQ_COL + 512, 512), ("bv", BQ_COL + 1024, 512)]
GROUPS += [(f"gate{n}", GATE_COL + 512 * n, 512) for n in range(4)]
NG = len(GROUPS)
SEEN = [128, 256, 256]
SELECT = [64, 64, 36]
HALF = 4
VRING = 2 * HALF
HALVES = SLOTS // HALF
QH, QG, QS = 2, 4, 32
LAID = 2 * HALVES + 8
EXT = 384


class Group:

    def __init__(self, name, tiles, qkv, hT, qk, tmp, merged, merge_tmp, gates, oT, h2T, pqT, scores, trans, accum, iqT,
                 ix, ikrep, loads, w0):
        self.name, self.tiles, self.n, self.w0 = name, tiles, len(tiles), w0
        self.qkv, self.hT, self.qk, self.tmp, self.merged, self.merge_tmp = qkv, hT, qk, tmp, merged, merge_tmp
        self.gates, self.oT, self.pqT, self.scores, self.trans, self.accum = gates, oT, pqT, scores, trans, accum
        self.iqT, self.ix, self.ikrep, self.h2T, self.loads = iqT, ix, ikrep, h2T, loads


PROJ = [0, 1, 2, 4, 5, 6, 8]
GATES = [43, 45, 46, 48]
NORM = [p + 2 for p in PROJ]
AT = dict(heads_a=15, index=16, select=19, score_a=[20, 21, 23, 24], soft_a=25, values_a=[28, 29, 30, 31],
          heads_b=25, score_b=[32, 33, 34, 35], soft_b=36, values_b=[39, 40, 41, 42], branch=49, merge=51,
          out=[52, 53], scale=54, h2=56)
QUERY = dict(prompt=[-3, -3, -1, 0], sample=[57, 58, 60, 62])
ROUTE = [[-3, 0, 2, 4], [6, 8, 10, 12], [58, 60, 62, 64]]
GATES_INDEX = [1, 1]
GATES_HEADS = [2, 2, 1, 1]


def build(nc, i, o):
    with ExitStack() as ctx:
        def sb(name, shape, dt=F32):
            return ctx.enter_context(nc.sbuf_tensor(name, shape, dt))

        def psum(name, shape):
            return ctx.enter_context(nc.psum_tensor(name, shape, F32))

        sems, counts = {}, {}

        def S(name):
            if name not in sems:
                sems[name] = ctx.enter_context(nc.semaphore(name))
                counts[name] = 0
            return sems[name]

        def signal(ins, name):
            ins.then_inc(S(name), 1)
            counts[name] += 1

        def chain(eng, ins, name):
            signal(ins, name)
            eng.wait_ge(sems[name], counts[name])

        ident = sb("ident", [P, P])
        ropet = sb("ropet", [P, 2, TILES, HD // 2])
        ropei = sb("ropei", [P, 2, TILES, ID // 2])
        gain = sb("gain", [P, D])
        hgain = sb("hgain", [P, 4, HD])
        igain = sb("igain", [P, ID])
        iota16 = sb("iota16", [P, 16])
        own = sb("own", [P, P])
        rows_ring = sb("rows_ring", [P, (HALF + VRING) * D])
        shared = sb("shared", [P, 8448])
        ring = sb("ring", [P, 2, 4096])
        x1 = sb("x1", [P, TILES, D])
        h2 = sb("h2", [P, TILES, D])
        qkv1 = sb("qkv1", [P, 6 * 512])
        hT1 = sb("hT1", [P, DC, P])
        qk1 = sb("qk1", [P, 2 * PAIRS * P])
        iqTs = sb("iqTs", [P, 512])
        ixs = sb("ixs", [P, 2, 296])
        prob = sb("prob", [P, HEADS * 256])
        probT = sb("probT", [P, 2, 512])
        bias = sb("bias", [P, 2, HEADS, P])
        score = sb("score", [P, 2, 264])
        mask = sb("mask", [P, 2, 256])
        ikT = sb("ikT", [P, 256])
        diag = sb("diag", [P, VRING, P])
        cT = sb("cT", [P, 2, P])
        rtop = sb("rtop", [P, QG, 16])
        rtopi = sb("rtopi", [P, QG, 16], U32)
        rtopf = sb("rtopf", [P, QG, 16])
        sv = sb("sv", [P, QH, PEER_K])
        si = sb("si", [P, QH, PEER_K], U32)
        sj = sb("sj", [P, QH, PEER_K], U32)
        sif = sb("sif", [P, 2, QS])
        expert = sb("expert", [P, TILES, SLOTS], U32)
        gate = sb("gate", [P, TILES, SLOTS])
        staged = sb("staged", [P, 2, HALF], U32)
        dots = sb("dots", [P, 2, HALF])
        gelu = sb("gelu", [P, 2, HALF])
        wexp = sb("wexp", [P, 2, HALF])
        ssx = sb("ssx", [P, 2, TILES])
        rsx = sb("rsx", [P, 2, TILES])
        ssh = sb("ssh", [P, 5, 16])
        rsh = sb("rsh", [P, 5, 16])
        mhalf = sb("mhalf", [P, 16])
        mx8 = sb("mx8", [P, 8])
        rowmax = sb("rowmax", [P, HEADS])
        rowsum = sb("rowsum", [P, HEADS])
        rowinv = sb("rowinv", [P, HEADS])
        esum = sb("esum", [P, QH])

        AQ, BQ, AK, AV, BK, BV = range(6)
        where = {"aq": AQ, "bq": BQ, "ak": AK, "av": AV, "bk": BK, "bv": BV}
        qkv0 = rows_ring[:, 0:6144]
        sc = [shared[:, 2048 + 2048 * n:4096 + 2048 * n].rearrange("p (g k) -> p g k", g=16) for n in range(2)]
        cand = shared[:, 6144:6656].rearrange("p (h k) -> p h k", h=QH)
        pick = [shared[:, 6656 + 512 * n:7168 + 512 * n].rearrange("p (h k j) -> p h k j", h=QH, k=PEER_K)
                for n in range(2)]
        ext = shared[:, 2048:2048 + HEADS * EXT].rearrange("p (h k) -> p h k", h=HEADS)
        rbias = shared[:, 5120:5120 + HEADS * 257].rearrange("p (h k) -> p h k", h=HEADS)
        raw = shared[:, 0:2048].rearrange("p (s b c) -> p s b c", s=2, b=STREAMS)
        kcT = shared[:, 2048:4096].rearrange("p (s b c) -> p s b c", s=2, b=STREAMS)
        vc = shared[:, 4096:6144].rearrange("p (s b c) -> p s b c", s=2, b=STREAMS)
        cikT = shared[:, 4096:5120].rearrange("p (b c) -> p b c", b=STREAMS)
        QM = 9 * P
        qm = shared[:, 6144:6144 + 2 * QM].rearrange("p (s c) -> p s c", s=2)
        cik = prob[:, 0:256].rearrange("p (b d) -> p b d", b=STREAMS)
        cikrep = prob[:, 256:1280].rearrange("p (b r d) -> p b r d", b=STREAMS, r=4)
        probs = prob[:, :].rearrange("p (h k) -> p h k", h=HEADS)
        ubuf = rows_ring[:, 0:HALF * D].rearrange("p (s c) -> p s c", s=HALF)
        vbuf = rows_ring[:, HALF * D:].rearrange("p (s c) -> p s c", s=VRING)

        wide = psum("wide", [P, 4, 512])
        widef = wide[:, :, :].rearrange("p b c -> p (b c)")
        logits = widef.rearrange("p (h k) -> p h k", h=HEADS)
        trans = [psum("transA", [P, 512]), psum("transB", [P, 512])]
        accum = [psum("accumA", [P, 512]), psum("accumB", [P, 512])]
        ysum = [trans[0], accum[0]]

        def group(name, tiles, qkv, hT, qk, tmp, merge_tmp, gates, h2T, scores, trans, accum, loads, first_load):
            n = len(tiles)
            return Group(
                name, tiles, qkv=qkv.rearrange("p (a t c) -> p a t c", a=6, t=n),
                hT=hT, qk=qk.rearrange("p (a c n) -> p a c n", a=2, c=PAIRS), tmp=tmp,
                merged=qk.rearrange("p (t c) -> p t c", t=n), merge_tmp=merge_tmp, gates=gates,
                oT=[qkv[:, k * n * 512:(k + 1) * n * 512].rearrange("p (c n) -> p c n", c=PAIRS) for k in range(2)],
                h2T=h2T, pqT=prob[:, 0:QG * n * P].rearrange("p (g n) -> p g n", g=QG), scores=scores, trans=trans, accum=accum,
                iqT=iqTs[:, 0:2 * n * P].rearrange("p (c n) -> p c n", c=2), ix=ixs[:, 0:n, :],
                ikrep=prob[:, 1280:1280 + n * P].rearrange("p (t r d) -> p t r d", t=n, r=4), loads=loads,
                w0=first_load)

        LOADS = [name for name, _, _ in GROUPS] + ["br_a", "br_b", "out1", "pq0", "pq1", "pq2", "pq3"]
        G0 = group("prompt", [0, 1], qkv0, rows_ring[:, 6144:8192].rearrange("p (c n) -> p c n", c=DC),
                   shared[:, 0:2048], shared[:, 0:2048], prob[:, 0:D], [shared[:, 2048:4096], shared[:, 4096:6144]],
                   shared[:, 0:2048].rearrange("p (c n) -> p c n", c=DC), sc, trans, accum, LOADS, 0)
        G1 = group("sample", [SAMPLE], qkv1[:, :], hT1[:, :, :], qk1[:, :], qk1[:, :], shared[:, 0:D],
                   [prob[:, :]], hT1[:, :, :], [sc[0]], trans[1:], accum[1:], LOADS[:-5] + ["out0"] + LOADS[-5:],
                   len(LOADS))
        qbanks = [accum[1], trans[1]]
        out0_weights = rows_ring[:, 8192:12288]

        bias_rows = nc.dram_tensor("bias_rows", [P, HEADS * EXT], F32).ap()

        def weights_dram(name):
            for group_name, c0, c in GROUPS:
                if name == group_name:
                    return i["w_in"][:, c0:c0 + c].rearrange("(k p) c -> p k c", p=P)
            if name[:2] == "br":
                return i["w_" + name].rearrange("(k p) c -> p k c", p=P)
            c0 = 512 * int(name[-1])
            return i["w_out" if name[:3] == "out" else "w_pq"][:, c0:c0 + 512].rearrange("(k p) c -> p k c", p=P)

        def load_of(G, name):
            return G.w0 + G.loads.index(name)

        def slot_weights(G, name):
            if name not in G.loads:
                return out0_weights.rearrange("p (k c) -> p k c", k=DC)
            n = load_of(G, name)
            chunks, c = weights_dram(name).shape[1:]
            return ring[:, n % 2, 0:chunks * c].rearrange("p (k c) -> p k c", k=chunks)

        def weights_wait(eng, G, name):
            if name not in G.loads:
                eng.wait_ge(S("out0_in"), 16)
                return
            n = load_of(G, name)
            eng.wait_ge(S(f"weights_in{n % 2}"), 16 * (n // 2 + 1))

        def at_index(h):
            return (h % 4) * 2 + h // 4

        def cols(t):
            return slice(t * P, t * P + P)

        def to_all_rows(row):
            return bass.AP(tensor=row.tensor, offset=row.offset, ap=[[0, P], [1, row.shape[-1]]])

        for G in (G0, G1):
            every = range(G.n)
            G.batches = [("h", t, half) for t in every for half in range(2)]
            if G is G1:
                G.batches += [("cik", half) for half in range(2)]
            G.batches += [("index", t) for t in every]
            if G is G0:
                G.batches += [("centroids",)]
            for br in range(2):
                G.batches += [(name, br, t) for name in "qk" for t in every]
                for t in every:
                    if G is G1:
                        G.batches += [("cache", br, hp, half) for hp in range(PAIRS) for half in range(2)]
                    G.batches += [("prob", br, t, hp) for hp in range(PAIRS)]
            G.batches += [("merged", t, half) for t in every for half in range(2)]
            G.batches += [("h2", t, half) for t in every for half in range(2)]
        bs = [b for b in G1.batches if b[0] in "qk" and b[1] == 1]
        rest = [b for b in G1.batches if b not in bs]
        k = rest.index(("prob", 0, 0, 0))
        G1.batches = rest[:k] + bs + rest[k:]

        def batch(G, *key):
            return G.batches.index(key)

        def to(G, name):
            return S(f"{G.name}_{name}")

        block = ctx.enter_context(nc.Block())

        def laid(steps):
            k = next(steps)
            m = yield
            while True:
                while k <= m:
                    k = next(steps, 1 << 30)
                m = yield

        def start_laid(between):
            for b in between:
                next(b)
            for m in range(-3, 0):
                for b in between:
                    b.send(m)

        def gate_banks():
            units = [n % 2 for n in range(sum(GATES_INDEX))]
            for r, n in enumerate(GATES_HEADS):
                units += [(r + 1) % 2] * n
            return [(7 * G0.n + n, accum[bank]) for n, bank in enumerate(units)]

        @block.sync
        def _(sp):
            for t in range(TILES):
                src = i["x_prompt"][0, cols(t), :] if t < SAMPLE else i["x_sample"].rearrange("b s c -> (b s) c")
                sp.dma_start(x1[:, t, :], src).then_inc(S(f"x_in{t}"), 16)
                if t == 0:
                    sp.dma_start(gain[:, :], to_all_rows(i["g_attn"])).then_inc(S("gain_in"), 16)
            for n, name in enumerate(G0.loads[:2]):
                sp.dma_start(slot_weights(G0, name), weights_dram(name)).then_inc(S(f"weights_in{n}"), 16)
            sp.dma_start(ropet[:, :, :, :], i["rope_head"]).then_inc(S("rope_in"), 16)
            sp.dma_start(ropei[:, :, :, :], i["rope_index"]).then_inc(S("rope_in"), 16)
            for n, g in enumerate(("g_qa", "g_ka", "g_qb", "g_kb")):
                sp.dma_start(hgain[:, n, :], to_all_rows(i[g])).then_inc(S("rope_in"), 16)
            sp.dma_start(igain[:, :], to_all_rows(i["g_ik"])).then_inc(S("rope_in"), 16)
            sp.dma_start(rbias, bass.AP(tensor=i["rel_bias"].tensor, offset=i["rel_bias"].offset,
                                        ap=[[0, P], [2 * REL + 1, HEADS], [1, 2 * REL + 1]])).then_inc(S("rbias_in"), 16)
            sp.wait_ge(S("ext_built"), 1)
            sp.dma_start(bias_rows, ext.rearrange("p h k -> p (h k)")).then_inc(S("ext_stored"), 16)
            sp.wait_ge(S("ext_stored"), 16)

            def load_bias(kind, rows, keys, first, counted):
                for odd in range(2):
                    src = bass.AP(tensor=bias_rows.tensor, offset=bias_rows.offset + odd * EXT + first,
                                  ap=[[HEADS * EXT - 1, rows.stop - rows.start], [2 * EXT, 4],
                                      [1, keys.stop - keys.start]])
                    sp.dma_start(bias[rows, kind, 4 * odd:4 * odd + 4, keys], src).then_inc(S(counted), 16)

            sp.wait_ge(to(G0, "transposed"), 2)
            for n in range(2):
                sp.dma_start(h2[:, 0, n * P:n * P + P], i[f"peer_c{n + 1}"][0]).then_inc(S("centroids_in"), 16)
            every = slice(0, P)
            load_bias(0, every, every, 255, "bias_in")
            load_bias(1, every, every, 127, "bias_in")

            def weights(G, name, signalled, value):
                sp.wait_ge(S(signalled), value)
                sp.dma_start(slot_weights(G, name), weights_dram(name)).then_inc(
                    S(f"weights_in{load_of(G, name) % 2}"), 16)

            def cache_load(what, n):
                br, hp = divmod(n, PAIRS)
                src = i[f"cache_{'ab'[br]}_{what}"][0].rearrange("b k h d -> k b (h d)")[:, :, hp * P:hp * P + P]
                if n >= 2:
                    b2, hp2 = divmod(n - 2, PAIRS)
                    if what == "k":
                        sp.wait_ge(to(G1, "transposed"), batch(G1, "cache", b2, hp2, 1) + 1)
                    else:
                        sp.wait_ge(to(G1, "pv_done"), b2 * PAIRS + hp2 + 1)
                dst = raw if what == "k" else vc
                sp.dma_start(dst[:, n % 2], src).then_inc(S(f"{what}cache_in{n % 2}"), 16)

            for G in (G0, G1):
                names = [name for name, _, _ in GROUPS]
                for n in range(2 if G is G0 else 0, 7 if G is G1 else NG):
                    if n < 2:
                        weights(G, names[n], f"{G0.name}_query_done", 4 * (n + 3))
                    else:
                        weights(G, names[n], f"{G.name}_group_done", G.n * (n - 1))
                if G is G1:
                    sp.wait_ge(S("routed"), 8)
                    sp.dma_start(cik, i["cache_a_ik"][0].rearrange("b k d -> k b d")).then_inc(S("cik_in"), 16)
                    sp.wait_ge(S("bias_cleared"), 1)
                    for b in range(STREAMS):
                        rows = slice(b * NEW, b * NEW + NEW)
                        load_bias(0, rows, rows, 255, "sample_bias_in")
                        load_bias(1, rows, every, 127, "sample_bias_in")
                    cache_load("k", 0)
                    cache_load("k", 1)
                    sp.wait_ge(to(G1, "index_done"), 1)
                    cache_load("v", 0)
                    cache_load("v", 1)
                    for what, first, last in (("k", 2, 6), ("v", 2, 6), ("k", 6, 8), ("v", 6, 8)):
                        for n in range(first, last):
                            cache_load(what, n)
                    for n in range(7, NG):
                        weights(G, names[n], f"{G.name}_group_done", G.n * (n - 1))
                else:
                    sp.dma_start(out0_weights.rearrange("p (k c) -> p k c", k=DC), weights_dram("out0")).then_inc(
                        S("out0_in"), 16)
                    sp.wait_ge(to(G0, "h_ready"), 2)
                    sp.wait_ge(to(G1, "h_ready"), 1)
                    sp.dma_start(gain[:, :], to_all_rows(i["g_ffn"])).then_inc(S("gain_in"), 16)
                weights(G, "br_a", f"{G.name}_group_done", G.n * (NG - 1))
                weights(G, "br_b", f"{G.name}_group_done", G.n * NG)
                before = [("branches_done", G.n), ("branches_done", 2 * G.n)]
                before += [("out_done", G.n * (2 - k)) for k in (1, 0)][1 if G is G0 else 0:]
                before += [("query_done", 4), ("query_done", 8)]
                for name, (signalled, value) in zip(G.loads[NG + 2:], before):
                    weights(G, name, f"{G.name}_{signalled}", value)
            for t in range(TILES):
                sp.wait_ge(S("y_ready"), t + 1)
                dst = o["y_prompt"][0, cols(t), :] if t < SAMPLE else o["y_sample"].rearrange("b s c -> (b s) c")
                sp.dma_start(dst, x1[:, t, :]).then_inc(S("y_stored"), 16)
            sp.wait_ge(S("y_stored"), 16 * TILES)

        @block.gpsimd
        def _(pool):
            pool.memset(mhalf[:, :], -0.5).then_inc(S("pool_set"), 1)
            pool.memset(ident[:, :], 0.0).then_inc(S("pool_set"), 1)
            pool.wait_ge(S("pool_set"), 2)
            pool.affine_select(out=ident[:, :], in_=ident[:, :], compare_op=ALU.not_equal, fill=1.0, base=0,
                               pattern=[[-1, P]], channel_multiplier=1).then_inc(S("ident_set"), 1)
            pool.iota(iota16[:, :], pattern=[[1, 16]], base=0, channel_multiplier=0,
                      allow_small_or_imprecise_dtypes=True).then_inc(S("iota_set"), 1)
            own3 = own[:, :].rearrange("p (b j) -> p b j", j=NEW)
            pool.memset(own[:, :], 0.0).then_inc(S("pool_set"), 1)
            pool.wait_ge(S("pool_set"), 3)
            pool.affine_select(out=own3, in_=own3, compare_op=ALU.is_ge, fill=NEG, base=0,
                               pattern=[[-NEW, STREAMS], [0, NEW]], channel_multiplier=1).then_inc(S("pool_set"), 1)
            pool.wait_ge(S("pool_set"), 4)
            pool.affine_select(out=own3, in_=own3, compare_op=ALU.is_ge, fill=NEG, base=NEW - 1,
                               pattern=[[NEW, STREAMS], [0, NEW]], channel_multiplier=-1).then_inc(S("own_set"), 1)

            def inverse_rms(src, dst, n, width, signalled):
                chain(pool, pool.tensor_scalar(src, src, 1.0 / width, EPS, ALU.mult, ALU.add), "pool_step")
                signal(pool.tensor_tensor(dst, src, mhalf[:, 0:n], ALU.pow), signalled)

            for t in range(TILES):
                pool.wait_ge(S("squares_summed"), t + 1)
                inverse_rms(ssx[:, 0, t:t + 1], rsx[:, 0, t:t + 1], 1, D, "row_scale")

            def steps(G):
                def store(src, name, width):
                    dst = o[f"{name}_{G.name}"]
                    if G is G1:
                        dst = dst[0].rearrange("b t h d -> (b t) (h d)" if width > ID else "b t d -> (b t) d")
                        pool.dma_start(dst, src[:, 0, 0:width]).then_inc(S("state_stored"), 16)
                        return
                    dst = dst[0, 0].rearrange("t h d -> t (h d)") if width > ID else dst[0, 0]
                    pool.dma_start(dst.rearrange("(t p) c -> p t c", p=P), src[:, :, 0:width]).then_inc(
                        S("state_stored"), 16)

                head = ready = 0
                for g, (name, _, _) in enumerate(GROUPS[:7]):
                    yield NORM[g] + 1
                    if name == "ix" or name in ("aq", "ak", "bq", "bk"):
                        m, n, w = (4, G.n, ID) if name == "ix" else (("aq", "ak", "bq", "bk").index(name), 8 * G.n, HD)
                        head += 1
                        pool.wait_ge(to(G, "heads_squared"), head)
                        inverse_rms(ssh[:, m, 0:n], rsh[:, m, 0:n], n, w, f"{G.name}_head_scale")
                    yield NORM[g] + 3
                    if name == "ix":
                        pool.wait_ge(to(G, "ik_ready"), 1)
                        store(G.ix[:, :, 256:288], "a_ik", ID)
                    elif name in ("aq", "ak", "bq", "bk"):
                        ready += 1
                        if name[1] == "k":
                            pool.wait_ge(to(G, "heads_ready"), ready)
                            store(G.qkv[:, where[name]], f"{name[0]}_k", 512)
                    else:
                        pool.wait_ge(to(G, "group_copied"), G.n * (g + 1))
                        store(G.qkv[:, where[name]], f"{name[0]}_v", 512)
                yield AT["scale"] + 1
                for t in G.tiles:
                    pool.wait_ge(S("squares_summed"), TILES + t + 1)
                    inverse_rms(ssx[:, 1, t:t + 1], rsx[:, 1, t:t + 1], 1, D, "row_scale")

            for _ in steps(G0):
                pass

            u_rows, v_rows = i["peer_u"][0], i["peer_v"][0]

            pool.wait_ge(S("state_stored"), 16 * 5)

            def gather(t, j, sub):
                m = (j * 2) + (t * HALVES + sub)
                known = isinstance(m, int)
                if not (known and m < 2):
                    for s in range(HALF):
                        pool.wait_ge(S(f"v_rows{sub * HALF + s}"), j * 16 + (t * HALVES // 2) * 16)
                    pool.wait_ge(S("dot_done"), m * HALF - HALF)
                pool.tensor_copy(staged[:, sub, :], expert[:, t, bass.ds(j * VRING + sub * HALF, HALF)]).then_inc(
                    S(f"experts_staged{sub}"), 1)
                pool.wait_ge(S(f"experts_staged{sub}"), j + (t * HALVES // 2 + 1))
                for s in range(HALF):
                    index = bass.IndirectOffsetOnAxis(ap=staged[:, sub, s:s + 1], axis=0)
                    if not (known and m < 1):
                        pool.wait_ge(S("dot_done"), m * HALF + (s + 1 - HALF))
                        pool.sem_inc(S("u_slot_free"), 1)
                    pool.indirect_dma_start(ubuf[:, s, :], None, u_rows, index).then_inc(S(f"u_rows{s}"), 16)
                    if not (known and m < 2):
                        pool.wait_ge(S("v_added"), m * HALF + (s + 1 - VRING))
                        pool.sem_inc(S("v_slot_free"), 1)
                    q = sub * HALF + s
                    pool.indirect_dma_start(vbuf[:, q, :], None, v_rows, index).then_inc(S(f"v_rows{q}"), 16)

            between = [laid(steps(G1))]
            start_laid(between)
            for m in range(LAID):
                t = m // HALVES
                if m % (HALVES // 4) == 0:
                    pool.wait_ge(S("routed"), m // (HALVES // 4) + 1)
                gather(t, m % HALVES // 2, m % 2)
                for b in between:
                    b.send(m)
            pool.wait_ge(S("routed"), TILES * 4)
            with pool.Fori(LAID // 2 - HALVES, HALVES // 2) as j:
                for sub in range(2):
                    gather(SAMPLE, j, sub)
            pool.wait_ge(S("state_stored"), 16 * 10)

        @block.scalar
        def _(act):
            for t in range(TILES):
                act.wait_ge(S(f"x_in{t}"), 16)
                chain(act, act.activation(prob[:, 0:D], x1[:, t, :], ACT.Square, accum_out=ssx[:, 0, t:t + 1]),
                      "squares_summed")

            def copy_out(G, key, pieces, *waits):
                n = batch(G, *key)
                act.wait_ge(to(G, "transposed"), n + 1)
                for name, value in waits:
                    act.wait_ge(S(name), value)
                for m, (dst, c0, c1) in enumerate(pieces):
                    src = G.trans[n % len(G.trans)][:, c0:c1]
                    if len(dst.shape) == 3:
                        src = src.rearrange("p (c n) -> p c n", c=dst.shape[1])
                    ins = act.activation(dst, src, ACT.Copy)
                    if m == len(pieces) - 1:
                        ins.then_inc(to(G, "transposes_copied"), 1)

            def copy_rows(G, name, t, half):
                dst = G.h2T if name == "h2" else G.hT
                copy_out(G, (name, t, half), [(dst[:, 4 * half:4 * half + 4, cols(t)], 0, 512)])

            for G in (G0, G1):
                for t in range(G.n):
                    for half in range(2):
                        copy_rows(G, "h", t, half)

            def steps(G):
                every = range(G.n)

                def groups(gs, lay):
                    for g, at in zip(gs, lay):
                        yield at
                        for t in every:
                            u = g * G.n + t
                            unit(u, G.accum[u % len(G.accum)])

                def unit(u, bank):
                    g, t = divmod(u, G.n)
                    name, _, c = GROUPS[g]
                    act.wait_ge(to(G, "group_done"), u + 1)
                    src = bank[:, 0:c]
                    if name.startswith("gate"):
                        if G is G0:
                            act.wait_ge(S("ext_stored"), 16)
                        m = g - 7
                        act.activation(G.gates[t][:, m * 512:m * 512 + 512], src, ACT.Sigmoid).then_inc(
                            to(G, "group_copied"), 1)
                    else:
                        dst = G.ix[:, t, :] if name == "ix" else G.qkv[:, where[name], t, :]
                        act.activation(dst, src, ACT.Copy).then_inc(to(G, "group_copied"), 1)

                def heads_out(br):
                    for m, name in enumerate("qk"):
                        for t in every:
                            copy_out(G, (name, br, t), [(G.qk[:, m, :, cols(t)], 0, 512)])

                units = iter(gate_banks())

                def gate_units(n):
                    for _ in range(n):
                        unit(*next(units))

                yield from groups(range(7), [p + 1 for p in PROJ])
                yield AT["heads_a"]
                if G is G1:
                    for half in range(2):
                        copy_out(G, ("cik", half), [(cikT[:, 4 * half:4 * half + 4, :], 0, 512)])
                for t in every:
                    copy_out(G, ("index", t), [(G.iqT[:, :, cols(t)], 0, 256), (ikT[:, cols(t)], 256, 384)])
                if G is G0:
                    copy_out(G, ("centroids",), [(cT[:, :, :], 0, 256)])
                heads_out(0)
                yield AT["index"] + 1
                for t in every:
                    seen = SEEN[G.tiles[t]]
                    act.wait_ge(to(G, "index_done"), t + 1)
                    if t:
                        act.wait_ge(to(G, "scored"), t)
                    act.activation(probs[:, :, 0:seen], logits[:, :, 0:seen], ACT.Relu).then_inc(to(G, "relu_done"), 1)
                    if G is G0:
                        gate_units(GATES_INDEX[t])
                for br in range(2):
                    ab = "ab"[br]
                    if br and G is G0:
                        heads_out(1)
                    for t in every:
                        r = br * G.n + t
                        seen = SEEN[G.tiles[t]]
                        nk = seen // P
                        if G is G1:
                            for hp in range(PAIRS):
                                yield AT["score_" + ab][hp]
                                n = br * PAIRS + hp
                                for half in range(2):
                                    waits = [(f"{G.name}_pair_scored", n - 1)] if n >= 2 else []
                                    copy_out(G, ("cache", br, hp, half),
                                             [(kcT[:, n % 2, 4 * half:4 * half + 4, :], 0, 512)], *waits)
                        if G is G0:
                            gate_units(GATES_HEADS[r] - 1)
                        yield AT["soft_" + ab] + 1
                        act.wait_ge(to(G, "rowmax_ready"), r + 1)
                        for h in range(HEADS):
                            act.activation(probs[:, h, 0:seen], probs[:, h, 0:seen], ACT.Exp, bias=rowmax[:, h:h + 1],
                                           accum_out=rowsum[:, h:h + 1]).then_inc(to(G, "exp_done"), 1)
                        if G is G0:
                            gate_units(1)
                        elif not br:
                            heads_out(1)
                        for hp in range(PAIRS):
                            yield AT["values_" + ab][hp]
                            m = r * PAIRS + hp
                            waits = [(f"{G.name}_pv_done", m - 1)] if m >= 2 else []
                            copy_out(G, ("prob", br, t, hp), [(probT[:, hp % 2, 0:2 * nk * P], 0, 2 * nk * P)], *waits)
                        act.wait_ge(to(G, "pv_done"), (r + 1) * PAIRS)
                        act.activation(G.oT[br][:, :, cols(t)],
                                       G.accum[r % len(G.accum)][:, :].rearrange("p (c n) -> p c n", c=PAIRS),
                                       ACT.Copy).then_inc(to(G, "attended"), 1)
                if G is G1:
                    yield from groups(range(7, NG), [p + 1 for p in GATES])
                yield AT["merge"]
                for t in every:
                    for half in range(2):
                        copy_rows(G, "merged", t, half)
                yield AT["scale"]
                for t in every:
                    act.wait_ge(to(G, "x1_added"), G.n + t + 1)
                    tile = G.tiles[t]
                    chain(act, act.activation(prob[:, 0:D], x1[:, tile, :], ACT.Square, accum_out=ssx[:, 1, tile:tile + 1]),
                          "squares_summed")
                yield AT["h2"]
                for t in every:
                    for half in range(2):
                        copy_rows(G, "h2", t, half)
            def queries(G):
                for q in range(4):
                    yield QUERY[G.name][q]
                    for k in range(QG):
                        u = QG * q + k
                        act.wait_ge(to(G, "query_done"), u + 1)
                        if q:
                            act.wait_ge(to(G, "score_done"), q * G.n)
                        act.activation(G.pqT[:, k, :], qbanks[u % 2][:, 0:G.n * P], ACT.Copy).then_inc(
                            to(G, "query_copied"), 1)
                    for t in range(G.n):
                        r = q * G.n + t
                        act.wait_ge(to(G, "score_done"), r + 1)
                        act.activation(G.scores[t][:, QG * q:QG * q + QG, :],
                                       wide[:, r % 4, :].rearrange("p (g k) -> p g k", g=QG), ACT.Copy).then_inc(
                            to(G, "router_copied"), 1)

            def softmax_exps(t):
                for q in range(4):
                    yield ROUTE[t][q]
                    act.wait_ge(S("picked"), 4 * t + q + 1)
                    act.activation(sv[:, :, :], sv[:, :, :], ACT.Exp).then_inc(S("expert_exp"), 1)

            for _ in steps(G0):
                pass

            def weigh(t, j, sub):
                m = (j * 2) + (t * HALVES + sub)
                act.wait_ge(S("dot_done"), m * HALF + HALF)
                act.activation(gelu[:, sub, :], dots[:, sub, :], ACT.Gelu).then_inc(S("gelu_done"), 1)
                act.wait_ge(S("gelu_done"), m + 1)
                for s in range(HALF):
                    act.activation(wexp[:, sub, s:s + 1], gate[:, t, bass.ds(j * VRING + (sub * HALF + s), 1)],
                                   ACT.Copy, scale=gelu[:, sub, s:s + 1]).then_inc(S("wexp_ready"), 1)
                for s in range(HALF):
                    act.wait_ge(S("wexp_ready"), m * HALF + (s + 1))
                    if not (isinstance(m, int) and m < 2):
                        act.wait_ge(S("v_added"), m * HALF + (s + 1 - VRING))
                    act.activation(diag[:, sub * HALF + s, :], ident[:, :], ACT.Copy, scale=wexp[:, sub, s:s + 1]
                                   ).then_inc(S("diag_done"), 1)

            between = [laid(x) for x in (queries(G0), softmax_exps(0), softmax_exps(1), steps(G1), queries(G1),
                                         softmax_exps(SAMPLE))]
            start_laid(between)
            for m in range(LAID):
                weigh(m // HALVES, m % HALVES // 2, m % 2)
                for b in between:
                    b.send(m)
            with act.Fori(LAID // 2 - HALVES, HALVES // 2) as j:
                for sub in range(2):
                    weigh(SAMPLE, j, sub)

        @block.tensor
        def _(pe):
            pe.wait_ge(S("ident_set"), 1)

            def transposes(G, key, sources):
                n, banks = batch(G, *key), len(G.trans)
                if n >= banks:
                    pe.wait_ge(to(G, "transposes_copied"), n - banks + 1)
                elif G is G1:
                    pe.wait_ge(to(G0, "transposes_copied"), 4)
                for m, src in enumerate(sources):
                    ins = pe.transpose(G.trans[n % banks][:, m * P:m * P + P], src, ident[:, :])
                ins.then_inc(to(G, "transposed"), 1)

            def rows(G, name, src, t, half):
                transposes(G, (name, t, half), [src[:, c * P:c * P + P] for c in range(4 * half, 4 * half + 4)])

            for G in (G0, G1):
                for t in range(G.n):
                    pe.wait_ge(to(G, "h_ready"), t + 1)
                    for half in range(2):
                        rows(G, "h", h2[:, G.tiles[t], :], t, half)

            def steps(G):
                every = range(G.n)
                banks = len(G.accum)

                def unit(u, bank):
                    g, t = divmod(u, G.n)
                    name, _, c1 = GROUPS[g]
                    weights_wait(pe, G, name)
                    for c in range(DC):
                        ins = pe.matmul(bank[:, 0:c1], G.hT[:, c, cols(t)], slot_weights(G, name)[:, c, :],
                                        start=c == 0, stop=c == DC - 1)
                    ins.then_inc(to(G, "group_done"), 1)

                def projection(gs, lay):
                    for g, at in zip(gs, lay):
                        yield at
                        for t in every:
                            u = g * G.n + t
                            if G is G1 and g == 7:
                                pe.wait_ge(to(G, "attended"), 2)
                            elif G is G1 and u == 0:
                                pe.wait_ge(to(G0, "query_copied"), 16)
                            elif u >= banks:
                                pe.wait_ge(to(G, "group_copied"), u - banks + 1)
                            unit(u, G.accum[u % banks])

                units = iter(gate_banks())

                def gate_units(n, attended=0):
                    for _ in range(n):
                        u, bank = next(units)
                        pe.wait_ge(to(G, "group_copied"), u)
                        if attended:
                            pe.wait_ge(to(G, "attended"), attended)
                        unit(u, bank)

                pe.wait_ge(to(G, "transposes_copied"), 2 * G.n)
                yield from projection(range(7), PROJ)
                yield AT["heads_a"]
                pe.wait_ge(to(G, "index_ready"), 1)
                pe.wait_ge(to(G, "heads_ready"), 4)
                if G is G1:
                    for half in range(2):
                        transposes(G, ("cik", half), [cikrep[:, b].rearrange("p r d -> p (r d)")
                                                      for b in range(4 * half, 4 * half + 4)])
                for t in every:
                    transposes(G, ("index", t), [G.ix[:, t, 0:P], G.ix[:, t, P:2 * P],
                                                 G.ikrep[:, t].rearrange("p r d -> p (r d)")])
                if G is G0:
                    pe.wait_ge(S("centroids_in"), 32)
                    transposes(G, ("centroids",), [h2[:, 0, n * P:n * P + P] for n in range(2)])

                def heads_in(br):
                    for name, w in (("q", BQ if br else AQ), ("k", BK if br else AK)):
                        for t in every:
                            transposes(G, (name, br, t), [G.qkv[:, w, t, hp * P:hp * P + P] for hp in range(PAIRS)])

                heads_in(0)
                yield AT["index"]
                pe.wait_ge(to(G, "transposes_copied"), batch(G, "index", G.n - 1) + 1)
                if G is G1:
                    pe.wait_ge(to(G0, "router_copied"), 8)
                    pe.wait_ge(S("iqm_ready"), 1)
                for t in every:
                    seen = SEEN[G.tiles[t]]
                    if t:
                        pe.wait_ge(to(G, "relu_done"), t)
                    for h in range(IH):
                        if h == IH // 2:
                            yield AT["index"] + 1
                        r0 = ID * (h % 4)
                        part = slice(r0, r0 + ID)
                        c0 = at_index(h) * 256
                        q = G.iqT[part, h // 4, cols(t)]
                        if G is G0:
                            ins = pe.matmul(widef[:, c0:c0 + seen], q, ikT[part, 0:seen], start=True, stop=True,
                                            tile_position=(r0, 0))
                            continue
                        for b in range(STREAMS):
                            pe.matmul(widef[:, c0:c0 + P], qm[part, h // 4, b * P:b * P + P], cikT[part, b, :],
                                      start=b == 0, stop=b == STREAMS - 1, tile_position=(r0, 0))
                        ins = pe.matmul(widef[:, c0 + P:c0 + 2 * P], q, ikT[part, 0:P], start=True, stop=True,
                                        tile_position=(r0, 0))
                    ins.then_inc(to(G, "index_done"), 1)
                    if G is G0:
                        gate_units(GATES_INDEX[t])

                def score_heads(br, t):
                    r = br * G.n + t
                    seen = SEEN[G.tiles[t]]
                    if r == 0:
                        pe.wait_ge(to(G, "relu_done"), G.n)
                    else:
                        pe.wait_ge(to(G, "logits_read"), r)
                    if t == 0:
                        pe.wait_ge(to(G, "transposes_copied"), batch(G, "k", br, G.n - 1) + 1)
                    for hp in range(PAIRS):
                        n = br * PAIRS + hp
                        if G is G1:
                            if hp:
                                yield AT["score_" + "ab"[br]][hp]
                            pe.wait_ge(S(f"kcache_in{n % 2}"), 16 * (n // 2 + 1))
                            for half in range(2):
                                transposes(G, ("cache", br, hp, half), [raw[:, n % 2, b]
                                                                        for b in range(4 * half, 4 * half + 4)])
                            pe.wait_ge(to(G, "transposes_copied"), batch(G, "cache", br, hp, 1) + 1)
                            pe.wait_ge(S("qm_ready"), n + 1)
                        for odd in range(2):
                            part = slice(HD * odd, HD * odd + HD)
                            c0 = (odd * 4 + hp) * 256
                            if G is G0:
                                ins = pe.matmul(widef[:, c0:c0 + seen], G.qk[part, 0, hp, cols(t)],
                                                G.qk[part, 1, hp, 0:seen], start=True, stop=True)
                                continue
                            pe.matmul(widef[:, c0 + P:c0 + 2 * P], G.qk[part, 0, hp, :], G.qk[part, 1, hp, :],
                                      start=True, stop=True)
                            for b in range(STREAMS):
                                ins = pe.matmul(widef[:, c0:c0 + P], qm[part, n % 2, b * P:b * P + P],
                                                kcT[part, n % 2, b, :], start=b == 0, stop=b == STREAMS - 1)
                        if G is G1:
                            ins.then_inc(to(G, "pair_scored"), 1)
                    if G is G0:
                        ins.then_inc(to(G, "logits_done"), 1)

                def weigh_values(br, t):
                    r = br * G.n + t
                    nk = SEEN[G.tiles[t]] // P
                    v = BV if br else AV
                    pe.wait_ge(to(G, "probs_ready"), r + 1)
                    if r >= banks:
                        pe.wait_ge(to(G, "attended"), r - banks + 1)
                    if G is G0:
                        pe.wait_ge(to(G, "group_copied"), 7 * G.n + sum(GATES_INDEX) + sum(GATES_HEADS[:r]))
                    elif r == 0:
                        pe.wait_ge(to(G, "group_copied"), 7)
                    for hp in range(PAIRS):
                        if hp:
                            yield AT["values_" + "ab"[br]][hp]
                        transposes(G, ("prob", br, t, hp), [probs[:, odd * 4 + hp, k * P:k * P + P]
                                                            for odd in range(2) for k in range(nk)])
                        pe.wait_ge(to(G, "transposes_copied"), batch(G, "prob", br, t, hp) + 1)
                        n = br * PAIRS + hp
                        if G is G1:
                            pe.wait_ge(S(f"vcache_in{n % 2}"), 16 * (n // 2 + 1))
                        for odd in range(2):
                            out = G.accum[r % banks][HD * odd:HD * odd + HD, hp * P:hp * P + P]
                            vcols = slice(hp * P + HD * odd, hp * P + HD * odd + HD)
                            if G is G0:
                                for k in range(nk):
                                    p0 = (odd * nk + k) * P
                                    ins = pe.matmul(out, G.qkv[:, v, k, vcols], probT[:, hp % 2, p0:p0 + P],
                                                    start=k == 0, stop=k == nk - 1)
                                continue
                            p0 = odd * 2 * P
                            pe.matmul(out, G.qkv[:, v, 0, vcols], probT[:, hp % 2, p0 + P:p0 + 2 * P], start=True,
                                      stop=False, skip_group_check=True)
                            for b in range(STREAMS):
                                ins = pe.matmul(out[:, b * NEW:b * NEW + NEW], vc[:, n % 2, b, HD * odd:HD * odd + HD],
                                                probT[:, hp % 2, p0 + b * NEW:p0 + b * NEW + NEW], start=False,
                                                stop=b == STREAMS - 1, skip_group_check=True)
                        ins.then_inc(to(G, "pv_done"), 1)

                for br in range(2):
                    ab = "ab"[br]
                    if br and G is G0:
                        heads_in(1)
                    for t in every:
                        yield AT["score_" + ab][0]
                        yield from score_heads(br, t)
                        if G is G0:
                            r = br * G.n + t
                            gate_units(GATES_HEADS[r], r)
                        elif not br:
                            yield AT["heads_b"]
                            heads_in(1)
                        yield AT["values_" + ab][0]
                        yield from weigh_values(br, t)
                if G is G1:
                    yield from projection(range(7, NG), GATES)
                yield AT["branch"]
                pe.wait_ge(to(G, "attended"), 2 * G.n)
                pe.wait_ge(to(G, "logits_read"), 2 * G.n)
                for br in range(2):
                    name = "br_" + "ab"[br]
                    weights_wait(pe, G, name)
                    for t in every:
                        u = br * G.n + t
                        if u >= 2:
                            pe.wait_ge(to(G, "branches_read"), u - 1)
                        for n in range(2):
                            for c in range(PAIRS):
                                ins = pe.matmul(wide[:, 2 * (u % 2) + n, :], G.oT[br][:, c, cols(t)],
                                                slot_weights(G, name)[:, c, 512 * n:512 * n + 512],
                                                start=c == 0, stop=c == PAIRS - 1)
                        ins.then_inc(to(G, "branches_done"), 1)
                yield AT["merge"]
                for t in every:
                    pe.wait_ge(to(G, "merged_ready"), t + 1)
                    for half in range(2):
                        rows(G, "merged", G.merged[:, t, :], t, half)
                for n in range(2):
                    yield AT["out"][n]
                    weights_wait(pe, G, f"out{n}")
                    for t in every:
                        u = n * G.n + t
                        pe.wait_ge(to(G, "transposes_copied"), batch(G, "merged", t, 1) + 1)
                        if u >= banks:
                            pe.wait_ge(to(G, "x1_added"), u - banks + 1)
                        elif G is G1:
                            pe.wait_ge(to(G, "group_copied"), NG)
                        for c in range(DC):
                            ins = pe.matmul(G.accum[u % banks][:, :], G.hT[:, c, cols(t)],
                                            slot_weights(G, f"out{n}")[:, c, :], start=c == 0, stop=c == DC - 1)
                        ins.then_inc(to(G, "out_done"), 1)
                yield AT["h2"]
                for t in every:
                    pe.wait_ge(S("h2_ready"), G.tiles[t] + 1)
                    for half in range(2):
                        rows(G, "h2", h2[:, G.tiles[t], :], t, half)

            def queries(G):
                for q in range(4):
                    yield QUERY[G.name][q]
                    weights_wait(pe, G, f"pq{q}")
                    if q == 0:
                        pe.wait_ge(to(G, "transposes_copied"), len(G.batches))
                        pe.wait_ge(to(G, "x1_added"), 2 * G.n)
                    for k in range(QG):
                        u = QG * q + k
                        if u >= 2:
                            pe.wait_ge(to(G, "query_copied"), u - 1)
                        for c in range(DC):
                            ins = pe.matmul(qbanks[u % 2][:, 0:G.n * P], slot_weights(G, f"pq{q}")[:, c, k * P:k * P + P],
                                            G.h2T[:, c, :], start=c == 0, stop=c == DC - 1)
                        ins.then_inc(to(G, "query_done"), 1)
                    pe.wait_ge(to(G, "query_copied"), QG * q + QG)
                    pe.wait_ge(to(G, "branches_read"), 2 * G.n)
                    for t in range(G.n):
                        r = q * G.n + t
                        if r >= 4:
                            pe.wait_ge(to(G, "router_copied"), r - 3)
                        for k in range(QG):
                            ins = pe.matmul(wide[:, r % 4, k * P:k * P + P], G.pqT[:, k, cols(t)], cT[:, k % 2, :],
                                            start=True, stop=True)
                        ins.then_inc(to(G, "score_done"), 1)

            for _ in steps(G0):
                pass

            def add_rows(t, j, sub, start=False, stop=False):
                m = (j * 2) + (t * HALVES + sub)
                for s in range(HALF):
                    q = sub * HALF + s
                    pe.wait_ge(S("diag_done"), m * HALF + (s + 1))
                    pe.wait_ge(S(f"v_rows{q}"), j * 16 + (t * HALVES // 2 + 1) * 16)
                    for n in range(2):
                        ins = pe.matmul(ysum[n][:, :], diag[:, q, :], vbuf[:, q, n * 512:n * 512 + 512],
                                        start=start and s == 0, stop=stop and s == HALF - 1)
                    ins.then_inc(S("v_added"), 1)

            between = [laid(queries(G0)), laid(steps(G1)), laid(queries(G1))]
            start_laid(between)
            for m in range(LAID):
                t = m // HALVES
                if t and m % HALVES == 0:
                    pe.wait_ge(S("y_ready"), t)
                add_rows(t, m % HALVES // 2, m % 2, start=m % HALVES == 0, stop=m % HALVES == HALVES - 1)
                for b in between:
                    b.send(m)
            with pe.Fori(LAID // 2 - HALVES, HALVES // 2 - 1) as j:
                for sub in range(2):
                    add_rows(SAMPLE, j, sub)
            for sub in range(2):
                add_rows(SAMPLE, HALVES // 2 - 1, sub, stop=sub == 1)

        @block.vector
        def _(v):
            def step(ins, name="dve_step"):
                chain(v, ins, name)

            v.wait_ge(S("gain_in"), 16)
            for t in range(TILES):
                G = G1 if t == SAMPLE else G0
                v.wait_ge(S("row_scale"), t + 1)
                signal(v.scalar_tensor_tensor(out=h2[:, t, :], in0=x1[:, t, :], scalar=rsx[:, 0, t:t + 1],
                                              in1=gain[:, :], op0=ALU.mult, op1=ALU.mult), f"{G.name}_h_ready")
            v.wait_ge(S("rbias_in"), 16)
            step(v.tensor_copy(ext[:, :, 0:REL - 1],
                               rbias[:, :, 2 * REL:2 * REL + 1].to_broadcast([P, HEADS, REL - 1])))
            step(v.tensor_copy(ext[:, :, REL - 1:EXT], rbias[:, :, ::-1]), "ext_built")
            v.wait_ge(S("bias_in"), 16 * 4)
            step(v.memset(bias[0:CHUNK, 0, :, CHUNK:P], NEG), "bias_masked")
            v.wait_ge(S("rope_in"), 16 * 7)

            def rope(x, cos, sin, half, tmp, ready):
                lo, hi = x[..., 0:half], x[..., half:2 * half]
                signal(v.tensor_tensor(tmp[0], lo, cos, ALU.mult), "dve_step")
                signal(v.tensor_tensor(tmp[1], hi, sin, ALU.mult), "dve_step")
                signal(v.tensor_tensor(tmp[2], hi, cos, ALU.mult), "dve_step")
                step(v.tensor_tensor(tmp[3], lo, sin, ALU.mult))
                step(v.tensor_tensor(lo, tmp[0], tmp[1], ALU.subtract))
                step(v.tensor_tensor(hi, tmp[2], tmp[3], ALU.add), ready)

            def streams_apart(dst, src):
                return v.tensor_copy(dst.rearrange("p (b c) -> p b c", c=P + NEW)[:, :, 0:NEW],
                                     src.rearrange("p (b j) -> p b j", j=NEW))

            def steps(G):
                every = range(G.n)
                g0, name = G.tiles[0], G.name
                tiles = slice(g0, g0 + G.n)
                head = 0
                for g, (what, _, _) in enumerate(GROUPS[:7]):
                    yield NORM[g]
                    if what in ("aq", "ak", "bq", "bk"):
                        k, n = ("aq", "ak", "bq", "bk").index(what), 8 * G.n
                        v.wait_ge(to(G, "group_copied"), G.n * (g + 1))
                        x = G.qkv[:, where[what]].rearrange("p t (h d) -> p (t h) d", d=HD)
                        sq = G.tmp[:, 0:512 * G.n].rearrange("p (n d) -> p n d", d=HD)
                        step(v.tensor_tensor(sq, x, x, ALU.mult))
                        step(v.tensor_reduce(ssh[:, k, 0:n], sq, AX, ALU.add), name + "_heads_squared")
                        head += 1
                        yield NORM[g] + 2
                        v.wait_ge(to(G, "head_scale"), head)
                        step(v.tensor_tensor(x, x, rsh[:, k, 0:n].unsqueeze(2).to_broadcast([P, n, HD]), ALU.mult))
                        last = v.tensor_tensor(x, x, hgain[:, k:k + 1, :].to_broadcast([P, n, HD]), ALU.mult)
                        if what[0] == "b":
                            step(last, name + "_heads_ready")
                            continue
                        step(last)
                        w = 256 * G.n
                        tmp = [G.tmp[:, m * w:m * w + w].rearrange("p (t h d) -> p t h d", t=G.n, h=HEADS)
                               for m in range(4)]
                        cs = [ropet[:, m, tiles].unsqueeze(2).to_broadcast([P, G.n, HEADS, HD // 2]) for m in range(2)]
                        rope(G.qkv[:, where[what]].rearrange("p t (h d) -> p t h d", d=HD), cs[0], cs[1], HD // 2, tmp,
                             name + "_heads_ready")
                    if what == "ix":
                        v.wait_ge(to(G, "group_copied"), G.n * (g + 1))
                        ik = G.ix[:, :, 256:288]
                        sq = G.tmp[:, 0:ID * G.n].rearrange("p (t d) -> p t d", d=ID)
                        step(v.tensor_tensor(sq, ik, ik, ALU.mult))
                        step(v.tensor_reduce(ssh[:, 4, 0:G.n], sq, AX, ALU.add), name + "_heads_squared")
                        head += 1
                        step(v.tensor_scalar(G.ix[:, :, 288:296], G.ix[:, :, 288:296], IH ** -0.5, None, ALU.mult))
                        iq = G.ix[:, :, 0:256].rearrange("p t (h d) -> p t h d", d=ID)
                        w = 128 * G.n
                        tmp = [G.tmp[:, m * w:m * w + w].rearrange("p (t h d) -> p t h d", t=G.n, h=IH)
                               for m in range(4)]
                        cs = [ropei[:, m, tiles].unsqueeze(2).to_broadcast([P, G.n, IH, ID // 2]) for m in range(2)]
                        rope(iq, cs[0], cs[1], ID // 2, tmp, "dve_step")
                        yield NORM[g] + 2
                        v.wait_ge(to(G, "head_scale"), head)
                        step(v.tensor_tensor(ik, ik, rsh[:, 4, 0:G.n].unsqueeze(2).to_broadcast([P, G.n, ID]), ALU.mult))
                        step(v.tensor_tensor(ik, ik, igain[:, :].unsqueeze(1).to_broadcast([P, G.n, ID]), ALU.mult))
                        w = 16 * G.n
                        tmp = [G.tmp[:, m * w:m * w + w].rearrange("p (t d) -> p t d", t=G.n) for m in range(4)]
                        rope(ik, ropei[:, 0, tiles], ropei[:, 1, tiles], ID // 2, tmp, name + "_ik_ready")
                yield AT["heads_a"] - 1
                if G is G1:
                    step(v.memset(bias[:, 0], NEG), "bias_cleared")
                    step(v.memset(qm, 0.0))
                    v.wait_ge(S("cik_in"), 16)
                    step(v.tensor_copy(cikrep, cik.unsqueeze(2).to_broadcast([P, STREAMS, 4, ID])))
                step(v.tensor_copy(G.ikrep, G.ix[:, :, 256:288].unsqueeze(2).to_broadcast([P, G.n, 4, ID])),
                     name + "_index_ready")
                yield AT["index"]
                if G is G1:
                    v.wait_ge(to(G, "transposes_copied"), batch(G, "index", 0) + 1)
                    for c in range(2):
                        signal(streams_apart(qm[:, c, :], G.iqT[:, c, :]), "iqm_ready" if c else "dve_step")
                yield AT["select"]
                v.wait_ge(S("own_set"), 1)
                for t in every:
                    tile = G.tiles[t]
                    n = SEEN[tile]
                    v.wait_ge(to(G, "relu_done"), t + 1)
                    s = score[:, t, 0:n]
                    for h in range(IH):
                        rel = probs[:, at_index(h), 0:n]
                        w = G.ix[:, t, 288 + h:289 + h]
                        if h == 0:
                            step(v.tensor_scalar(s, rel, w, None, ALU.mult))
                        else:
                            step(v.scalar_tensor_tensor(out=s, in0=rel, scalar=w, in1=s, op0=ALU.mult, op1=ALU.add),
                                 name + "_scored" if h == IH - 1 else "dve_step")
                    if G is G1:
                        for hp in range(2):
                            v.wait_ge(to(G, "index_done"), 1)
                            signal(streams_apart(qm[:, hp, :], G.qk[:, 0, hp, :]), "qm_ready")
                        yield AT["select"] + 1
                    if tile < SAMPLE:
                        step(v.memset(score[0:CHUNK, t, n - CHUNK:n], NEG))
                    else:
                        step(v.tensor_tensor(score[:, t, P:2 * P], score[:, t, P:2 * P], own[:, :], ALU.add))
                        step(v.memset(score[:, t, 256:264], PAD))
                    for _ in range(SELECT[tile] // 8):
                        step(v.max(mx8[:, :], s))
                        step(v.match_replace(s, mx8[:, :], s, TAKEN))
                    if SELECT[tile] % 8:
                        step(v.max(mx8[:, :], s))
                        step(v.memset(mx8[:, SELECT[tile] % 8:8], PAD))
                        step(v.match_replace(score[:, t, :], mx8[:, :], score[:, t, :], TAKEN))
                    step(v.tensor_scalar(mask[:, t, 0:n], s, TAKEN / 2, NEG, ALU.is_gt, ALU.mult), "mask_ready")

                for br in range(2):
                    ab = "ab"[br]
                    for t in every:
                        r = br * G.n + t
                        n = SEEN[G.tiles[t]]
                        pr = probs[:, :, 0:n]
                        if G is G1:
                            for hp in range(0 if br else 2, PAIRS):
                                yield AT["score_" + ab][hp] - 1
                                m = br * PAIRS + hp
                                v.wait_ge(to(G, "pair_scored"), m - 1)
                                if br and hp == 0:
                                    v.wait_ge(to(G, "transposes_copied"), batch(G, "q", 1, 0) + 1)
                                signal(streams_apart(qm[:, m % 2, :], G.qk[:, 0, hp, :]), "qm_ready")
                            yield AT["soft_" + ab]
                            v.wait_ge(to(G, "pair_scored"), (br + 1) * PAIRS)
                        else:
                            v.wait_ge(to(G, "logits_done"), r + 1)
                        if r:
                            v.wait_ge(to(G, "transposed"), batch(G, "prob", *divmod(r - 1, G.n), PAIRS - 1) + 1)
                        if br == 0:
                            step(v.scalar_tensor_tensor(out=pr, in0=logits[:, :, 0:n], scalar=HD ** -0.5,
                                                        in1=mask[:, t:t + 1, 0:n].to_broadcast([P, HEADS, n]),
                                                        op0=ALU.mult, op1=ALU.add), name + "_logits_read")
                        else:
                            if G is G1:
                                v.wait_ge(S("sample_bias_in"), 16 * 4 * STREAMS)
                            kinds = [[0], [1, 0], [1, 0]][G.tiles[t]]
                            for k, kind in enumerate(kinds):
                                step(v.scalar_tensor_tensor(out=probs[:, :, k * P:k * P + P],
                                                            in0=logits[:, :, k * P:k * P + P], scalar=HD ** -0.5,
                                                            in1=bias[:, kind], op0=ALU.mult, op1=ALU.add),
                                     name + "_logits_read" if k == len(kinds) - 1 else "dve_step")
                        step(v.tensor_reduce(rowmax[:, :], pr, AX, ALU.max))
                        step(v.tensor_scalar(rowmax[:, :], rowmax[:, :], -1.0, None, ALU.mult), name + "_rowmax_ready")
                        yield AT["soft_" + ab] + 2
                        v.wait_ge(to(G, "exp_done"), HEADS * (r + 1))
                        step(v.reciprocal(rowinv[:, :], rowsum[:, :]))
                        step(v.tensor_tensor(pr, pr, rowinv[:, :].unsqueeze(2).to_broadcast([P, HEADS, n]), ALU.mult),
                             name + "_probs_ready")

                yield AT["branch"] + 1
                for t in every:
                    v.wait_ge(to(G, "branches_done"), t + 1)
                    v.wait_ge(to(G, "group_copied"), G.n * NG)
                    step(v.tensor_tensor(G.merged[:, t, :], widef[:, t * D:t * D + D], G.gates[t][:, 0:D], ALU.mult),
                         name + "_branches_read")
                for t in every:
                    u = G.n + t
                    v.wait_ge(to(G, "branches_done"), u + 1)
                    step(v.tensor_tensor(G.merge_tmp, widef[:, u % 2 * D:u % 2 * D + D], G.gates[t][:, D:2 * D],
                                         ALU.mult), name + "_branches_read")
                    step(v.tensor_tensor(G.merged[:, t, :], G.merged[:, t, :], G.merge_tmp, ALU.add),
                         name + "_merged_ready")
                for n in range(2):
                    yield AT["out"][n] + 1
                    for t in every:
                        u = n * G.n + t
                        v.wait_ge(to(G, "out_done"), u + 1)
                        part = x1[:, G.tiles[t], n * 512:n * 512 + 512]
                        step(v.tensor_tensor(part, G.accum[u % len(G.accum)][:, :], part, ALU.add), name + "_x1_added")
                yield AT["scale"] + 2
                v.wait_ge(S("gain_in"), 32)
                for t in G.tiles:
                    v.wait_ge(S("row_scale"), TILES + t + 1)
                    signal(v.scalar_tensor_tensor(out=h2[:, t, :], in0=x1[:, t, :], scalar=rsx[:, 1, t:t + 1],
                                                  in1=gain[:, :], op0=ALU.mult, op1=ALU.mult), "h2_ready")

            for _ in steps(G0):
                pass

            def together(instructions, name="dve_step"):
                for ins in instructions:
                    signal(ins, name)
                v.wait_ge(sems[name], counts[name])

            def top16(values, top, index, rows):
                together(v.max(top(n)[:, 0:8], values(n)) for n in rows)
                together(v.max_index(index(n)[:, 0:8], top(n)[:, 0:8], values(n)) for n in rows)
                together(v.match_replace(values(n), top(n)[:, 0:8], values(n), TAKEN) for n in rows)
                together(v.max(top(n)[:, 8:16], values(n)) for n in rows)
                together(v.max_index(index(n)[:, 8:16], top(n)[:, 8:16], values(n)) for n in rows)

            def route(t):
                G, scores = (G1, sc[0]) if t == SAMPLE else (G0, sc[t])
                v.wait_ge(S("iota_set"), 1)
                full = [P, QH, PEER_K, PEER_K]
                for q in range(4):
                    at = ROUTE[t][q]
                    yield at
                    v.wait_ge(to(G, "router_copied"), q + 1 if t == SAMPLE else 2 * q + t + 1)
                    top16(lambda n: scores[:, QG * q + n, :], lambda n: rtop[:, n, :], lambda n: rtopi[:, n, :],
                          range(QG))
                    yield at
                    step(v.tensor_copy(rtopf[:, :, :], rtopi[:, :, :]))
                    r4 = rtop[:, :, :].rearrange("p (h s) k -> p h s k", s=2)
                    f4 = rtopf[:, :, :].rearrange("p (h s) k -> p h s k", s=2)
                    cand4 = cand.rearrange("p h (a b) -> p h a b", b=PEER_K)
                    step(v.tensor_tensor(cand4, r4[:, :, 0, :].unsqueeze(3).to_broadcast(full),
                                         r4[:, :, 1, :].unsqueeze(2).to_broadcast(full), ALU.add))
                    top16(lambda n: cand[:, n, :], lambda n: sv[:, n, :], lambda n: si[:, n, :], range(QH))
                    gt = gate[:, t, QS * q:QS * q + QS].rearrange("p (h k) -> p h k", k=PEER_K)
                    step(v.tensor_tensor(gt, sv[:, :, :], sv[:, :, 0:1].to_broadcast([P, QH, PEER_K]), ALU.subtract))
                    step(v.tensor_copy(sv[:, :, :], gt), "picked")
                    yield at + 1
                    halves = [sif[:, s, :].rearrange("p (h k) -> p h k", k=PEER_K) for s in range(2)]
                    step(v.tensor_scalar(sj[:, :, :], si[:, :, :], 4, None, ALU.logical_shift_right))
                    step(v.tensor_copy(halves[0], sj[:, :, :]))
                    step(v.tensor_scalar(sj[:, :, :], si[:, :, :], 15, None, ALU.bitwise_and))
                    step(v.tensor_copy(halves[1], sj[:, :, :]))
                    io = iota16[:, :].unsqueeze(1).unsqueeze(1).to_broadcast(full)
                    together(v.tensor_tensor(pick[s], halves[s].unsqueeze(3).to_broadcast(full), io, ALU.is_equal)
                             for s in range(2))
                    together(v.tensor_tensor(pick[s], pick[s], f4[:, :, s, :].unsqueeze(2).to_broadcast(full),
                                             ALU.mult) for s in range(2))
                    together(v.tensor_reduce(halves[s], pick[s], AX, ALU.add) for s in range(2))
                    step(v.scalar_tensor_tensor(out=sif[:, 0, :], in0=sif[:, 0, :], scalar=float(NKEYS),
                                                in1=sif[:, 1, :], op0=ALU.mult, op1=ALU.add))
                    v.wait_ge(S("expert_exp"), 4 * t + q + 1)
                    step(v.tensor_reduce(esum[:, :], sv[:, :, :], AX, ALU.add))
                    step(v.reciprocal(esum[:, :], esum[:, :]))
                    step(v.tensor_tensor(gt, sv[:, :, :], esum[:, :].unsqueeze(2).to_broadcast([P, QH, PEER_K]),
                                         ALU.mult))
                    step(v.tensor_copy(expert[:, t, QS * q:QS * q + QS], sif[:, 0, :]), "routed")

            def dot(t, j, sub):
                m = (j * 2) + (t * HALVES + sub)
                if not (isinstance(m, int) and m < 2):
                    v.wait_ge(S("gelu_done"), m - 1)
                for s in range(HALF):
                    v.wait_ge(S(f"u_rows{s}"), m * 16 + 16)
                    v.tensor_tensor_reduce(ubuf[:, s, :], ubuf[:, s, :], h2[:, t, :], 1.0, 0.0, ALU.mult, ALU.add,
                                           dots[:, sub, s:s + 1]).then_inc(S("dot_done"), 1)

            def add_y(t):
                v.wait_ge(S("v_added"), (t + 1) * SLOTS)
                for n in range(2):
                    part = x1[:, t, n * 512:n * 512 + 512]
                    signal(v.tensor_tensor(part, ysum[n][:, :], part, ALU.add), "y_ready" if n else "dve_step")

            between = [laid(x) for x in (route(0), route(1), steps(G1), route(SAMPLE))]
            start_laid(between)
            for m in range(LAID):
                if m % HALVES == 1 and m > HALVES:
                    add_y(m // HALVES - 1)
                dot(m // HALVES, m % HALVES // 2, m % 2)
                for b in between:
                    b.send(m)
            with v.Fori(LAID // 2 - HALVES, HALVES // 2) as j:
                for sub in range(2):
                    dot(SAMPLE, j, sub)
            add_y(SAMPLE)


NAMES = ["x_prompt", "x_sample", "cache_a_k", "cache_a_v", "cache_a_ik", "cache_b_k", "cache_b_v", "g_attn", "w_in",
         "g_qa", "g_ka", "g_ik", "g_qb", "g_kb", "rel_bias", "w_br_a", "w_br_b", "w_out", "g_ffn", "w_pq",
         "peer_c1", "peer_c2", "peer_u", "peer_v"]
MATRICES = ("w_in", "w_br_a", "w_br_b", "w_out", "w_pq")
OUTS = [("y_prompt", (1, 256, D)), ("y_sample", (STREAMS, NEW, D)),
        ("a_k_prompt", (1, 1, 256, HEADS, HD)), ("a_v_prompt", (1, 1, 256, HEADS, HD)),
        ("a_ik_prompt", (1, 1, 256, ID)), ("b_k_prompt", (1, 1, 256, HEADS, HD)),
        ("b_v_prompt", (1, 1, 256, HEADS, HD)),
        ("a_k_sample", (1, STREAMS, NEW, HEADS, HD)), ("a_v_sample", (1, STREAMS, NEW, HEADS, HD)),
        ("a_ik_sample", (1, STREAMS, NEW, ID)), ("b_k_sample", (1, STREAMS, NEW, HEADS, HD)),
        ("b_v_sample", (1, STREAMS, NEW, HEADS, HD))]


def rope_table(half):
    inverse = np.power(np.float32(10000.0), -np.arange(half, dtype=np.float32) / np.float32(half))
    row = np.arange(P)
    positions = np.stack([row, row + P, PAST + row % NEW], axis=1).astype(np.float32)
    angle = (positions[:, :, None] * inverse[None, None, :].astype(np.float32)).astype(np.float32)
    return np.ascontiguousarray(np.stack([np.cos(angle), np.sin(angle)], axis=1).astype(np.float32))


def kernel(**inputs):
    import concourse.bacc as bacc
    from concourse.bass_utils import run_bass_kernel_spmd

    nc = bacc.Bacc("TRN2", target_bir_lowering=False, num_devices=1)
    arrays, ins, outs = {}, {}, {}
    given = {n: np.ascontiguousarray(inputs[n]) for n in NAMES}
    given["rope_head"] = rope_table(HD // 2)
    given["rope_index"] = rope_table(ID // 2)
    for name, a in given.items():
        arrays[f"in_{name}"] = a
        ap = nc.dram_tensor(f"in_{name}", a.shape, mybir.dt.from_np(a.dtype), kind="ExternalInput").ap()
        ins[name] = ap[0] if name in MATRICES else ap
    for name, shape in OUTS:
        outs[name] = nc.dram_tensor(f"out_{name}", shape, F32, kind="ExternalOutput").ap()
    build(nc, ins, outs)
    r = run_bass_kernel_spmd(nc, [arrays], core_ids=[0])
    return tuple(r.results[0][f"out_{name}"] for name, _ in OUTS)
```

```python
from contextlib import ExitStack

import numpy as np

import concourse.bass as bass
from concourse import mybir

F32 = mybir.dt.float32
U32 = mybir.dt.uint32
ALU = mybir.AluOpType
ACT = mybir.ActivationFunctionType
AX = mybir.AxisListType.X

P = 128
D = 1024
DC = D // P
TILES = 3
SAMPLE = 2
NTOK = TILES * P
STREAMS, NEW, PAST = 8, 16, 128
HEADS, HD = 8, 64
PAIRS = HEADS // 2
IH, ID = 8, 32
CHUNK = 64
REL = 128
PEER_H, PEER_K, NKEYS, DQ = 8, 16, 128, 256
SLOTS = PEER_H * PEER_K
EPS = 1e-6
NEG = -1e30
TAKEN = -3e38
PAD = -2e30
BQ_COL = 1832
GATE_COL = 3368
GROUPS = [("aq", 0, 512), ("ak", 512, 512), ("ix", 1536, 296), ("av", 1024, 512),
          ("bq", BQ_COL, 512), ("bk", BQ_COL + 512, 512), ("bv", BQ_COL + 1024, 512)]
GROUPS += [(f"gate{n}", GATE_COL + 512 * n, 512) for n in range(4)]
NG = len(GROUPS)
SEEN = [128, 256, 256]
SELECT = [64, 64, 36]
HALF = 4
VRING = 2 * HALF
HALVES = SLOTS // HALF
QH, QG, QS = 2, 4, 32
LAID = 2 * HALVES + 8
EXT = 384


class Group:

    def __init__(self, name, tiles, qkv, hT, qk, tmp, merged, merge_tmp, gates, oT, h2T, pqT, scores, trans, accum, iqT,
                 ix, ikrep, loads, w0):
        self.name, self.tiles, self.n, self.w0 = name, tiles, len(tiles), w0
        self.qkv, self.hT, self.qk, self.tmp, self.merged, self.merge_tmp = qkv, hT, qk, tmp, merged, merge_tmp
        self.gates, self.oT, self.pqT, self.scores, self.trans, self.accum = gates, oT, pqT, scores, trans, accum
        self.iqT, self.ix, self.ikrep, self.h2T, self.loads = iqT, ix, ikrep, h2T, loads


PROJ = [5, 6, 8, 9, 10, 12, 13]
GATES = [46, 47, 49, 50]
NORM = [p + 2 for p in PROJ]
AT = dict(heads_a=18, index=19, select=23, score_a=[24, 25, 26, 27], soft_a=28, values_a=[31, 32, 33, 34],
          heads_b=29, score_b=[35, 36, 37, 38], soft_b=39, values_b=[42, 43, 44, 45], branch=51, merge=53,
          out=[54, 55], scale=56, h2=57)
FIRST = -9
QUERY = dict(prompt=[-8, -4, -3, 1, 3], sample=[57, 59, 61, 63])

def query_at(group, n, part, lag=0):
    at = QUERY[group][n]
    return at if at < 0 else at + part + lag


QUERY_STEPS = dict(prompt=[(0, 0, 1), (0, 1, 2), (1, 0, 2), (2, 0, 2), (3, 0, 2)],
                   sample=[(q, 0, 1) for q in range(4)])
ROUTE = [[(-7, -5, -3), (0, 1, 2), (5, 5, 6), (7, 7, 8)], [(m, m, m + 1) for m in (9, 11, 13, 15)],
         [(m, m, m + 1) for m in (61, 63, 65, 67)]]
LAST = dict(out=-7, x1=-6, h2=-4)
GATES_INDEX = [1, 1]
GATES_HEADS = [2, 2, 1, 1]


def build(nc, i, o):
    with ExitStack() as ctx:
        def sb(name, shape, dt=F32):
            return ctx.enter_context(nc.sbuf_tensor(name, shape, dt))

        def psum(name, shape):
            return ctx.enter_context(nc.psum_tensor(name, shape, F32))

        sems, counts = {}, {}

        def S(name):
            if name not in sems:
                sems[name] = ctx.enter_context(nc.semaphore(name))
                counts[name] = 0
            return sems[name]

        def signal(ins, name):
            ins.then_inc(S(name), 1)
            counts[name] += 1

        def chain(eng, ins, name):
            signal(ins, name)
            eng.wait_ge(sems[name], counts[name])

        ident = sb("ident", [P, P])
        ropet = sb("ropet", [P, 2, TILES, HD // 2])
        ropei = sb("ropei", [P, 2, TILES, ID // 2])
        gain = sb("gain", [P, D])
        hgain = sb("hgain", [P, 4, HD])
        igain = sb("igain", [P, ID])
        iota16 = sb("iota16", [P, 16])
        own = sb("own", [P, P])
        rows_ring = sb("rows_ring", [P, (HALF + VRING) * D])
        shared = sb("shared", [P, 8448])
        ring = sb("ring", [P, 2, 4096])
        x1 = sb("x1", [P, TILES, D])
        h2 = sb("h2", [P, TILES, D])
        qkv1 = sb("qkv1", [P, 6 * 512])
        hT1 = sb("hT1", [P, DC, P])
        qk1 = sb("qk1", [P, 2 * PAIRS * P])
        iqTs = sb("iqTs", [P, 512])
        ixs = sb("ixs", [P, 2, 296])
        prob = sb("prob", [P, HEADS * 256])
        probT = sb("probT", [P, 2, 512])
        bias = sb("bias", [P, 2, HEADS, P])
        score = sb("score", [P, 2, 264])
        mask = sb("mask", [P, 2, 256])
        ikT = sb("ikT", [P, 256])
        new_bias = sb("new_bias", [P, HEADS, NEW])
        diag = sb("diag", [P, VRING, P])
        cT = sb("cT", [P, 2, P])
        rtop = sb("rtop", [P, QG, 16])
        rtopi = sb("rtopi", [P, QG, 16], U32)
        rtopf = sb("rtopf", [P, QG, 16])
        sv = sb("sv", [P, QH, PEER_K])
        si = sb("si", [P, QH, PEER_K], U32)
        sj = sb("sj", [P, QH, PEER_K], U32)
        sif = sb("sif", [P, 2, QS])
        expert = sb("expert", [P, TILES, SLOTS], U32)
        gate = sb("gate", [P, TILES, SLOTS])
        staged = sb("staged", [P, 2, HALF], U32)
        dots = sb("dots", [P, 2, HALF])
        gelu = sb("gelu", [P, 2, HALF])
        wexp = sb("wexp", [P, 2, HALF])
        ssx = sb("ssx", [P, 2, TILES])
        rsx = sb("rsx", [P, 2, TILES])
        ssh = sb("ssh", [P, 5, 16])
        rsh = sb("rsh", [P, 5, 16])
        mhalf = sb("mhalf", [P, 16])
        mx8 = sb("mx8", [P, 8])
        rowmax = sb("rowmax", [P, HEADS])
        rowsum = sb("rowsum", [P, HEADS])
        rowinv = sb("rowinv", [P, HEADS])
        esum = sb("esum", [P, QH])

        AQ, BQ, AK, AV, BK, BV = range(6)
        where = {"aq": AQ, "bq": BQ, "ak": AK, "av": AV, "bk": BK, "bv": BV}
        qkv0 = rows_ring[:, 0:6144]
        sc = [shared[:, 2048 + 2048 * n:4096 + 2048 * n].rearrange("p (g k) -> p g k", g=16) for n in range(2)]
        cand = shared[:, 6144:6656].rearrange("p (h k) -> p h k", h=QH)
        pick = [shared[:, 6656 + 512 * n:7168 + 512 * n].rearrange("p (h k j) -> p h k j", h=QH, k=PEER_K)
                for n in range(2)]
        ext = shared[:, 2048:2048 + HEADS * EXT].rearrange("p (h k) -> p h k", h=HEADS)
        rbias = shared[:, 5120:5120 + HEADS * 257].rearrange("p (h k) -> p h k", h=HEADS)
        raw = shared[:, 0:2048].rearrange("p (s b c) -> p s b c", s=2, b=STREAMS)
        kcT = shared[:, 2048:4096].rearrange("p (s b c) -> p s b c", s=2, b=STREAMS)
        vc = shared[:, 4096:6144].rearrange("p (s b c) -> p s b c", s=2, b=STREAMS)
        cikT = shared[:, 4096:5120].rearrange("p (b c) -> p b c", b=STREAMS)
        QM = 9 * P
        qm = shared[:, 6144:6144 + 2 * QM].rearrange("p (s c) -> p s c", s=2)
        probs2 = h2[:, 1:3, :].rearrange("p t (h k) -> p (t h) k", h=4)

        def probs_of(G, r):
            return probs2 if G.name == "prompt" and r % 2 else probs

        cik = prob[:, 0:256].rearrange("p (b d) -> p b d", b=STREAMS)
        cikrep = prob[:, 256:1280].rearrange("p (b r d) -> p b r d", b=STREAMS, r=4)
        probs = prob[:, :].rearrange("p (h k) -> p h k", h=HEADS)
        ubuf = rows_ring[:, 0:HALF * D].rearrange("p (s c) -> p s c", s=HALF)
        vbuf = rows_ring[:, HALF * D:].rearrange("p (s c) -> p s c", s=VRING)

        wide = psum("wide", [P, 4, 512])
        widef = wide[:, :, :].rearrange("p b c -> p (b c)")
        logits = widef.rearrange("p (h k) -> p h k", h=HEADS)
        trans = [psum("transA", [P, 512]), psum("transB", [P, 512])]
        accum = [psum("accumA", [P, 512]), psum("accumB", [P, 512])]
        ysum = [trans[0], accum[0]]

        def group(name, tiles, qkv, hT, qk, tmp, merge_tmp, gates, h2T, scores, trans, accum, loads, first_load):
            n = len(tiles)
            return Group(
                name, tiles, qkv=qkv.rearrange("p (a t c) -> p a t c", a=6, t=n),
                hT=hT, qk=qk.rearrange("p (a c n) -> p a c n", a=2, c=PAIRS), tmp=tmp,
                merged=qk.rearrange("p (t c) -> p t c", t=n), merge_tmp=merge_tmp, gates=gates,
                oT=[qkv[:, k * n * 512:(k + 1) * n * 512].rearrange("p (c n) -> p c n", c=PAIRS) for k in range(2)],
                h2T=h2T, pqT=prob[:, 0:QG * n * P].rearrange("p (g n) -> p g n", g=QG), scores=scores, trans=trans, accum=accum,
                iqT=iqTs[:, 0:2 * n * P].rearrange("p (c n) -> p c n", c=2), ix=ixs[:, 0:n, :],
                ikrep=prob[:, 1280:1280 + n * P].rearrange("p (t r d) -> p t r d", t=n, r=4), loads=loads,
                w0=first_load)

        LOADS = [name for name, _, _ in GROUPS] + ["br_a", "br_b", "out1", "pq0", "pq1", "pq2", "pq3"]
        G0 = group("prompt", [0, 1], qkv0, rows_ring[:, 6144:8192].rearrange("p (c n) -> p c n", c=DC),
                   shared[:, 0:2048], shared[:, 0:2048], prob[:, 0:D], [shared[:, 2048:4096], shared[:, 4096:6144]],
                   shared[:, 0:2048].rearrange("p (c n) -> p c n", c=DC), sc, trans, accum, LOADS, 0)
        G1 = group("sample", [SAMPLE], qkv1[:, :], hT1[:, :, :], qk1[:, :], qk1[:, :], shared[:, 0:D],
                   [prob[:, :]], hT1[:, :, :], [sc[0]], trans[1:], accum[1:], LOADS[:-5] + ["out0"] + LOADS[-5:],
                   len(LOADS))

        def query_bank(G, n, k):
            if G is G0 and n == 0:
                return wide[:, 2 + k % 2, :]
            return [accum[1], trans[1]][k % 2]

        out0_weights = rows_ring[:, 8192:12288]

        bias_rows = nc.dram_tensor("bias_rows", [P, HEADS * EXT], F32).ap()

        def weights_dram(name):
            for group_name, c0, c in GROUPS:
                if name == group_name:
                    return i["w_in"][:, c0:c0 + c].rearrange("(k p) c -> p k c", p=P)
            if name[:2] == "br":
                return i["w_" + name].rearrange("(k p) c -> p k c", p=P)
            c0 = 512 * int(name[-1])
            return i["w_out" if name[:3] == "out" else "w_pq"][:, c0:c0 + 512].rearrange("(k p) c -> p k c", p=P)

        def load_of(G, name):
            return G.w0 + G.loads.index(name)

        def slot_weights(G, name):
            if name not in G.loads:
                return out0_weights.rearrange("p (k c) -> p k c", k=DC)
            n = load_of(G, name)
            chunks, c = weights_dram(name).shape[1:]
            return ring[:, n % 2, 0:chunks * c].rearrange("p (k c) -> p k c", k=chunks)

        def weights_wait(eng, G, name):
            if name not in G.loads:
                eng.wait_ge(S("out0_in"), 16)
                return
            n = load_of(G, name)
            eng.wait_ge(S(f"weights_in{n % 2}"), 16 * (n // 2 + 1))

        def at_index(h):
            return (h % 4) * 2 + h // 4

        def cols(t):
            return slice(t * P, t * P + P)

        def to_all_rows(row):
            return bass.AP(tensor=row.tensor, offset=row.offset, ap=[[0, P], [1, row.shape[-1]]])

        for G in (G0, G1):
            every = range(G.n)
            G.batches = [("h", t, half) for t in every for half in range(2)]
            if G is G1:
                G.batches += [("cik", half) for half in range(2)]
            G.batches += [("index", t) for t in every]
            if G is G0:
                G.batches += [("centroids",)]
            for br in range(2):
                G.batches += [(name, br, t) for name in "qk" for t in every]
                for t in every:
                    if G is G1:
                        G.batches += [("cache", br, hp, half) for hp in range(PAIRS) for half in range(2)]
                    G.batches += [("prob", br, t, hp) for hp in range(PAIRS)]
            G.batches += [("merged", t, half) for t in every for half in range(2)]
            G.batches += [("h2", t, half) for t in every for half in range(2)]
        for G in (G0, G1):
            bs = [b for b in G.batches if b[0] in "qk" and b[1] == 1]
            rest = [b for b in G.batches if b not in bs]
            k = rest.index(("prob", 0, G.n - 1, 0))
            G.batches = rest[:k] + bs + rest[k:]

        def batch(G, *key):
            return G.batches.index(key)

        def to(G, name):
            return S(f"{G.name}_{name}")

        block = ctx.enter_context(nc.Block())

        def laid(steps):
            k = next(steps)
            m = yield
            while True:
                while k <= m:
                    k = next(steps, 1 << 30)
                m = yield

        def early(steps):
            for k in steps:
                yield FIRST if k >= 0 else k

        def start_laid(between):
            for b in between:
                next(b)
            for m in range(FIRST, 0):
                for b in between:
                    b.send(m)

        def gate_banks():
            banks = [n % 2 for n in range(sum(GATES_INDEX))]
            for r, n in enumerate(GATES_HEADS):
                banks += [(r + n - k) % 2 for k in range(n)]
            return [(7 * G0.n + n, bank) for n, bank in enumerate(banks)]

        def copied_before(bank, units):
            return max(u + 1 for u, b in [(12, 0), (13, 1)] + gate_banks() if u < units and b == bank)

        @block.sync
        def _(sp):
            for t in range(TILES):
                src = i["x_prompt"][0, cols(t), :] if t < SAMPLE else i["x_sample"].rearrange("b s c -> (b s) c")
                sp.dma_start(x1[:, t, :], src).then_inc(S(f"x_in{t}"), 16)
                if t == 0:
                    sp.dma_start(gain[:, :], to_all_rows(i["g_attn"])).then_inc(S("gain_in"), 16)
                else:
                    name = G0.loads[t - 1]
                    sp.dma_start(slot_weights(G0, name), weights_dram(name)).then_inc(S(f"weights_in{t - 1}"), 16)
            sp.dma_start(ropet[:, :, :, :], i["rope_head"]).then_inc(S("rope_in"), 16)
            sp.dma_start(ropei[:, :, :, :], i["rope_index"]).then_inc(S("rope_in"), 16)
            for n, g in enumerate(("g_qa", "g_ka", "g_qb", "g_kb")):
                sp.dma_start(hgain[:, n, :], to_all_rows(i[g])).then_inc(S("rope_in"), 16)
            sp.dma_start(igain[:, :], to_all_rows(i["g_ik"])).then_inc(S("rope_in"), 16)
            sp.dma_start(rbias, bass.AP(tensor=i["rel_bias"].tensor, offset=i["rel_bias"].offset,
                                        ap=[[0, P], [2 * REL + 1, HEADS], [1, 2 * REL + 1]])).then_inc(S("rbias_in"), 16)
            sp.wait_ge(S("ext_built"), 1)
            sp.dma_start(bias_rows, ext.rearrange("p h k -> p (h k)")).then_inc(S("ext_stored"), 16)

            def load_bias(dst, keys, first, counted):
                for n in range(HEADS):
                    h = n % 4 * 2 + n // 4
                    src = bass.AP(tensor=bias_rows.tensor, offset=bias_rows.offset + h * EXT + first,
                                  ap=[[0, STREAMS], [HEADS * EXT - 1, NEW], [1, keys]])
                    sp.dma_start(dst[:, n, :], src).then_inc(S(counted), 16)

            def load_tables():
                sp.wait_ge(S("ext_stored"), 16)
                sp.wait_ge(to(G0, "transposed"), 2)
                for n in range(2):
                    sp.dma_start(h2[:, 0, n * P:n * P + P], i[f"peer_c{n + 1}"][0]).then_inc(S("centroids_in"), 16)
                for kind, first in enumerate((255, 127)):
                    for odd in range(2):
                        src = bass.AP(tensor=bias_rows.tensor, offset=bias_rows.offset + odd * EXT + first,
                                      ap=[[HEADS * EXT - 1, P], [2 * EXT, 4], [1, P]])
                        sp.dma_start(bias[:, kind, 4 * odd:4 * odd + 4, :], src).then_inc(S("bias_in"), 16)
                load_bias(new_bias[:, :, :], NEW, 255, "new_bias_in")

            def weights(G, name, signalled, value):
                sp.wait_ge(S(signalled), value)
                sp.dma_start(slot_weights(G, name), weights_dram(name)).then_inc(
                    S(f"weights_in{load_of(G, name) % 2}"), 16)

            def cache_load(what, n):
                br, hp = divmod(n, PAIRS)
                src = i[f"cache_{'ab'[br]}_{what}"][0].rearrange("b k h d -> k b (h d)")[:, :, hp * P:hp * P + P]
                if n >= 2:
                    b2, hp2 = divmod(n - 2, PAIRS)
                    if what == "k":
                        sp.wait_ge(to(G1, "transposed"), batch(G1, "cache", b2, hp2, 1) + 1)
                    else:
                        sp.wait_ge(to(G1, "pv_done"), b2 * PAIRS + hp2 + 1)
                dst = raw if what == "k" else vc
                sp.dma_start(dst[:, n % 2], src).then_inc(S(f"{what}cache_in{n % 2}"), 16)

            for G in (G0, G1):
                names = [name for name, _, _ in GROUPS]
                for n in range(2 if G is G0 else 0, 7 if G is G1 else NG):
                    if n < 2:
                        weights(G, names[n], f"{G0.name}_query_done", 4 * (n + 4))
                    else:
                        weights(G, names[n], f"{G.name}_group_done", G.n * (n - 1))
                    if n == 3 and G is G0:
                        load_tables()
                if G is G1:
                    sp.wait_ge(S("routed"), 8)
                    sp.dma_start(cik, i["cache_a_ik"][0].rearrange("b k d -> k b d")).then_inc(S("cik_in"), 16)
                    sp.wait_ge(to(G0, "logits_read"), 4)
                    load_bias(bias[:, 1], P, 127, "sample_bias_in")
                    cache_load("k", 0)
                    cache_load("k", 1)
                    sp.wait_ge(to(G1, "index_done"), 1)
                    cache_load("v", 0)
                    cache_load("v", 1)
                    for what, first, last in (("k", 2, 6), ("v", 2, 6), ("k", 6, 8), ("v", 6, 8)):
                        for n in range(first, last):
                            cache_load(what, n)
                    for n in range(7, NG):
                        weights(G, names[n], f"{G.name}_group_done", G.n * (n - 1))
                else:
                    sp.dma_start(out0_weights.rearrange("p (k c) -> p k c", k=DC), weights_dram("out0")).then_inc(
                        S("out0_in"), 16)
                    sp.wait_ge(to(G0, "h_ready"), 2)
                    sp.wait_ge(to(G1, "h_ready"), 1)
                    sp.dma_start(gain[:, :], to_all_rows(i["g_ffn"])).then_inc(S("gain_in"), 16)
                weights(G, "br_a", f"{G.name}_group_done", G.n * (NG - 1))
                weights(G, "br_b", f"{G.name}_group_done", G.n * NG)
                before = [("branches_done", G.n), ("branches_done", 2 * G.n)]
                before += [("out_done", G.n * (2 - k)) for k in (1, 0)][1 if G is G0 else 0:]
                before += [("query_done", 8 if G is G0 else 4), ("query_done", 12 if G is G0 else 8)]
                for name, (signalled, value) in zip(G.loads[NG + 2:], before):
                    weights(G, name, f"{G.name}_{signalled}", value)
            for t in range(TILES):
                sp.wait_ge(S("y_ready"), t + 1)
                dst = o["y_prompt"][0, cols(t), :] if t < SAMPLE else o["y_sample"].rearrange("b s c -> (b s) c")
                sp.dma_start(dst, x1[:, t, :]).then_inc(S("y_stored"), 16)
            sp.wait_ge(S("y_stored"), 16 * TILES)

        @block.gpsimd
        def _(pool):
            pool.memset(mhalf[:, :], -0.5).then_inc(S("pool_set"), 1)
            pool.memset(ident[:, :], 0.0).then_inc(S("pool_set"), 1)
            pool.wait_ge(S("pool_set"), 2)
            pool.affine_select(out=ident[:, :], in_=ident[:, :], compare_op=ALU.not_equal, fill=1.0, base=0,
                               pattern=[[-1, P]], channel_multiplier=1).then_inc(S("ident_set"), 1)
            pool.iota(iota16[:, :], pattern=[[1, 16]], base=0, channel_multiplier=0,
                      allow_small_or_imprecise_dtypes=True).then_inc(S("iota_set"), 1)
            own3 = own[:, :].rearrange("p (b j) -> p b j", j=NEW)
            pool.memset(own[:, :], 0.0).then_inc(S("pool_set"), 1)
            pool.wait_ge(S("pool_set"), 3)
            pool.affine_select(out=own3, in_=own3, compare_op=ALU.is_ge, fill=NEG, base=0,
                               pattern=[[-NEW, STREAMS], [0, NEW]], channel_multiplier=1).then_inc(S("pool_set"), 1)
            pool.wait_ge(S("pool_set"), 4)
            pool.affine_select(out=own3, in_=own3, compare_op=ALU.is_ge, fill=NEG, base=NEW - 1,
                               pattern=[[NEW, STREAMS], [0, NEW]], channel_multiplier=-1).then_inc(S("own_set"), 1)

            def inverse_rms(src, dst, n, width, signalled):
                chain(pool, pool.tensor_scalar(src, src, 1.0 / width, EPS, ALU.mult, ALU.add), "pool_step")
                signal(pool.tensor_tensor(dst, src, mhalf[:, 0:n], ALU.pow), signalled)

            for t in range(TILES):
                pool.wait_ge(S("squares_summed"), t + 1)
                inverse_rms(ssx[:, 0, t:t + 1], rsx[:, 0, t:t + 1], 1, D, "row_scale")

            def steps(G):
                def store(src, name, width):
                    dst = o[f"{name}_{G.name}"]
                    if G is G1:
                        dst = dst[0].rearrange("b t h d -> (b t) (h d)" if width > ID else "b t d -> (b t) d")
                        pool.dma_start(dst, src[:, 0, 0:width]).then_inc(S("state_stored"), 16)
                        return
                    dst = dst[0, 0].rearrange("t h d -> t (h d)") if width > ID else dst[0, 0]
                    pool.dma_start(dst.rearrange("(t p) c -> p t c", p=P), src[:, :, 0:width]).then_inc(
                        S("state_stored"), 16)

                head = ready = 0
                for g, (name, _, _) in enumerate(GROUPS[:7]):
                    yield NORM[g] + 1
                    if name == "ix" or name in ("aq", "ak", "bq", "bk"):
                        m, n, w = (4, G.n, ID) if name == "ix" else (("aq", "ak", "bq", "bk").index(name), 8 * G.n, HD)
                        head += 1
                        pool.wait_ge(to(G, "heads_squared"), head)
                        inverse_rms(ssh[:, m, 0:n], rsh[:, m, 0:n], n, w, f"{G.name}_head_scale")
                    yield NORM[g] + 3
                    if name == "ix":
                        pool.wait_ge(to(G, "ik_ready"), 1)
                        store(G.ix[:, :, 256:288], "a_ik", ID)
                    elif name in ("aq", "ak", "bq", "bk"):
                        ready += 1
                        if name[1] == "k":
                            pool.wait_ge(to(G, "heads_ready"), ready)
                            store(G.qkv[:, where[name]], f"{name[0]}_k", 512)
                    else:
                        pool.wait_ge(to(G, "group_copied"), G.n * (g + 1))
                        store(G.qkv[:, where[name]], f"{name[0]}_v", 512)
                yield AT["scale"] + 1
                for t in G.tiles:
                    pool.wait_ge(S("squares_summed"), TILES + t + 1)
                    inverse_rms(ssx[:, 1, t:t + 1], rsx[:, 1, t:t + 1], 1, D, "row_scale")

            for _ in steps(G0):
                pass

            u_rows, v_rows = i["peer_u"][0], i["peer_v"][0]

            pool.wait_ge(S("state_stored"), 16 * 5)

            def gather(t, j, sub):
                m = (j * 2) + (t * HALVES + sub)
                known = isinstance(m, int)
                if not (known and m < 2):
                    for s in range(HALF):
                        pool.wait_ge(S(f"v_rows{sub * HALF + s}"), j * 16 + (t * HALVES // 2) * 16)
                    pool.wait_ge(S("dot_done"), m * HALF - HALF)
                pool.tensor_copy(staged[:, sub, :], expert[:, t, bass.ds(j * VRING + sub * HALF, HALF)]).then_inc(
                    S(f"experts_staged{sub}"), 1)
                pool.wait_ge(S(f"experts_staged{sub}"), j + (t * HALVES // 2 + 1))
                for s in range(HALF):
                    index = bass.IndirectOffsetOnAxis(ap=staged[:, sub, s:s + 1], axis=0)
                    if not (known and m < 1):
                        pool.wait_ge(S("dot_done"), m * HALF + (s + 1 - HALF))
                        pool.sem_inc(S("u_slot_free"), 1)
                    pool.indirect_dma_start(ubuf[:, s, :], None, u_rows, index).then_inc(S(f"u_rows{s}"), 16)
                    if not (known and m < 2):
                        pool.wait_ge(S("v_added"), m * HALF + (s + 1 - VRING))
                        pool.sem_inc(S("v_slot_free"), 1)
                    q = sub * HALF + s
                    pool.indirect_dma_start(vbuf[:, q, :], None, v_rows, index).then_inc(S(f"v_rows{q}"), 16)

            between = [laid(steps(G1))]
            start_laid(between)
            for m in range(LAID):
                t = m // HALVES
                if m % (HALVES // 4) == 0:
                    pool.wait_ge(S("routed"), m // (HALVES // 4) + 1)
                gather(t, m % HALVES // 2, m % 2)
                for b in between:
                    b.send(m)
            pool.wait_ge(S("routed"), TILES * 4)
            with pool.Fori(LAID // 2 - HALVES, HALVES // 2) as j:
                for sub in range(2):
                    gather(SAMPLE, j, sub)
            pool.wait_ge(S("state_stored"), 16 * 10)

        @block.scalar
        def _(act):
            def squares(t, n):
                chain(act, act.activation(prob[:, D:2 * D], x1[:, t, :], ACT.Square, accum_out=ssx[:, n, t:t + 1]),
                      "squares_summed")

            for t in range(SAMPLE):
                act.wait_ge(S(f"x_in{t}"), 16)
                squares(t, 0)

            def copy_out(G, key, pieces, *waits):
                n = batch(G, *key)
                act.wait_ge(to(G, "transposed"), n + 1)
                for name, value in waits:
                    act.wait_ge(S(name), value)
                for m, (dst, c0, c1) in enumerate(pieces):
                    src = G.trans[n % len(G.trans)][:, c0:c1]
                    if len(dst.shape) == 3:
                        src = src.rearrange("p (c n) -> p c n", c=dst.shape[1])
                    ins = act.activation(dst, src, ACT.Copy)
                    if m == len(pieces) - 1:
                        ins.then_inc(to(G, "transposes_copied"), 1)

            def copy_rows(G, name, t, half):
                dst = G.h2T if name == "h2" else G.hT
                copy_out(G, (name, t, half), [(dst[:, 4 * half:4 * half + 4, cols(t)], 0, 512)])

            for t in range(SAMPLE):
                for half in range(2):
                    copy_rows(G0, "h", t, half)
            act.wait_ge(S(f"x_in{SAMPLE}"), 16)
            squares(SAMPLE, 0)

            def steps(G):
                every = range(G.n)

                def groups(gs, lay):
                    for g, at in zip(gs, lay):
                        yield at
                        for t in every:
                            u = g * G.n + t
                            unit(u, G.accum[u % len(G.accum)])

                def unit(u, bank):
                    g, t = divmod(u, G.n)
                    name, _, c = GROUPS[g]
                    act.wait_ge(to(G, "group_done"), u + 1)
                    src = bank[:, 0:c]
                    if name.startswith("gate"):
                        if G is G0:
                            act.wait_ge(S("ext_stored"), 16)
                        m = g - 7
                        act.activation(G.gates[t][:, m * 512:m * 512 + 512], src, ACT.Sigmoid).then_inc(
                            to(G, "group_copied"), 1)
                    else:
                        dst = G.ix[:, t, :] if name == "ix" else G.qkv[:, where[name], t, :]
                        act.activation(dst, src, ACT.Copy).then_inc(to(G, "group_copied"), 1)

                def heads_out(br):
                    for m, name in enumerate("qk"):
                        for t in every:
                            copy_out(G, (name, br, t), [(G.qk[:, m, :, cols(t)], 0, 512)])

                units = iter(gate_banks())

                def gate_units(n):
                    for _ in range(n):
                        u, bank = next(units)
                        unit(u, accum[bank])

                yield from groups(range(7), [p + 1 for p in PROJ])
                yield AT["heads_a"]
                if G is G1:
                    for half in range(2):
                        copy_out(G, ("cik", half), [(cikT[:, 4 * half:4 * half + 4, :], 0, 512)])
                for t in every:
                    copy_out(G, ("index", t), [(G.iqT[:, :, cols(t)], 0, 256), (ikT[:, cols(t)], 256, 384)])
                if G is G0:
                    copy_out(G, ("centroids",), [(cT[:, :, :], 0, 256)])
                    for half in range(2):
                        copy_rows(G1, "h", 0, half)
                heads_out(0)
                yield AT["index"] + 4
                for t in every:
                    seen = SEEN[G.tiles[t]]
                    act.wait_ge(to(G, "index_done"), t + 1)
                    if t:
                        act.wait_ge(to(G, "scored"), t)
                    act.activation(probs[:, :, 0:seen], logits[:, :, 0:seen], ACT.Relu).then_inc(to(G, "relu_done"), 1)
                    if G is G0:
                        gate_units(GATES_INDEX[t])
                for br in range(2):
                    ab = "ab"[br]
                    for t in every:
                        r = br * G.n + t
                        pr = probs_of(G, r)
                        seen = SEEN[G.tiles[t]]
                        nk = seen // P
                        if G is G1:
                            for hp in range(PAIRS):
                                yield AT["score_" + ab][hp]
                                n = br * PAIRS + hp
                                for half in range(2):
                                    waits = [(f"{G.name}_pair_scored", n - 1)] if n >= 2 else []
                                    copy_out(G, ("cache", br, hp, half),
                                             [(kcT[:, n % 2, 4 * half:4 * half + 4, :], 0, 512)], *waits)
                        if r == 0 and G is G0:
                            gate_units(1)
                        yield AT["soft_" + ab] + 1
                        act.wait_ge(to(G, "rowmax_ready"), r + 1)
                        for h in range(HEADS):
                            act.activation(pr[:, h, 0:seen], pr[:, h, 0:seen], ACT.Exp, bias=rowmax[:, h:h + 1],
                                           accum_out=rowsum[:, h:h + 1]).then_inc(to(G, "exp_done"), 1)
                        if G is G0:
                            gate_units(GATES_HEADS[r] - (r == 0))
                        elif not br:
                            heads_out(1)
                        for hp in range(PAIRS):
                            yield AT["values_" + ab][hp]
                            m = r * PAIRS + hp
                            waits = [(f"{G.name}_pv_done", m - 1)] if m >= 2 else []
                            copy_out(G, ("prob", br, t, hp), [(probT[:, hp % 2, 0:2 * nk * P], 0, 2 * nk * P)], *waits)
                        act.wait_ge(to(G, "pv_done"), (r + 1) * PAIRS)
                        act.activation(G.oT[br][:, :, cols(t)],
                                       G.accum[r % len(G.accum)][:, :].rearrange("p (c n) -> p c n", c=PAIRS),
                                       ACT.Copy).then_inc(to(G, "attended"), 1)
                        if r == 0 and G is G0:
                            heads_out(1)
                if G is G1:
                    yield from groups(range(7, NG), [p + 1 for p in GATES])
                yield AT["merge"]
                for t in every:
                    for half in range(2):
                        copy_rows(G, "merged", t, half)
                for t in every:
                    yield LAST["out"] if t else AT["scale"]
                    act.wait_ge(to(G, "x1_added"), 2 * t + 2)
                    squares(G.tiles[t], 1)
                    yield LAST["out"] if t else AT["h2"]
                    for half in range(2):
                        copy_rows(G, "h2", t, half)

            def queries(G):
                r = 0
                for n, (q, t0, t1) in enumerate(QUERY_STEPS[G.name]):
                    for k in range(QG):
                        if k % 2 == 0:
                            yield query_at(G.name, n, k // 2, 1)
                        act.wait_ge(to(G, "query_done"), QG * n + k + 1)
                        if n:
                            act.wait_ge(to(G, "score_done"), r)
                        act.activation(G.pqT[:, k, t0 * P:t1 * P], query_bank(G, n, k)[:, 0:(t1 - t0) * P],
                                       ACT.Copy).then_inc(to(G, "query_copied"), 1)
                    yield query_at(G.name, n, 2, 1)
                    for t in range(t0, t1):
                        act.wait_ge(to(G, "score_done"), r + 1)
                        act.activation(G.scores[t][:, QG * q:QG * q + QG, :],
                                       wide[:, r % 4, :].rearrange("p (g k) -> p g k", g=QG), ACT.Copy).then_inc(
                            to(G, "router_copied"), 1)
                        r += 1

            def softmax_exps(t):
                for q in range(4):
                    yield ROUTE[t][q][1]
                    act.wait_ge(S("picked"), 4 * t + q + 1)
                    act.activation(sv[:, :, :], sv[:, :, :], ACT.Exp).then_inc(S("expert_exp"), 1)

            def weigh(t, j, sub):
                m = (j * 2) + (t * HALVES + sub)
                act.wait_ge(S("dot_done"), m * HALF + HALF)
                act.activation(gelu[:, sub, :], dots[:, sub, :], ACT.Gelu).then_inc(S("gelu_done"), 1)
                act.wait_ge(S("gelu_done"), m + 1)
                for s in range(HALF):
                    act.activation(wexp[:, sub, s:s + 1], gate[:, t, bass.ds(j * VRING + (sub * HALF + s), 1)],
                                   ACT.Copy, scale=gelu[:, sub, s:s + 1]).then_inc(S("wexp_ready"), 1)
                for s in range(HALF):
                    act.wait_ge(S("wexp_ready"), m * HALF + (s + 1))
                    if not (isinstance(m, int) and m < 2):
                        act.wait_ge(S("v_added"), m * HALF + (s + 1 - VRING))
                    act.activation(diag[:, sub * HALF + s, :], ident[:, :], ACT.Copy, scale=wexp[:, sub, s:s + 1]
                                   ).then_inc(S("diag_done"), 1)

            between = [laid(x) for x in (early(steps(G0)), queries(G0), softmax_exps(0), softmax_exps(1), steps(G1),
                                         queries(G1), softmax_exps(SAMPLE))]
            start_laid(between)
            for m in range(LAID):
                if m % (HALVES // 4) == 0:
                    act.wait_ge(S("gates_ready"), m // (HALVES // 4) + 1)
                weigh(m // HALVES, m % HALVES // 2, m % 2)
                for b in between:
                    b.send(m)
            act.wait_ge(S("gates_ready"), TILES * 4)
            with act.Fori(LAID // 2 - HALVES, HALVES // 2) as j:
                for sub in range(2):
                    weigh(SAMPLE, j, sub)

        @block.tensor
        def _(pe):
            pe.wait_ge(S("ident_set"), 1)

            def transposes(G, key, sources):
                n, banks = batch(G, *key), len(G.trans)
                if n >= banks:
                    pe.wait_ge(to(G, "transposes_copied"), n - banks + 1)
                elif G is G1:
                    pe.wait_ge(to(G0, "transposes_copied"), batch(G0, "centroids") + 1)
                for m, src in enumerate(sources):
                    ins = pe.transpose(G.trans[n % banks][:, m * P:m * P + P], src, ident[:, :])
                ins.then_inc(to(G, "transposed"), 1)

            def rows(G, name, src, t, half):
                transposes(G, (name, t, half), [src[:, c * P:c * P + P] for c in range(4 * half, 4 * half + 4)])

            def h_rows(G):
                for t in range(G.n):
                    pe.wait_ge(to(G, "h_ready"), t + 1)
                    for half in range(2):
                        rows(G, "h", h2[:, G.tiles[t], :], t, half)

            h_rows(G0)

            def steps(G):
                every = range(G.n)
                banks = len(G.accum)

                def unit(u, bank):
                    g, t = divmod(u, G.n)
                    name, _, c1 = GROUPS[g]
                    weights_wait(pe, G, name)
                    for c in range(DC):
                        ins = pe.matmul(bank[:, 0:c1], G.hT[:, c, cols(t)], slot_weights(G, name)[:, c, :],
                                        start=c == 0, stop=c == DC - 1)
                    ins.then_inc(to(G, "group_done"), 1)

                def projection(gs, lay):
                    for g, at in zip(gs, lay):
                        yield at
                        for t in every:
                            u = g * G.n + t
                            if G is G1 and g == 7:
                                pe.wait_ge(to(G, "attended"), 2)
                            elif G is G1 and u == 0:
                                pe.wait_ge(to(G0, "query_copied"), 20)
                            elif u >= banks:
                                pe.wait_ge(to(G, "group_copied"), u - banks + 1)
                            unit(u, G.accum[u % banks])

                units = iter(gate_banks())

                def gate_units(n, r=0):
                    for _ in range(n):
                        u, bank = next(units)
                        pe.wait_ge(to(G, "group_copied"), copied_before(bank, u))
                        if r > 1 or (r and bank != r % 2):
                            pe.wait_ge(to(G, "attended"), r if bank != r % 2 else r - 1)
                        unit(u, accum[bank])

                if G is G1:
                    yield PROJ[0]
                pe.wait_ge(to(G, "transposes_copied"), 2 * G.n)
                yield from projection(range(7), PROJ)
                yield AT["heads_a"]
                pe.wait_ge(to(G, "index_ready"), 1)
                pe.wait_ge(to(G, "heads_ready"), 4)
                if G is G1:
                    for half in range(2):
                        transposes(G, ("cik", half), [cikrep[:, b].rearrange("p r d -> p (r d)")
                                                      for b in range(4 * half, 4 * half + 4)])
                for t in every:
                    transposes(G, ("index", t), [G.ix[:, t, 0:P], G.ix[:, t, P:2 * P],
                                                 G.ikrep[:, t].rearrange("p r d -> p (r d)")])
                if G is G0:
                    pe.wait_ge(S("centroids_in"), 32)
                    transposes(G, ("centroids",), [h2[:, 0, n * P:n * P + P] for n in range(2)])
                    h_rows(G1)
                    pe.wait_ge(to(G1, "transposes_copied"), 2)

                def heads_in(br):
                    for name, w in (("q", BQ if br else AQ), ("k", BK if br else AK)):
                        for t in every:
                            transposes(G, (name, br, t), [G.qkv[:, w, t, hp * P:hp * P + P] for hp in range(PAIRS)])

                heads_in(0)
                yield AT["index"]
                pe.wait_ge(to(G, "transposes_copied"), batch(G, "index", G.n - 1) + 1)
                if G is G1:
                    pe.wait_ge(to(G0, "router_copied"), 8)
                    pe.wait_ge(S("iqm_ready"), 1)
                for t in every:
                    seen = SEEN[G.tiles[t]]
                    if t:
                        pe.wait_ge(to(G, "relu_done"), t)
                    for h in range(IH):
                        if h and h % 2 == 0:
                            yield AT["index"] + h // 2
                        r0 = ID * (h % 4)
                        part = slice(r0, r0 + ID)
                        c0 = at_index(h) * 256
                        q = G.iqT[part, h // 4, cols(t)]
                        if G is G0:
                            ins = pe.matmul(widef[:, c0:c0 + seen], q, ikT[part, 0:seen], start=True, stop=True,
                                            tile_position=(r0, 0))
                            continue
                        for b in range(STREAMS):
                            pe.matmul(widef[:, c0:c0 + P], qm[part, h // 4, b * P:b * P + P], cikT[part, b, :],
                                      start=b == 0, stop=b == STREAMS - 1, tile_position=(r0, 0))
                        ins = pe.matmul(widef[:, c0 + P:c0 + 2 * P], q, ikT[part, 0:P], start=True, stop=True,
                                        tile_position=(r0, 0))
                    ins.then_inc(to(G, "index_done"), 1)
                    if G is G0:
                        gate_units(GATES_INDEX[t])

                def score_heads(br, t):
                    r = br * G.n + t
                    seen = SEEN[G.tiles[t]]
                    if r == 0:
                        pe.wait_ge(to(G, "relu_done"), G.n)
                    else:
                        pe.wait_ge(to(G, "logits_read"), r)
                    if t == 0:
                        pe.wait_ge(to(G, "transposes_copied"), batch(G, "k", br, G.n - 1) + 1)
                    for hp in range(PAIRS):
                        n = br * PAIRS + hp
                        if G is G1:
                            if hp:
                                yield AT["score_" + "ab"[br]][hp]
                            pe.wait_ge(S(f"kcache_in{n % 2}"), 16 * (n // 2 + 1))
                            for half in range(2):
                                transposes(G, ("cache", br, hp, half), [raw[:, n % 2, b]
                                                                        for b in range(4 * half, 4 * half + 4)])
                            pe.wait_ge(to(G, "transposes_copied"), batch(G, "cache", br, hp, 1) + 1)
                            pe.wait_ge(S("qm_ready"), n + 1)
                        for odd in range(2):
                            part = slice(HD * odd, HD * odd + HD)
                            c0 = (odd * 4 + hp) * 256
                            if G is G0:
                                ins = pe.matmul(widef[:, c0:c0 + seen], G.qk[part, 0, hp, cols(t)],
                                                G.qk[part, 1, hp, 0:seen], start=True, stop=True)
                                continue
                            pe.matmul(widef[:, c0 + P:c0 + 2 * P], G.qk[part, 0, hp, :], G.qk[part, 1, hp, :],
                                      start=True, stop=True)
                            for b in range(STREAMS):
                                ins = pe.matmul(widef[:, c0:c0 + P], qm[part, n % 2, b * P:b * P + P],
                                                kcT[part, n % 2, b, :], start=b == 0, stop=b == STREAMS - 1)
                        if G is G1:
                            ins.then_inc(to(G, "pair_scored"), 1)
                    if G is G0:
                        ins.then_inc(to(G, "logits_done"), 1)

                def probs_in(br, t, hp):
                    pr = probs_of(G, br * G.n + t)
                    transposes(G, ("prob", br, t, hp), [pr[:, odd * 4 + hp, k * P:k * P + P] for odd in range(2)
                                                        for k in range(SEEN[G.tiles[t]] // P)])

                def weigh_values(br, t):
                    r = br * G.n + t
                    nk = SEEN[G.tiles[t]] // P
                    v = BV if br else AV
                    pe.wait_ge(to(G, "probs_ready"), r + 1)
                    if r >= banks:
                        pe.wait_ge(to(G, "attended"), r - banks + 1)
                    if G is G0:
                        issued = 7 * G.n + sum(GATES_INDEX) + sum(GATES_HEADS[:r + 1])
                        pe.wait_ge(to(G, "group_copied"), copied_before(r % 2, issued))
                    elif r == 0:
                        pe.wait_ge(to(G, "group_copied"), 7)
                    for hp in range(PAIRS):
                        if hp:
                            yield AT["values_" + "ab"[br]][hp]
                        for k in {0: range(0, 2), PAIRS - 1: []}.get(hp, [hp + 1]) if G is G0 else [hp]:
                            probs_in(br, t, k)
                        pe.wait_ge(to(G, "transposes_copied"), batch(G, "prob", br, t, hp) + 1)
                        n = br * PAIRS + hp
                        if G is G1:
                            pe.wait_ge(S(f"vcache_in{n % 2}"), 16 * (n // 2 + 1))
                        for odd in range(2):
                            out = G.accum[r % banks][HD * odd:HD * odd + HD, hp * P:hp * P + P]
                            vcols = slice(hp * P + HD * odd, hp * P + HD * odd + HD)
                            if G is G0:
                                for k in range(nk):
                                    p0 = (odd * nk + k) * P
                                    ins = pe.matmul(out, G.qkv[:, v, k, vcols], probT[:, hp % 2, p0:p0 + P],
                                                    start=k == 0, stop=k == nk - 1)
                                continue
                            p0 = odd * 2 * P
                            pe.matmul(out, G.qkv[:, v, 0, vcols], probT[:, hp % 2, p0 + P:p0 + 2 * P], start=True,
                                      stop=False, skip_group_check=True)
                            for b in range(STREAMS):
                                ins = pe.matmul(out[:, b * NEW:b * NEW + NEW], vc[:, n % 2, b, HD * odd:HD * odd + HD],
                                                probT[:, hp % 2, p0 + b * NEW:p0 + b * NEW + NEW], start=False,
                                                stop=b == STREAMS - 1, skip_group_check=True)
                        ins.then_inc(to(G, "pv_done"), 1)

                if G is G0:
                    yield from score_heads(0, 0)
                    for r in range(4):
                        gate_units(GATES_HEADS[r], r)
                        if r < 3:
                            yield from score_heads(*divmod(r + 1, 2))
                        yield from weigh_values(*divmod(r, 2))
                        if r == 0:
                            heads_in(1)
                else:
                    for br in range(2):
                        yield AT["score_" + "ab"[br]][0]
                        yield from score_heads(br, 0)
                        if not br:
                            yield AT["heads_b"]
                            heads_in(1)
                        yield AT["values_" + "ab"[br]][0]
                        yield from weigh_values(br, 0)
                if G is G1:
                    yield from projection(range(7, NG), GATES)
                yield AT["branch"]
                pe.wait_ge(to(G, "attended"), 2 * G.n)
                pe.wait_ge(to(G, "logits_read"), 2 * G.n)
                for br in range(2):
                    name = "br_" + "ab"[br]
                    weights_wait(pe, G, name)
                    for t in every:
                        u = br * G.n + t
                        if u >= 2:
                            pe.wait_ge(to(G, "branches_read"), u - 1)
                        for n in range(2):
                            for c in range(PAIRS):
                                ins = pe.matmul(wide[:, 2 * (u % 2) + n, :], G.oT[br][:, c, cols(t)],
                                                slot_weights(G, name)[:, c, 512 * n:512 * n + 512],
                                                start=c == 0, stop=c == PAIRS - 1)
                        ins.then_inc(to(G, "branches_done"), 1)
                yield AT["merge"]
                for t in every:
                    pe.wait_ge(to(G, "merged_ready"), t + 1)
                    for half in range(2):
                        rows(G, "merged", G.merged[:, t, :], t, half)
                for t in every:
                    for n in range(2):
                        yield LAST["out"] if (t, n) == (1, 1) else AT["out"][n]
                        weights_wait(pe, G, f"out{n}")
                        u = 2 * t + n
                        if n == 0:
                            pe.wait_ge(to(G, "transposes_copied"), batch(G, "merged", t, 1) + 1)
                        if u >= banks:
                            pe.wait_ge(to(G, "x1_added"), u - banks + 1)
                        elif G is G1:
                            pe.wait_ge(to(G, "group_copied"), NG)
                        for c in range(DC):
                            ins = pe.matmul(G.accum[u % banks][:, :], G.hT[:, c, cols(t)], slot_weights(G, f"out{n}")[:, c, :],
                                            start=c == 0, stop=c == DC - 1)
                        ins.then_inc(to(G, "out_done"), 1)
                        if t == 1 and n == 0:
                            h2_rows(G, 0)
                    if G is G1:
                        yield AT["h2"]
                    if t == G.n - 1:
                        h2_rows(G, t)

            def h2_rows(G, t):
                pe.wait_ge(S("h2_ready"), G.tiles[t] + 1)
                for half in range(2):
                    rows(G, "h2", h2[:, G.tiles[t], :], t, half)

            def queries(G):
                r = 0
                for n, (q, t0, t1) in enumerate(QUERY_STEPS[G.name]):
                    yield query_at(G.name, n, 0)
                    weights_wait(pe, G, f"pq{q}")
                    pe.wait_ge(to(G, "transposes_copied"), batch(G, "h2", t1 - 1, 1) + 1)
                    pe.wait_ge(to(G, "branches_read"), 2 * G.n)
                    if t1 == G.n:
                        pe.wait_ge(to(G, "x1_added"), 2 * G.n)
                    for k in range(QG):
                        if k == 2:
                            yield query_at(G.name, n, 1)
                        if n or k >= 2:
                            pe.wait_ge(to(G, "query_copied"), QG * n + k - 1)
                        for c in range(DC):
                            ins = pe.matmul(query_bank(G, n, k)[:, 0:(t1 - t0) * P],
                                            slot_weights(G, f"pq{q}")[:, c, k * P:k * P + P],
                                            G.h2T[:, c, t0 * P:t1 * P], start=c == 0, stop=c == DC - 1)
                        ins.then_inc(to(G, "query_done"), 1)
                    yield query_at(G.name, n, 2)
                    pe.wait_ge(to(G, "query_copied"), QG * n + QG)
                    for t in range(t0, t1):
                        if r >= 4:
                            pe.wait_ge(to(G, "router_copied"), r - 3)
                        for k in range(QG):
                            ins = pe.matmul(wide[:, r % 4, k * P:k * P + P], G.pqT[:, k, cols(t)], cT[:, k % 2, :],
                                            start=True, stop=True)
                        ins.then_inc(to(G, "score_done"), 1)
                        r += 1

            def add_rows(t, j, sub, start=False, stop=False):
                m = (j * 2) + (t * HALVES + sub)
                for s in range(HALF):
                    q = sub * HALF + s
                    pe.wait_ge(S("diag_done"), m * HALF + (s + 1))
                    pe.wait_ge(S(f"v_rows{q}"), j * 16 + (t * HALVES // 2 + 1) * 16)
                    for n in range(2):
                        ins = pe.matmul(ysum[n][:, :], diag[:, q, :], vbuf[:, q, n * 512:n * 512 + 512],
                                        start=start and s == 0, stop=stop and s == HALF - 1)
                    ins.then_inc(S("v_added"), 1)

            between = [laid(x) for x in (early(steps(G0)), queries(G0), steps(G1), queries(G1))]
            start_laid(between)
            for m in range(LAID):
                t = m // HALVES
                if t and m % HALVES == 0:
                    pe.wait_ge(S("y_ready"), t)
                add_rows(t, m % HALVES // 2, m % 2, start=m % HALVES == 0, stop=m % HALVES == HALVES - 1)
                for b in between:
                    b.send(m)
            with pe.Fori(LAID // 2 - HALVES, HALVES // 2 - 1) as j:
                for sub in range(2):
                    add_rows(SAMPLE, j, sub)
            for sub in range(2):
                add_rows(SAMPLE, HALVES // 2 - 1, sub, stop=sub == 1)

        @block.vector
        def _(v):
            def step(ins, name="dve_step"):
                chain(v, ins, name)

            v.wait_ge(S("gain_in"), 16)
            for t in range(TILES):
                G = G1 if t == SAMPLE else G0
                v.wait_ge(S("row_scale"), t + 1)
                signal(v.scalar_tensor_tensor(out=h2[:, t, :], in0=x1[:, t, :], scalar=rsx[:, 0, t:t + 1],
                                              in1=gain[:, :], op0=ALU.mult, op1=ALU.mult), f"{G.name}_h_ready")
            v.wait_ge(S("rbias_in"), 16)
            step(v.tensor_copy(ext[:, :, 0:REL - 1],
                               rbias[:, :, 2 * REL:2 * REL + 1].to_broadcast([P, HEADS, REL - 1])))
            step(v.tensor_copy(ext[:, :, REL - 1:EXT], rbias[:, :, ::-1]), "ext_built")
            v.wait_ge(S("rope_in"), 16 * 7)

            def rope(x, cos, sin, half, tmp, ready):
                lo, hi = x[..., 0:half], x[..., half:2 * half]
                signal(v.tensor_tensor(tmp[0], lo, cos, ALU.mult), "dve_step")
                signal(v.tensor_tensor(tmp[1], hi, sin, ALU.mult), "dve_step")
                signal(v.tensor_tensor(tmp[2], hi, cos, ALU.mult), "dve_step")
                step(v.tensor_tensor(tmp[3], lo, sin, ALU.mult))
                step(v.tensor_tensor(lo, tmp[0], tmp[1], ALU.subtract))
                step(v.tensor_tensor(hi, tmp[2], tmp[3], ALU.add), ready)

            def streams_apart(dst, src):
                return v.tensor_copy(dst.rearrange("p (b c) -> p b c", c=P + NEW)[:, :, 0:NEW],
                                     src.rearrange("p (b j) -> p b j", j=NEW))

            def steps(G):
                every = range(G.n)
                g0, name = G.tiles[0], G.name
                tiles = slice(g0, g0 + G.n)
                head = 0
                for g, (what, _, _) in enumerate(GROUPS[:7]):
                    yield NORM[g]
                    if what in ("aq", "ak", "bq", "bk"):
                        k, n = ("aq", "ak", "bq", "bk").index(what), 8 * G.n
                        v.wait_ge(to(G, "group_copied"), G.n * (g + 1))
                        x = G.qkv[:, where[what]].rearrange("p t (h d) -> p (t h) d", d=HD)
                        sq = G.tmp[:, 0:512 * G.n].rearrange("p (n d) -> p n d", d=HD)
                        step(v.tensor_tensor(sq, x, x, ALU.mult))
                        step(v.tensor_reduce(ssh[:, k, 0:n], sq, AX, ALU.add), name + "_heads_squared")
                        head += 1
                        yield NORM[g] + 2
                        v.wait_ge(to(G, "head_scale"), head)
                        step(v.tensor_tensor(x, x, rsh[:, k, 0:n].unsqueeze(2).to_broadcast([P, n, HD]), ALU.mult))
                        last = v.tensor_tensor(x, x, hgain[:, k:k + 1, :].to_broadcast([P, n, HD]), ALU.mult)
                        if what[0] == "b":
                            step(last, name + "_heads_ready")
                            continue
                        step(last)
                        w = 256 * G.n
                        tmp = [G.tmp[:, m * w:m * w + w].rearrange("p (t h d) -> p t h d", t=G.n, h=HEADS)
                               for m in range(4)]
                        cs = [ropet[:, m, tiles].unsqueeze(2).to_broadcast([P, G.n, HEADS, HD // 2]) for m in range(2)]
                        rope(G.qkv[:, where[what]].rearrange("p t (h d) -> p t h d", d=HD), cs[0], cs[1], HD // 2, tmp,
                             name + "_heads_ready")
                    if what == "ix":
                        v.wait_ge(to(G, "group_copied"), G.n * (g + 1))
                        ik = G.ix[:, :, 256:288]
                        sq = G.tmp[:, 0:ID * G.n].rearrange("p (t d) -> p t d", d=ID)
                        step(v.tensor_tensor(sq, ik, ik, ALU.mult))
                        step(v.tensor_reduce(ssh[:, 4, 0:G.n], sq, AX, ALU.add), name + "_heads_squared")
                        head += 1
                        step(v.tensor_scalar(G.ix[:, :, 288:296], G.ix[:, :, 288:296], IH ** -0.5, None, ALU.mult))
                        iq = G.ix[:, :, 0:256].rearrange("p t (h d) -> p t h d", d=ID)
                        w = 128 * G.n
                        tmp = [G.tmp[:, m * w:m * w + w].rearrange("p (t h d) -> p t h d", t=G.n, h=IH)
                               for m in range(4)]
                        cs = [ropei[:, m, tiles].unsqueeze(2).to_broadcast([P, G.n, IH, ID // 2]) for m in range(2)]
                        rope(iq, cs[0], cs[1], ID // 2, tmp, "dve_step")
                        yield NORM[g] + 2
                        v.wait_ge(to(G, "head_scale"), head)
                        step(v.tensor_tensor(ik, ik, rsh[:, 4, 0:G.n].unsqueeze(2).to_broadcast([P, G.n, ID]), ALU.mult))
                        step(v.tensor_tensor(ik, ik, igain[:, :].unsqueeze(1).to_broadcast([P, G.n, ID]), ALU.mult))
                        w = 16 * G.n
                        tmp = [G.tmp[:, m * w:m * w + w].rearrange("p (t d) -> p t d", t=G.n) for m in range(4)]
                        rope(ik, ropei[:, 0, tiles], ropei[:, 1, tiles], ID // 2, tmp, name + "_ik_ready")
                yield AT["heads_a"] - 1
                if G is G1:
                    v.wait_ge(S("new_bias_in"), 16 * HEADS)
                    blocks = bias[:, 0].rearrange("p h (b j) -> p h b j", j=NEW)
                    step(v.tensor_tensor(blocks, new_bias[:, :, :].unsqueeze(2).to_broadcast([P, HEADS, STREAMS, NEW]),
                                         own[:, :].rearrange("p (b j) -> p b j", j=NEW).unsqueeze(1).to_broadcast(
                                             [P, HEADS, STREAMS, NEW]), ALU.add))
                    step(v.memset(qm, 0.0))
                    v.wait_ge(S("cik_in"), 16)
                    step(v.tensor_copy(cikrep, cik.unsqueeze(2).to_broadcast([P, STREAMS, 4, ID])))
                step(v.tensor_copy(G.ikrep, G.ix[:, :, 256:288].unsqueeze(2).to_broadcast([P, G.n, 4, ID])),
                     name + "_index_ready")
                yield AT["index"]
                if G is G1:
                    v.wait_ge(to(G, "transposes_copied"), batch(G, "index", 0) + 1)
                    for c in range(2):
                        signal(streams_apart(qm[:, c, :], G.iqT[:, c, :]), "iqm_ready" if c else "dve_step")
                yield AT["select"]
                v.wait_ge(S("own_set"), 1)
                for t in every:
                    tile = G.tiles[t]
                    n = SEEN[tile]
                    v.wait_ge(to(G, "relu_done"), t + 1)
                    s = score[:, t, 0:n]
                    for h in range(IH):
                        rel = probs[:, at_index(h), 0:n]
                        w = G.ix[:, t, 288 + h:289 + h]
                        if h == 0:
                            step(v.tensor_scalar(s, rel, w, None, ALU.mult))
                        else:
                            step(v.scalar_tensor_tensor(out=s, in0=rel, scalar=w, in1=s, op0=ALU.mult, op1=ALU.add),
                                 name + "_scored" if h == IH - 1 else "dve_step")
                    if G is G1:
                        for hp in range(2):
                            v.wait_ge(to(G, "index_done"), 1)
                            signal(streams_apart(qm[:, hp, :], G.qk[:, 0, hp, :]), "qm_ready")
                        yield AT["select"] + 1
                    if tile < SAMPLE:
                        step(v.memset(score[0:CHUNK, t, n - CHUNK:n], NEG))
                    else:
                        step(v.tensor_tensor(score[:, t, P:2 * P], score[:, t, P:2 * P], own[:, :], ALU.add))
                        step(v.memset(score[:, t, 256:264], PAD))
                    for _ in range(SELECT[tile] // 8):
                        step(v.max(mx8[:, :], s))
                        step(v.match_replace(s, mx8[:, :], s, TAKEN))
                    if SELECT[tile] % 8:
                        step(v.max(mx8[:, :], s))
                        step(v.memset(mx8[:, SELECT[tile] % 8:8], PAD))
                        step(v.match_replace(score[:, t, :], mx8[:, :], score[:, t, :], TAKEN))
                    step(v.tensor_scalar(mask[:, t, 0:n], s, TAKEN / 2, NEG, ALU.is_gt, ALU.mult), "mask_ready")

                for br in range(2):
                    ab = "ab"[br]
                    for t in every:
                        r = br * G.n + t
                        n = SEEN[G.tiles[t]]
                        place = probs_of(G, r)
                        pr = place[:, :, 0:n]
                        if G is G1:
                            for hp in range(0 if br else 2, PAIRS):
                                yield AT["score_" + ab][hp] - 1
                                m = br * PAIRS + hp
                                v.wait_ge(to(G, "pair_scored"), m - 1)
                                if br and hp == 0:
                                    v.wait_ge(to(G, "transposes_copied"), batch(G, "q", 1, 0) + 1)
                                signal(streams_apart(qm[:, m % 2, :], G.qk[:, 0, hp, :]), "qm_ready")
                            yield AT["soft_" + ab]
                            v.wait_ge(to(G, "pair_scored"), (br + 1) * PAIRS)
                        else:
                            v.wait_ge(to(G, "logits_done"), r + 1)
                        if r >= G.n:
                            v.wait_ge(to(G, "transposed"), batch(G, "prob", 0, t, PAIRS - 1) + 1)
                        if br == 0:
                            step(v.scalar_tensor_tensor(out=pr, in0=logits[:, :, 0:n], scalar=HD ** -0.5,
                                                        in1=mask[:, t:t + 1, 0:n].to_broadcast([P, HEADS, n]),
                                                        op0=ALU.mult, op1=ALU.add), name + "_logits_read")
                        else:
                            if G is G1:
                                v.wait_ge(S("sample_bias_in"), 16 * HEADS)
                            elif t == 0:
                                v.wait_ge(S("bias_in"), 16 * 4)
                                step(v.memset(bias[0:CHUNK, 0, :, CHUNK:P], NEG), "bias_masked")
                            kinds = [[0], [1, 0], [1, 0]][G.tiles[t]]
                            for k, kind in enumerate(kinds):
                                step(v.scalar_tensor_tensor(out=place[:, :, k * P:k * P + P],
                                                            in0=logits[:, :, k * P:k * P + P], scalar=HD ** -0.5,
                                                            in1=bias[:, kind], op0=ALU.mult, op1=ALU.add),
                                     name + "_logits_read" if k == len(kinds) - 1 else "dve_step")
                        step(v.tensor_reduce(rowmax[:, :], pr, AX, ALU.max))
                        step(v.tensor_scalar(rowmax[:, :], rowmax[:, :], -1.0, None, ALU.mult), name + "_rowmax_ready")
                        yield AT["soft_" + ab] + 2
                        v.wait_ge(to(G, "exp_done"), HEADS * (r + 1))
                        step(v.reciprocal(rowinv[:, :], rowsum[:, :]))
                        step(v.tensor_tensor(pr, pr, rowinv[:, :].unsqueeze(2).to_broadcast([P, HEADS, n]), ALU.mult),
                             name + "_probs_ready")

                yield AT["branch"] + 1
                for t in every:
                    v.wait_ge(to(G, "branches_done"), t + 1)
                    v.wait_ge(to(G, "group_copied"), G.n * NG)
                    step(v.tensor_tensor(G.merged[:, t, :], widef[:, t * D:t * D + D], G.gates[t][:, 0:D], ALU.mult),
                         name + "_branches_read")
                for t in every:
                    u = G.n + t
                    v.wait_ge(to(G, "branches_done"), u + 1)
                    step(v.tensor_tensor(G.merge_tmp, widef[:, u % 2 * D:u % 2 * D + D], G.gates[t][:, D:2 * D],
                                         ALU.mult), name + "_branches_read")
                    step(v.tensor_tensor(G.merged[:, t, :], G.merged[:, t, :], G.merge_tmp, ALU.add),
                         name + "_merged_ready")
                v.wait_ge(S("gain_in"), 32)
                for t in every:
                    for n in range(2):
                        yield LAST["x1"] if (t, n) == (1, 1) else AT["out"][n] + 1
                        u = 2 * t + n
                        v.wait_ge(to(G, "out_done"), u + 1)
                        part = x1[:, G.tiles[t], n * 512:n * 512 + 512]
                        step(v.tensor_tensor(part, G.accum[u % len(G.accum)][:, :], part, ALU.add), name + "_x1_added")
                    yield LAST["h2"] if t else AT["scale"] + 1
                    tile = G.tiles[t]
                    v.wait_ge(S("row_scale"), TILES + tile + 1)
                    signal(v.scalar_tensor_tensor(out=h2[:, tile, :], in0=x1[:, tile, :], scalar=rsx[:, 1, tile:tile + 1],
                                                  in1=gain[:, :], op0=ALU.mult, op1=ALU.mult), "h2_ready")

            def together(instructions, name="dve_step"):
                for ins in instructions:
                    signal(ins, name)
                v.wait_ge(sems[name], counts[name])

            def top16(values, top, index, rows):
                together(v.max(top(n)[:, 0:8], values(n)) for n in rows)
                together(v.max_index(index(n)[:, 0:8], top(n)[:, 0:8], values(n)) for n in rows)
                together(v.match_replace(values(n), top(n)[:, 0:8], values(n), TAKEN) for n in rows)
                together(v.max(top(n)[:, 8:16], values(n)) for n in rows)
                together(v.max_index(index(n)[:, 8:16], top(n)[:, 8:16], values(n)) for n in rows)

            def route(t):
                G, scores = (G1, sc[0]) if t == SAMPLE else (G0, sc[t])
                v.wait_ge(S("iota_set"), 1)
                full = [P, QH, PEER_K, PEER_K]
                for q in range(4):
                    at = ROUTE[t][q]
                    yield at[0]
                    v.wait_ge(to(G, "router_copied"), q + 1 if t == SAMPLE else 2 * q + t + 1)
                    top16(lambda n: scores[:, QG * q + n, :], lambda n: rtop[:, n, :], lambda n: rtopi[:, n, :],
                          range(QG))
                    yield at[1]
                    step(v.tensor_copy(rtopf[:, :, :], rtopi[:, :, :]))
                    r4 = rtop[:, :, :].rearrange("p (h s) k -> p h s k", s=2)
                    f4 = rtopf[:, :, :].rearrange("p (h s) k -> p h s k", s=2)
                    cand4 = cand.rearrange("p h (a b) -> p h a b", b=PEER_K)
                    step(v.tensor_tensor(cand4, r4[:, :, 0, :].unsqueeze(3).to_broadcast(full),
                                         r4[:, :, 1, :].unsqueeze(2).to_broadcast(full), ALU.add))
                    top16(lambda n: cand[:, n, :], lambda n: sv[:, n, :], lambda n: si[:, n, :], range(QH))
                    gt = gate[:, t, QS * q:QS * q + QS].rearrange("p (h k) -> p h k", k=PEER_K)
                    step(v.tensor_tensor(gt, sv[:, :, :], sv[:, :, 0:1].to_broadcast([P, QH, PEER_K]), ALU.subtract))
                    step(v.tensor_copy(sv[:, :, :], gt), "picked")
                    yield at[2]
                    halves = [sif[:, s, :].rearrange("p (h k) -> p h k", k=PEER_K) for s in range(2)]
                    step(v.tensor_scalar(sj[:, :, :], si[:, :, :], 4, None, ALU.logical_shift_right))
                    step(v.tensor_copy(halves[0], sj[:, :, :]))
                    step(v.tensor_scalar(sj[:, :, :], si[:, :, :], 15, None, ALU.bitwise_and))
                    step(v.tensor_copy(halves[1], sj[:, :, :]))
                    io = iota16[:, :].unsqueeze(1).unsqueeze(1).to_broadcast(full)
                    together(v.tensor_tensor(pick[s], halves[s].unsqueeze(3).to_broadcast(full), io, ALU.is_equal)
                             for s in range(2))
                    together(v.tensor_tensor(pick[s], pick[s], f4[:, :, s, :].unsqueeze(2).to_broadcast(full),
                                             ALU.mult) for s in range(2))
                    together(v.tensor_reduce(halves[s], pick[s], AX, ALU.add) for s in range(2))
                    step(v.scalar_tensor_tensor(out=sif[:, 0, :], in0=sif[:, 0, :], scalar=float(NKEYS),
                                                in1=sif[:, 1, :], op0=ALU.mult, op1=ALU.add))
                    step(v.tensor_copy(expert[:, t, QS * q:QS * q + QS], sif[:, 0, :]), "routed")
                    v.wait_ge(S("expert_exp"), 4 * t + q + 1)
                    step(v.tensor_reduce(esum[:, :], sv[:, :, :], AX, ALU.add))
                    step(v.reciprocal(esum[:, :], esum[:, :]))
                    step(v.tensor_tensor(gt, sv[:, :, :], esum[:, :].unsqueeze(2).to_broadcast([P, QH, PEER_K]),
                                         ALU.mult), "gates_ready")

            def dot(t, j, sub):
                m = (j * 2) + (t * HALVES + sub)
                if not (isinstance(m, int) and m < 2):
                    v.wait_ge(S("gelu_done"), m - 1)
                for s in range(HALF):
                    v.wait_ge(S(f"u_rows{s}"), m * 16 + 16)
                    v.tensor_tensor_reduce(ubuf[:, s, :], ubuf[:, s, :], h2[:, t, :], 1.0, 0.0, ALU.mult, ALU.add,
                                           dots[:, sub, s:s + 1]).then_inc(S("dot_done"), 1)

            def add_y(t):
                v.wait_ge(S("v_added"), (t + 1) * SLOTS)
                for n in range(2):
                    part = x1[:, t, n * 512:n * 512 + 512]
                    signal(v.tensor_tensor(part, ysum[n][:, :], part, ALU.add), "y_ready" if n else "dve_step")

            between = [laid(x) for x in (early(steps(G0)), route(0), route(1), steps(G1), route(SAMPLE))]
            start_laid(between)
            for m in range(LAID):
                if m % HALVES == 1 and m > HALVES:
                    add_y(m // HALVES - 1)
                dot(m // HALVES, m % HALVES // 2, m % 2)
                for b in between:
                    b.send(m)
            with v.Fori(LAID // 2 - HALVES, HALVES // 2) as j:
                for sub in range(2):
                    dot(SAMPLE, j, sub)
            add_y(SAMPLE)


NAMES = ["x_prompt", "x_sample", "cache_a_k", "cache_a_v", "cache_a_ik", "cache_b_k", "cache_b_v", "g_attn", "w_in",
         "g_qa", "g_ka", "g_ik", "g_qb", "g_kb", "rel_bias", "w_br_a", "w_br_b", "w_out", "g_ffn", "w_pq",
         "peer_c1", "peer_c2", "peer_u", "peer_v"]
MATRICES = ("w_in", "w_br_a", "w_br_b", "w_out", "w_pq")
OUTS = [("y_prompt", (1, 256, D)), ("y_sample", (STREAMS, NEW, D)),
        ("a_k_prompt", (1, 1, 256, HEADS, HD)), ("a_v_prompt", (1, 1, 256, HEADS, HD)),
        ("a_ik_prompt", (1, 1, 256, ID)), ("b_k_prompt", (1, 1, 256, HEADS, HD)),
        ("b_v_prompt", (1, 1, 256, HEADS, HD)),
        ("a_k_sample", (1, STREAMS, NEW, HEADS, HD)), ("a_v_sample", (1, STREAMS, NEW, HEADS, HD)),
        ("a_ik_sample", (1, STREAMS, NEW, ID)), ("b_k_sample", (1, STREAMS, NEW, HEADS, HD)),
        ("b_v_sample", (1, STREAMS, NEW, HEADS, HD))]


def rope_table(half):
    inverse = np.power(np.float32(10000.0), -np.arange(half, dtype=np.float32) / np.float32(half))
    row = np.arange(P)
    positions = np.stack([row, row + P, PAST + row % NEW], axis=1).astype(np.float32)
    angle = (positions[:, :, None] * inverse[None, None, :].astype(np.float32)).astype(np.float32)
    return np.ascontiguousarray(np.stack([np.cos(angle), np.sin(angle)], axis=1).astype(np.float32))


def kernel(**inputs):
    import concourse.bacc as bacc
    from concourse.bass_utils import run_bass_kernel_spmd

    nc = bacc.Bacc("TRN2", target_bir_lowering=False, num_devices=1)
    arrays, ins, outs = {}, {}, {}
    given = {n: np.ascontiguousarray(inputs[n]) for n in NAMES}
    given["rope_head"] = rope_table(HD // 2)
    given["rope_index"] = rope_table(ID // 2)
    for name, a in given.items():
        arrays[f"in_{name}"] = a
        ap = nc.dram_tensor(f"in_{name}", a.shape, mybir.dt.from_np(a.dtype), kind="ExternalInput").ap()
        ins[name] = ap[0] if name in MATRICES else ap
    for name, shape in OUTS:
        outs[name] = nc.dram_tensor(f"out_{name}", shape, F32, kind="ExternalOutput").ap()
    build(nc, ins, outs)
    r = run_bass_kernel_spmd(nc, [arrays], core_ids=[0])
    return tuple(r.results[0][f"out_{name}"] for name, _ in OUTS)
```
